# Optimizing a Trainium2 kernel written in Bass

```python
import math
import jax, jax.numpy as jnp
from jax import lax
import numpy as np

D_MODEL = 2048
BATCH = 1
SEQ = 256
DEPTH = 2

HEAD_DIM = 64
N_Q_HEADS = D_MODEL // 2 // HEAD_DIM
N_KV_HEADS = N_Q_HEADS // 4
ATTN_WIDTH = N_Q_HEADS * HEAD_DIM
KV_WIDTH = N_KV_HEADS * HEAD_DIM
WINDOW = 128
ATTN_BLOCK = 128
ROPE_THETA = 10000.0
POOL_WINDOWS = (2, 4, 8, 16)
POOL_WIDTH = D_MODEL // 4
POOL_GROUP = POOL_WIDTH // len(POOL_WINDOWS)
SSM_WIDTH = D_MODEL // 4
SSM_GROUP = 16
SSM_N_GROUPS = SSM_WIDTH // SSM_GROUP
SSM_STATE = 64
MIX_WIDTH = ATTN_WIDTH + POOL_WIDTH + SSM_WIDTH
IN_WIDTH = ATTN_WIDTH + 2 * KV_WIDTH + POOL_WIDTH + SSM_WIDTH
D_FF = 5504
CONV_WIDTH = 3
LN_EPS = 1e-5
DEEPNORM_ALPHA = (2 * DEPTH) ** 0.25
DEEPNORM_BETA = (8 * DEPTH) ** -0.25

kernel_name = 'hybrid_swa_pool_s5_convffn'

F32 = jnp.float32

def layer_norm(x, g, b):
    xf = x.astype(F32)
    mu = xf.mean(-1, keepdims=True)
    var = jnp.square(xf - mu).mean(-1, keepdims=True)
    return ((xf - mu) * lax.rsqrt(var + LN_EPS) * g.astype(F32) + b.astype(F32)).astype(x.dtype)

def rope(t, pos):
    half = HEAD_DIM // 2
    inv = ROPE_THETA ** (-jnp.arange(half, dtype=F32) / half)
    ang = pos.astype(F32)[:, None] * inv[None, :]
    cos = jnp.cos(ang)[None, :, None, :]
    sin = jnp.sin(ang)[None, :, None, :]
    tf = t.astype(F32)
    t1, t2 = tf[..., :half], tf[..., half:]
    return jnp.concatenate([t1 * cos - t2 * sin, t2 * cos + t1 * sin], -1).astype(t.dtype)

def sliding_window_attention(q, k, v, sinks):
    bsz, s_len = q.shape[0], q.shape[1]
    nb = s_len // ATTN_BLOCK
    grp = N_Q_HEADS // N_KV_HEADS
    qb = q.reshape(bsz, nb, ATTN_BLOCK, N_KV_HEADS, grp, HEAD_DIM).astype(F32)

    def band(t):
        tb = t.reshape(bsz, nb, ATTN_BLOCK, N_KV_HEADS, HEAD_DIM)
        prev = jnp.concatenate([jnp.zeros_like(tb[:, :1]), tb[:, :-1]], axis=1)
        return jnp.concatenate([prev, tb], axis=2).astype(F32)

    kw, vw = band(k), band(v)
    s = jnp.einsum('bnqkgd,bnjkd->bnkgqj', qb, kw) * (HEAD_DIM ** -0.5)
    i = jnp.arange(ATTN_BLOCK)[:, None]
    j = jnp.arange(2 * ATTN_BLOCK)[None, :]
    dist = i + ATTN_BLOCK - j
    in_win = (dist >= 0) & (dist < WINDOW)
    blk = jnp.arange(nb)[:, None, None]
    valid = in_win[None] & ((blk > 0) | (j[None] >= ATTN_BLOCK))
    s = jnp.where(valid[None, :, None, None], s, -1e30)
    sink = sinks.astype(F32).reshape(N_KV_HEADS, grp)[None, None, :, :, None, None]
    m = jnp.maximum(s.max(-1, keepdims=True), sink)
    p = jnp.exp(s - m)
    denom = p.sum(-1, keepdims=True) + jnp.exp(sink - m)
    o = jnp.einsum('bnkgqj,bnjkd->bnqkgd', p / denom, vw)
    return o.reshape(bsz, s_len, ATTN_WIDTH).astype(q.dtype)

def multiscale_pool(u, pool_w, pool_scale):
    uf = u.astype(F32)
    s_len = u.shape[1]
    t = jnp.arange(s_len, dtype=F32)[None, :, None]
    outs = []
    for gi, w in enumerate(POOL_WINDOWS):
        ug = uf[..., gi * POOL_GROUP:(gi + 1) * POOL_GROUP]
        c = jnp.cumsum(ug, axis=1)
        c_shift = jnp.pad(c, ((0, 0), (w, 0), (0, 0)))[:, :s_len]
        mean = (c - c_shift) / jnp.minimum(t + 1.0, float(w))
        outs.append(jnp.einsum('bsc,cd->bsd', mean - ug, pool_w[gi].astype(F32)))
    return (jnp.concatenate(outs, -1) * pool_scale.astype(F32)).astype(u.dtype)

def s5_ssm(u, lam_re, lam_im, log_dt, b_re, b_im, c_re, c_im, d, glu_w):
    bsz, s_len = u.shape[0], u.shape[1]
    uf = u.astype(F32).reshape(bsz, s_len, SSM_N_GROUPS, SSM_GROUP)
    lr, li = lam_re.astype(F32), lam_im.astype(F32)
    dt = jnp.exp(log_dt.astype(F32))[:, None]
    mag = jnp.exp(lr * dt)
    ab_re, ab_im = mag * jnp.cos(li * dt), mag * jnp.sin(li * dt)
    nr, ni = ab_re - 1.0, ab_im
    den = lr * lr + li * li
    zr = (nr * lr + ni * li) / den
    zi = (ni * lr - nr * li) / den
    br, bi = b_re.astype(F32), b_im.astype(F32)
    bbr = zr[..., None] * br - zi[..., None] * bi
    bbi = zr[..., None] * bi + zi[..., None] * br
    xr = jnp.einsum('gph,bsgh->bsgp', bbr, uf)
    xi = jnp.einsum('gph,bsgh->bsgp', bbi, uf)
    ar = jnp.broadcast_to(ab_re, xr.shape)
    ai = jnp.broadcast_to(ab_im, xi.shape)

    def combine(e1, e2):
        a1r, a1i, x1r, x1i = e1
        a2r, a2i, x2r, x2i = e2
        return (a2r * a1r - a2i * a1i, a2r * a1i + a2i * a1r,
                a2r * x1r - a2i * x1i + x2r, a2r * x1i + a2i * x1r + x2i)

    _, _, sr, si = lax.associative_scan(combine, (ar, ai, xr, xi), axis=1)
    y = (jnp.einsum('ghp,bsgp->bsgh', c_re.astype(F32), sr)
         - jnp.einsum('ghp,bsgp->bsgh', c_im.astype(F32), si)
         + d.astype(F32) * uf)
    y = jax.nn.gelu(y.reshape(bsz, s_len, SSM_WIDTH))
    ab = jnp.einsum('bsc,ce->bse', y, glu_w.astype(F32))
    out = ab[..., :SSM_WIDTH] * jax.nn.sigmoid(ab[..., SSM_WIDTH:])
    return out.astype(u.dtype)

def conv_glu_ffn(x, w_up, conv_w, conv_b, w_down):
    s_len = x.shape[1]
    h = jnp.einsum('bsd,df->bsf', x, w_up)
    hp = jnp.pad(h, ((0, 0), (CONV_WIDTH - 1, 0), (0, 0)))
    hc = conv_b + hp[:, 0:s_len] * conv_w[0]
    for tap in range(1, CONV_WIDTH):
        hc = hc + hp[:, tap:tap + s_len] * conv_w[tap]
    val, gate = hc[..., :D_FF], hc[..., D_FF:]
    act = (jax.nn.silu(gate.astype(F32)) * val.astype(F32)).astype(x.dtype)
    return jnp.einsum('bsf,fd->bsd', act, w_down)

def setup_inputs(seed: int = 0) -> dict:
    key = jax.random.key(seed)
    ks = jax.random.split(key, 32)
    L = DEPTH
    nrm = lambda k, shape, std: jax.random.normal(k, shape, F32) * std
    lam_im_base = math.pi * jnp.arange(SSM_STATE, dtype=F32)
    return {
        'x': nrm(ks[0], (BATCH, SEQ, D_MODEL), 1.0),
        'w_in': nrm(ks[1], (L, D_MODEL, IN_WIDTH), D_MODEL ** -0.5),
        'attn_sinks': nrm(ks[2], (L, N_Q_HEADS), 0.5),
        'pool_w': nrm(ks[3], (L, len(POOL_WINDOWS), POOL_GROUP, POOL_GROUP), POOL_GROUP ** -0.5),
        'pool_scale': 1.0 + nrm(ks[4], (L, POOL_WIDTH), 0.02),
        'ssm_lam_re': -0.5 + nrm(ks[5], (L, SSM_N_GROUPS, SSM_STATE), 0.01),
        'ssm_lam_im': lam_im_base + nrm(ks[6], (L, SSM_N_GROUPS, SSM_STATE), 0.01),
        'ssm_log_dt': jax.random.uniform(ks[7], (L, SSM_N_GROUPS), F32, math.log(1e-3), math.log(1e-1)),
        'ssm_b_re': nrm(ks[8], (L, SSM_N_GROUPS, SSM_STATE, SSM_GROUP), (2 * SSM_GROUP) ** -0.5),
        'ssm_b_im': nrm(ks[9], (L, SSM_N_GROUPS, SSM_STATE, SSM_GROUP), (2 * SSM_GROUP) ** -0.5),
        'ssm_c_re': nrm(ks[10], (L, SSM_N_GROUPS, SSM_GROUP, SSM_STATE), (2 * SSM_STATE) ** -0.5),
        'ssm_c_im': nrm(ks[11], (L, SSM_N_GROUPS, SSM_GROUP, SSM_STATE), (2 * SSM_STATE) ** -0.5),
        'ssm_d': nrm(ks[12], (L, SSM_N_GROUPS, SSM_GROUP), 1.0),
        'ssm_glu_w': nrm(ks[13], (L, SSM_WIDTH, 2 * SSM_WIDTH), SSM_WIDTH ** -0.5),
        'w_out': nrm(ks[14], (L, MIX_WIDTH, D_MODEL), MIX_WIDTH ** -0.5 * DEEPNORM_BETA),
        'ln1_g': 1.0 + nrm(ks[15], (L, D_MODEL), 0.02),
        'ln1_b': nrm(ks[16], (L, D_MODEL), 0.02),
        'ffn_w_up': nrm(ks[17], (L, D_MODEL, 2 * D_FF), D_MODEL ** -0.5),
        'ffn_conv_w': nrm(ks[18], (L, CONV_WIDTH, 2 * D_FF), CONV_WIDTH ** -0.5),
        'ffn_conv_b': nrm(ks[19], (L, 2 * D_FF), 0.01),
        'ffn_w_down': nrm(ks[20], (L, D_FF, D_MODEL), D_FF ** -0.5 * DEEPNORM_BETA),
        'ln2_g': 1.0 + nrm(ks[21], (L, D_MODEL), 0.02),
        'ln2_b': nrm(ks[22], (L, D_MODEL), 0.02),
    }

def reference(x, w_in, attn_sinks, pool_w, pool_scale, ssm_lam_re, ssm_lam_im, ssm_log_dt,
              ssm_b_re, ssm_b_im, ssm_c_re, ssm_c_im, ssm_d, ssm_glu_w, w_out, ln1_g, ln1_b,
              ffn_w_up, ffn_conv_w, ffn_conv_b, ffn_w_down, ln2_g, ln2_b):
    bsz, s_len = x.shape[0], x.shape[1]
    pos = jnp.arange(s_len)
    o_k = ATTN_WIDTH
    o_v = o_k + KV_WIDTH
    o_p = o_v + KV_WIDTH
    o_s = o_p + POOL_WIDTH
    for l in range(DEPTH):
        h = jnp.einsum('bsd,de->bse', x, w_in[l])
        q = rope(h[..., :o_k].reshape(bsz, s_len, N_Q_HEADS, HEAD_DIM), pos)
        k = rope(h[..., o_k:o_v].reshape(bsz, s_len, N_KV_HEADS, HEAD_DIM), pos)
        v = h[..., o_v:o_p].reshape(bsz, s_len, N_KV_HEADS, HEAD_DIM)
        y_attn = sliding_window_attention(q, k, v, attn_sinks[l])
        y_pool = multiscale_pool(h[..., o_p:o_s], pool_w[l], pool_scale[l])
        y_ssm = s5_ssm(h[..., o_s:], ssm_lam_re[l], ssm_lam_im[l], ssm_log_dt[l],
                       ssm_b_re[l], ssm_b_im[l], ssm_c_re[l], ssm_c_im[l], ssm_d[l],
                       ssm_glu_w[l])
        mix = jnp.concatenate([y_attn, y_pool, y_ssm], -1)
        mix = jnp.einsum('bse,ed->bsd', mix, w_out[l])
        x = layer_norm(DEEPNORM_ALPHA * x + mix, ln1_g[l], ln1_b[l])
        f = conv_glu_ffn(x, ffn_w_up[l], ffn_conv_w[l], ffn_conv_b[l], ffn_w_down[l])
        x = layer_norm(DEEPNORM_ALPHA * x + f, ln2_g[l], ln2_b[l])
    return x


_drawn_inputs = setup_inputs


def setup_inputs(seed=0):
    import zlib

    import numpy as np

    out = dict(_drawn_inputs(seed))
    spreads = {}
    factors = {'attn_sinks': 23.096,
     'pool_scale': 8.0,
     'ssm_lam_re': 64.0,
     'ssm_lam_im': 64.0,
     'ssm_log_dt': 64.0,
     'ssm_b_re': 64.0,
     'ssm_b_im': 64.0,
     'ssm_c_re': 64.0,
     'ssm_c_im': 64.0,
     'ffn_conv_b': 8.0}
    for name, (base, spread) in spreads.items():
        noise = np.random.default_rng([zlib.crc32(name.encode()), seed]).standard_normal(out[name].shape)
        drawn = base * np.exp(spread * noise) if base else spread * noise
        out[name] = __import__('jax').numpy.asarray(drawn.astype(out[name].dtype))
    for name, factor in factors.items():
        out[name] = (out[name] * factor).astype(out[name].dtype)
    return out
```

```python
from contextlib import ExitStack, contextmanager

import concourse.bass as bass
from concourse import mybir

F32 = mybir.dt.float32
F32R = mybir.dt.float32r
I32 = mybir.dt.int32
ALU = mybir.AluOpType
ACT = mybir.ActivationFunctionType
AX_X = mybir.AxisListType.X

P = 128
D = 2048
T = 256
DEPTH = 2
D_FF = 5504
KT = D // P
NT = T // P
IN_TILES = 20
SSM0, Q0, K0, V0, POOL0 = 0, 4, 12, 14, 16
FF_TILES = D_FF // P
SLOTS = 4
CHUNK = 1024
HALF = D // 2
BANK = 512
GBC = 256
ALPHA = (2 * DEPTH) ** 0.25
LN_EPS = 1e-5
SCALE = 64 ** -0.5
POOL_WINDOWS = (2, 4, 8, 16)
PAD = max(POOL_WINDOWS)

IN_M = 0
GLU_M = IN_M + IN_TILES // 2
OUT_M = GLU_M + 1
UP_M = OUT_M + 2 * KT // 4
DOWN_M = UP_M + FF_TILES
DOWN_GROUPS = (FF_TILES + 3) // 4
LAYER_M = DOWN_M + 2 * DOWN_GROUPS
LAYER_CHUNKS = 4 * LAYER_M
SHORT = 2
TILES = IN_TILES + 2 * FF_TILES

V_CONVW = 0
V_CONVB = V_CONVW + 3 * 2 * FF_TILES
V_G0 = V_CONVB + 2 * FF_TILES
V_G1 = V_G0 + 2 * KT
V_PSC = V_G1 + 2 * KT
V_D = V_PSC + 4
V_LR = V_D + 4
V_LI = V_LR + 16
V_LDT = V_LI + 16
V_SINK = V_LDT + 16
NV = V_SINK + 16

C_ID, C_PERM, C_COS, C_SIN, C_MASK, C_RECIP = 0, 128, 256, 512, 768, 1024
NC = C_RECIP + PAD

DVE_LAYER = 319
POOL_LAYER = 189
POOL_STATES = 76


class Steps:

    def __init__(self, eng, sem):
        self.eng, self.sem, self.base, self.n = eng, sem, 0, 0

    def mark(self, ins):
        ins.then_inc(self.sem, 1)
        self.n += 1

    def wait(self):
        self.eng.wait_ge(self.sem, self.base + self.n)

    @contextmanager
    def loop(self, n_iter, steps):
        base, n = self.base, self.n
        with self.eng.Fori(0, n_iter) as i:
            self.base = base + i * steps
            yield i
            if self.n - n != steps:
                raise ValueError(f"a loop body of {self.n - n} steps was declared with {steps}")
        self.base, self.n = base, n + n_iter * steps


def trunk(nc, a):
    ctx = ExitStack()
    with ctx:
        def sem(name):
            return ctx.enter_context(nc.semaphore(name))

        def sb(name, shape, dt=F32, stack=ctx):
            return stack.enter_context(nc.sbuf_tensor(name, shape, dt))

        raw = sb("w_raw", [P, SLOTS, CHUNK])
        w_hi = sb("w_hi", [P, SLOTS, CHUNK], F32R)
        w_lo = sb("w_lo", [P, SLOTS, CHUNK], F32R)
        xT = sb("xT", [P, KT, 2, T], F32R)
        xres = sb("xres", [P, NT, D])
        gb = sb("gb", [P, 2, GBC])
        xtmp = sb("xtmp", [P, 4, T])
        vec = sb("vec", [P, DEPTH * NV])
        const = sb("const", [P, NC])
        stats = sb("stats", [P, NT, 4, 6])
        mv = sb("mv", [P, NT, 2])
        rstd = sb("rstd", [P, 2, NT])
        neg_half = sb("neg_half", [P, NT])
        corr = sb("corr", [P, 2, T])

        mixers = ExitStack()
        with mixers:
            hT = sb("hT", [P, IN_TILES, T], F32, mixers)
            prm = sb("prm", [P, 15, 16], F32, mixers)
            ssm = ExitStack()
            with ssm:
                s1 = sb("s1", [P, 4, T], F32, ssm)
                s2 = sb("s2", [P, 4, T], F32, ssm)
                vr = sb("vr", [P, 4, T], F32, ssm)
                vi = sb("vi", [P, 4, T], F32, ssm)
                phase = sb("phase", [P, 2, 2, 4, T], F32, ssm)
                b_pad = sb("b_pad", [P, 2, 4, P], F32, ssm)
                c_raw = sb("c_raw", [P, 2, P], F32, ssm)
                c_pad = sb("c_pad", [P, 2, 640], F32, ssm)
                c_tmp = sb("c_tmp", [P, 2, P], F32, ssm)
                ptmp = sb("ptmp", [P, 2, 4, P], F32, ssm)
            mixT = sb("mixT", [P, KT, 2, T], F32R, mixers)
            glu = ExitStack()
            with glu:
                yT = sb("yT", [P, 4, 2, T], F32R, glu)
                pool_pad = sb("pool_pad", [P, 2, PAD + T], F32, glu)
                pool_d = sb("pool_d", [P, T], F32, glu)
                pool_w = sb("pool_w", [P, 4, P], F32, glu)
                ab = sb("ab", [P, 2, T], F32, glu)
            attn = ExitStack()
            with attn:
                qpad = sb("qpad", [P, 4, T], F32, attn)
                kdup = sb("kdup", [P, 4, T], F32, attn)
                vtok = sb("vtok", [P, NT, 4 * 64], F32, attn)
                vpad = sb("vpad", [P, NT, 2, P], F32, attn)
                rope = sb("rope", [P, 2, T], F32, attn)
                sc0 = sb("sc0", [P, 4, P], F32, attn)
                sc1 = sb("sc1", [P, 4, 2 * P], F32, attn)
                pT = sb("pT", [P, 12, P], F32, attn)
                sm = sb("sm", [P, 8, 8], F32, attn)
        mlp = ExitStack()
        with mlp:
            actT = sb("actT", [P, FF_TILES, 2, T], F32R, mlp)
            hbuf = sb("hbuf", [P, 2, T + 2], F32, mlp)
            cv = sb("cv", [P, 2, T], F32, mlp)
            sig = sb("sig", [P, T], F32, mlp)
            act_f = sb("act_f", [P, T], F32, mlp)

        ps = ctx.enter_context(nc.psum_tensor("ps", [P, 8, BANK], F32))

        x_loaded, const_loaded, vec_loaded = sem("x_loaded"), sem("const_loaded"), sem("vec_loaded")
        raw_loaded = [sem(f"raw_loaded{s}") for s in range(SLOTS)]
        hi_done, lo_done, chunk_used = sem("hi_done"), sem("lo_done"), sem("chunk_used")
        corr_ready, tile_evac = sem("corr_ready"), sem("tile_evac")
        z_ready, zT_ready, xtmp_ready, xT_ready = (sem("z_ready"), sem("zT_ready"), sem("xtmp_ready"),
                                                  sem("xT_ready"))
        gb_loaded, xres_ready = sem("gb_loaded"), sem("xres_ready")
        acc_evac, stats_ready, rstd_ready = sem("acc_evac"), sem("stats_ready"), sem("rstd_ready")
        prm_dve, prm_act, prm_ready = sem("prm_dve"), sem("prm_act"), sem("prm_ready")
        b_loaded, c_loaded = sem("b_loaded"), sem("c_loaded")
        phase_ready, phase_used, cpad_ready = sem("phase_ready"), sem("phase_used"), sem("cpad_ready")
        pads_zero = sem("pads_zero")
        bu_ready, bu_used, s_ready = sem("bu_ready"), sem("bu_used"), sem("s_ready")
        y_ready, y_used = sem("y_ready"), sem("y_used")
        gelu_dve, gelu_act, y_split = sem("gelu_dve"), sem("gelu_act"), sem("y_split")
        glu_corr, glu_sum, glu_sig, glu_out = sem("glu_corr"), sem("glu_sum"), sem("glu_sig"), sem("glu_out")
        mix_hi, mix_ready = sem("mix_hi"), sem("mix_ready")
        poolw_loaded, pool_in, pool_out = sem("poolw_loaded"), sem("pool_in"), sem("pool_out")
        swap_ready, rope_ready, kdup_ready = sem("swap_ready"), sem("rope_ready"), sem("kdup_ready")
        vT_ready, vtok_ready, vpad_ready = sem("vT_ready"), sem("vtok_ready"), sem("vpad_ready")
        q_ready = sem("q_ready")
        score_ready, max_ready, exp_ready, prob_ready = (sem("score_ready"), sem("max_ready"), sem("exp_ready"),
                                                         sem("prob_ready"))
        pT_ready, pT_copied, o_ready, attn_zero = sem("pT_ready"), sem("pT_copied"), sem("o_ready"), sem("attn_zero")
        conv_first, conv_done, sig_ready = sem("conv_first"), sem("conv_done"), sem("sig_ready")
        act_ready, act_hi, act_lo = sem("act_ready"), sem("act_hi"), sem("act_lo")
        dve_steps, pool_steps = sem("dve_steps"), sem("pool_steps")
        apart = sem("apart")
        out_ready, out_written = sem("out_ready"), sem("out_written")

        def settle(eng):
            eng.sem_inc(apart, 1)

        def chunks(l, m, s):
            return l * LAYER_CHUNKS + m * 4 + s + 1

        def vcol(l, col):
            return vec[:, bass.ds(l * NV + col, 1)]

        def flat(ap):
            return ap.rearrange("p a b -> p (a b)")

        block = ctx.enter_context(nc.Block())

        @block.sync
        def _(sp):
            sp.dma_start(xres[:], a["x"].rearrange("(t p) d -> p t d", p=P)).then_inc(x_loaded, 16)
            sp.dma_start(const[:], a["const"]).then_inc(const_loaded, 16)
            sp.dma_start(vec[:], a["vec"]).then_inc(vec_loaded, 16)

            def load(l, m, s, src):
                sp.wait_ge(lo_done, chunks(l, m, s))
                settle(sp)
                sp.dma_start(raw[:, s, :], src).then_inc(raw_loaded[s], 16)

            with sp.Fori(0, DEPTH) as l:
                with sp.Fori(0, IN_TILES // 2) as i:
                    for s in range(SLOTS):
                        load(l, IN_M + i, s, a["w_in"][l, i, s])
                for s in range(SLOTS):
                    load(l, GLU_M, s, a["glu_w"][l, s])
                with sp.Fori(0, 2) as h:
                    for k in range(KT):
                        e = (k + KT // 2) % KT
                        load(l, OUT_M + 4 * h + k // 4, k % 4,
                             a["w_out"][l, e * P:(e + 1) * P, bass.ds(h * HALF, HALF)])
                with sp.Fori(0, FF_TILES) as j:
                    for s in range(SLOTS):
                        load(l, UP_M + j, s, a["w_up"][l, j, s])
                with sp.Fori(0, 2) as h:
                    for k in range(FF_TILES):
                        load(l, DOWN_M + DOWN_GROUPS * h + k // 4, k % 4,
                             a["w_down"][l, k * P:(k + 1) * P, bass.ds(h * HALF, HALF)])
            for c in range(4):
                sp.wait_ge(out_ready, c + 1)
                sp.dma_start(a["out"].rearrange("(t p) d -> p t d", p=P)[:, :, c * BANK:(c + 1) * BANK],
                             xres[:, :, c * BANK:(c + 1) * BANK]).then_inc(out_written, 16)
            sp.wait_ge(out_written, 64)

        @block.tensor
        def _(pe):
            ident = const[:, C_ID:C_ID + P]
            perm = const[:, C_PERM:C_PERM + P]

            def parts_ready(l, m, s):
                pe.wait_ge(lo_done, SLOTS + chunks(l, m, s))

            def transpose_z(stage):
                for r in range(4):
                    if r >= 2:
                        pe.wait_ge(xtmp_ready, stage * 4 + r - 1)
                    for t in range(NT):
                        pe.wait_ge(z_ready, stage * 2 + t + 1)
                        for d in range(4):
                            mm = nc.tensor.transpose(
                                ps[:, 4 + 2 * (r % 2) + d // 2, bass.ds((d % 2) * T + t * P, P)],
                                xres[:, t, (4 * r + d) * P:(4 * r + d + 1) * P], ident)
                    mm.then_inc(zT_ready, 1)

            def project_tile(l, m, which, tile, stage):
                pe.wait_ge(tile_evac, l * TILES + tile + 1)
                for c in range(2):
                    s = 2 * which + c
                    parts_ready(l, m, s)
                    for k in range(8):
                        kk = 8 * c + k
                        if kk % 4 == 0:
                            pe.wait_ge(xT_ready, 1 + stage * 4 + kk // 4 + 1)
                        nc.tensor.matmul(ps[:, which, :], w_hi[:, s, k * P:(k + 1) * P], flat(xT[:, kk]),
                                         start=(kk == 0), stop=False)
                        mm = nc.tensor.matmul(ps[:, which, 0:T], w_lo[:, s, k * P:(k + 1) * P], xT[:, kk, 0, :],
                                              start=False, stop=(kk == KT - 1))
                    mm.then_inc(chunk_used, 1)

            def project_tokens(l, m0, act, n_k, half_no, before_k):
                for k in range(n_k):
                    before_k(k)
                    m, s = m0 + k // 4, k % 4
                    parts_ready(l, m, s)
                    for t in range(NT):
                        hi = act(k)[:, 0, t * P:(t + 1) * P]
                        lo = act(k)[:, 1, t * P:(t + 1) * P]
                        for c in range(2):
                            if k == 0:
                                pe.wait_ge(acc_evac, half_no * 4 + 2 * t + c + 1)
                            cols = slice(c * BANK, (c + 1) * BANK)
                            acc = ps[:, 2 * t + c, :]
                            nc.tensor.matmul(acc, hi, w_hi[:, s, cols], start=(k == 0), stop=False)
                            nc.tensor.matmul(acc, hi, w_lo[:, s, cols], start=False, stop=False)
                            mm = nc.tensor.matmul(acc, lo, w_hi[:, s, cols], start=False, stop=(k == n_k - 1))
                    mm.then_inc(chunk_used, 2 if k == n_k - 1 and n_k % 4 else 1)

            def input_of_states(l, c):
                pe.wait_ge(b_loaded, (l * 4 + c + 1) * 64)
                pe.wait_ge(bu_used, l * 4 + c + 1)
                for ri in range(2):
                    for j in range(4):
                        mm = nc.tensor.matmul(ps[:, 2 + 2 * ri + j // 2, bass.ds((j % 2) * T, T)], b_pad[:, ri, j, :],
                                              hT[:, bass.ds(SSM0 + c, 1), :].rearrange("p a b -> p (a b)"),
                                              start=True, stop=True)
                mm.then_inc(bu_ready, 1)

            def output_of_states(l, c):
                pe.wait_ge(s_ready, l * 4 + c + 1)
                pe.wait_ge(cpad_ready, l * 4 + c + 1)
                for j in range(4):
                    for ri, src in enumerate((s1, s2)):
                        mm = nc.tensor.matmul(ps[:, 6, 0:T], c_pad[:, ri, j * P:(j + 1) * P], src[:, j, :],
                                              start=(j == 0 and ri == 0), stop=(j == 3 and ri == 1))
                mm.then_inc(y_ready, 1)

            def attention_group(l, g):
                n = l * 4 + g
                nc.tensor.matmul(ps[:, 7, :], perm,
                                 hT[:, bass.ds(Q0 + 2 * g, 2), :].rearrange("p a b -> p (a b)"),
                                 start=True, stop=True).then_inc(swap_ready, 1)
                pe.wait_ge(q_ready, n + 1)
                for h in range(4):
                    nc.tensor.matmul(ps[:, 2, h * P:(h + 1) * P], qpad[:, h, 0:P],
                                     kdup[:, bass.ds(g, 1), 0:P].rearrange("p a b -> p (a b)"),
                                     start=True, stop=True)
                for h in range(4):
                    mm = nc.tensor.matmul(ps[:, 3 + h // 2, bass.ds((h % 2) * T, T)], qpad[:, h, P:T],
                                          kdup[:, bass.ds(g, 1), :].rearrange("p a b -> p (a b)"),
                                          start=True, stop=True)
                mm.then_inc(score_ready, 1)
                pe.wait_ge(prob_ready, n + 1)
                for h in range(4):
                    for b, src in enumerate((sc0[:, h, :], sc1[:, h, 0:P], sc1[:, h, P:2 * P])):
                        i = 3 * h + b
                        mm = nc.tensor.transpose(ps[:, 5 + i // 4, bass.ds((i % 4) * P, P)], src, ident)
                mm.then_inc(pT_ready, 1)
                pe.wait_ge(pT_copied, n + 1)
                pe.wait_ge(vpad_ready, n + 1)
                for hp in range(2):
                    for q in range(2):
                        out = ps[:, 2, bass.ds(hp * T + q * P, P)]
                        pairs = [(vpad[:, 0, par, :], pT[:, 3 * (2 * hp + par) + q, :]) for par in range(2)]
                        if q:
                            pairs += [(vpad[:, 1, par, :], pT[:, 3 * (2 * hp + par) + 2, :]) for par in range(2)]
                        for i, (v, p) in enumerate(pairs):
                            mm = nc.tensor.matmul(out, v, p, start=(i == 0), stop=(i == len(pairs) - 1))
                mm.then_inc(o_ready, 1)

            nc.tensor.sem_inc(chunk_used, SLOTS)
            pe.wait_ge(const_loaded, 16)
            with pe.Fori(0, DEPTH) as l:
                transpose_z(l * 2)
                with pe.Fori(0, IN_TILES // 2) as i:
                    for which in range(2):
                        project_tile(l, IN_M + i, which, i * 2 + which, l * 2)

                pe.wait_ge(tile_evac, l * TILES + IN_TILES + 2)
                input_of_states(l, 0)
                with pe.Fori(0, 3) as c:
                    input_of_states(l, c + 1)
                    output_of_states(l, c)
                output_of_states(l, 3)

                pe.wait_ge(y_split, l + 1)
                for s in range(4):
                    parts_ready(l, GLU_M, s)
                    pe.wait_ge(glu_sum, l * 4 + s + 1)
                    for k in range(4):
                        for ab_i in range(2):
                            wcol = slice((2 * k + ab_i) * P, (2 * k + ab_i + 1) * P)
                            nc.tensor.matmul(ps[:, 2 + ab_i, :], w_hi[:, s, wcol], flat(yT[:, k]),
                                             start=(k == 0), stop=False)
                            mm = nc.tensor.matmul(ps[:, 2 + ab_i, 0:T], w_lo[:, s, wcol], yT[:, k, 0, :],
                                                  start=False, stop=(k == 3))
                    mm.then_inc(chunk_used, 1)

                pe.wait_ge(poolw_loaded, (l + 1) * 16)
                for gi in range(4):
                    pe.wait_ge(pool_in, l * 4 + gi + 1)
                    nc.tensor.matmul(ps[:, 6, 0:T], pool_w[:, gi, :], pool_d[:], start=True,
                                     stop=True).then_inc(pool_out, 1)

                nc.tensor.matmul(ps[:, 7, :], perm, flat(hT[:, K0:K0 + 2, :]), start=True,
                                 stop=True).then_inc(swap_ready, 1)
                for b in range(NT):
                    for i in range(2):
                        mm = nc.tensor.transpose(ps[:, 5, bass.ds(b * T + i * P, P)], hT[:, V0 + i, b * P:(b + 1) * P],
                                                 ident)
                mm.then_inc(vT_ready, 1)
                pe.wait_ge(kdup_ready, l + 1)
                settle(pe)
                with pe.Fori(0, 4) as g:
                    attention_group(l, g)

                with pe.Fori(0, 2) as h:
                    project_tokens(l, OUT_M + 4 * h, lambda k: mixT[:, (k + KT // 2) % KT], KT, l * 4 + h,
                                   lambda k: pe.wait_ge(mix_ready, l * 16 + k + 1))
                transpose_z(l * 2 + 1)
                with pe.Fori(0, FF_TILES) as j:
                    for which in range(2):
                        project_tile(l, UP_M + j, which, IN_TILES + j * 2 + which, l * 2 + 1)
                with pe.Fori(0, 2) as h:
                    project_tokens(l, DOWN_M + DOWN_GROUPS * h, lambda k: actT[:, k], FF_TILES, l * 4 + 2 + h,
                                   lambda k: pe.wait_ge(act_lo, l * FF_TILES + k + 1))

        @block.scalar
        def _(act):
            def round_hi(l, m, s):
                act.wait_ge(raw_loaded[s], loads(l, m, s))
                act.wait_ge(chunk_used, chunks(l, m, s))
                nc.scalar.activation(w_hi[:, s, :], raw[:, s, :], ACT.Copy).then_inc(hi_done, 1)

            def loads(l, m, s):
                return (l * (LAYER_M - (SHORT if s == 3 else 0)) + m + 1) * 16

            def round_hi_down(l, h, q, s, count=1):
                act.wait_ge(raw_loaded[s], loads(l, DOWN_M + (DOWN_GROUPS - (1 if s == 3 else 0)) * h + q, s))
                act.wait_ge(chunk_used, chunks(l, DOWN_M + DOWN_GROUPS * h + q, s))
                nc.scalar.activation(w_hi[:, s, :], raw[:, s, :], ACT.Copy).then_inc(hi_done, count)

            def correction(l, tile, which, m, s):
                act.wait_ge(chunk_used, SLOTS + chunks(l, m, s))
                act.wait_ge(tile_evac, l * TILES + tile + 1)
                nc.scalar.activation(corr[:, which, :], ps[:, which, T:2 * T], ACT.Copy).then_inc(corr_ready, 1)

            def affine(l, stage, col, m):
                for r in range(4):
                    act.wait_ge(zT_ready, stage * 4 + r + 1)
                    act.wait_ge(xT_ready, stage * 4 + r + 1)
                    for d in range(4):
                        ins = nc.scalar.activation(
                            xtmp[:, d, :], ps[:, 4 + 2 * (r % 2) + d // 2, bass.ds((d % 2) * T, T)],
                            ACT.Identity, scale=vcol(l, col + 4 * r + d), bias=vcol(l, col + KT + 4 * r + d))
                    ins.then_inc(xtmp_ready, 1)
                    round_hi(l, m, r)

            def conv_first_tap(l, j, which, tile):
                f = j + FF_TILES * which
                act.wait_ge(tile_evac, 2 + l * TILES + tile + 1)
                nc.scalar.activation(cv[:, which, :], hbuf[:, which, 0:T], ACT.Identity,
                                     scale=vcol(l, V_CONVW + f), bias=vcol(l, V_CONVB + f)).then_inc(conv_first, 1)

            def gate_part(l, j, with_chunks, m):
                tile = IN_TILES + 2 * j + 1
                correction(l, tile, 1, UP_M + j, 3)
                conv_first_tap(l, j, 1, tile)
                if with_chunks:
                    round_hi(l, m, 2)
                act.wait_ge(conv_done, l * FF_TILES + j + 1)
                nc.scalar.activation(sig[:], cv[:, 1, :], ACT.Tanh, scale=0.5).then_inc(sig_ready, 1)
                if with_chunks:
                    round_hi(l, m, 3)
                act.wait_ge(act_ready, l * FF_TILES + j + 1)
                nc.scalar.activation(actT[:, bass.ds(j, 1), 0, :].rearrange("p a b -> p (a b)"), act_f[:],
                                     ACT.Copy).then_inc(act_hi, 1)

            def value_part(l, j):
                tile = IN_TILES + 2 * j
                correction(l, tile, 0, UP_M + j, 1)
                conv_first_tap(l, j, 0, tile)

            act.wait_ge(vec_loaded, 16)
            with act.Fori(0, DEPTH) as l:
                affine(l, l * 2, V_G0, IN_M)
                correction(l, 0, 0, IN_M, 1)
                with act.Fori(0, IN_TILES // 2 - 1) as i:
                    round_hi(l, IN_M + 1 + i, 0)
                    round_hi(l, IN_M + 1 + i, 1)
                    correction(l, 2 * i + 1, 1, IN_M + i, 3)
                    round_hi(l, IN_M + 1 + i, 2)
                    round_hi(l, IN_M + 1 + i, 3)
                    correction(l, 2 * i + 2, 0, IN_M + 1 + i, 1)
                correction(l, IN_TILES - 1, 1, IN_M + IN_TILES // 2 - 1, 3)
                for s in range(SLOTS):
                    round_hi(l, GLU_M, s)

                act.wait_ge(prm_dve, l + 1)
                nc.scalar.activation(prm[:, 6:9, :], prm[:, 6:9, :], ACT.Sin).then_inc(prm_act, 1)

                act.wait_ge(y_used, 1 + (l + 1) * 4)
                nc.scalar.activation(flat(s1[:]), flat(hT[:, SSM0:SSM0 + 4, :]), ACT.Square).then_inc(gelu_act, 1)
                act.wait_ge(gelu_dve, 2 * l + 1)
                nc.scalar.activation(flat(s2[:]), flat(s2[:]), ACT.Tanh,
                                     scale=0.7978845608028654).then_inc(gelu_act, 1)
                act.wait_ge(gelu_dve, 2 * l + 2)
                nc.scalar.activation(yT[:, :, 0, :], vr[:], ACT.Copy, scale=0.5).then_inc(gelu_act, 1)
                for s in range(4):
                    act.wait_ge(chunk_used, SLOTS + chunks(l, GLU_M, s))
                    if s:
                        act.wait_ge(mix_ready, l * 16 + s)
                    nc.scalar.activation(ab[:], ps[:, 2:4, T:2 * T], ACT.Copy).then_inc(glu_corr, 1)
                    act.wait_ge(glu_sum, 1 + l * 4 + s + 1)
                    nc.scalar.activation(ab[:, 1, :], ab[:, 1, :], ACT.Tanh, scale=0.5).then_inc(glu_sig, 1)
                    act.wait_ge(glu_out, l * 4 + s + 1)
                    nc.scalar.activation(mixT[:, 12 + s, 0, :], ab[:, 0, :], ACT.Copy).then_inc(mix_hi, 1)
                for gi in range(4):
                    act.wait_ge(pool_out, l * 4 + gi + 1)
                    nc.scalar.activation(mixT[:, 8 + gi, 0, :], ps[:, 6, 0:T], ACT.Copy,
                                         scale=vcol(l, V_PSC + gi)).then_inc(mix_hi, 1)
                act.wait_ge(vT_ready, l + 1)
                nc.scalar.activation(flat(vtok[:]), ps[:, 5, :], ACT.Copy).then_inc(vtok_ready, 1)
                act.wait_ge(rope_ready, l + 1)
                for kv in range(2):
                    for half in range(2):
                        ins = nc.scalar.activation(kdup[64 * half:64 * half + 64, kv::2, :],
                                                   hT[64 * kv:64 * kv + 64, K0:K0 + 2, :], ACT.Copy)
                ins.then_inc(kdup_ready, 1)
                with act.Fori(0, 4) as g:
                    n = l * 4 + g
                    act.wait_ge(max_ready, n + 1)
                    for b, scores in enumerate((sc0, sc1)):
                        for h in range(4):
                            nc.scalar.activation(scores[:, h, :], scores[:, h, :], ACT.Exp,
                                                 bias=sm[:, 2 + b, h:h + 1], accum_out=sm[:, 4 + b, h:h + 1])
                    nc.scalar.activation(sm[:, 6, :], sm[:, 6, :], ACT.Exp).then_inc(exp_ready, 1)
                    act.wait_ge(pT_ready, n + 1)
                    nc.scalar.activation(flat(pT[:]), ps[:, 5:8, :].rearrange("p a b -> p (a b)"),
                                         ACT.Copy).then_inc(pT_copied, 1)
                    act.wait_ge(o_ready, n + 1)
                    nc.scalar.activation(mixT[:, bass.ds(2 * g, 2), 0, :],
                                         ps[:, 2, :].rearrange("p (a b) -> p a b", a=2), ACT.Copy).then_inc(mix_hi, 1)

                with act.Fori(0, 8) as q:
                    for s in range(SLOTS):
                        round_hi(l, OUT_M + q, s)
                affine(l, l * 2 + 1, V_G1, UP_M)
                value_part(l, 0)
                with act.Fori(0, FF_TILES - 1) as j:
                    round_hi(l, UP_M + 1 + j, 0)
                    round_hi(l, UP_M + 1 + j, 1)
                    gate_part(l, j, True, UP_M + 1 + j)
                    value_part(l, j + 1)
                gate_part(l, FF_TILES - 1, False, 0)
                with act.Fori(0, 2) as h:
                    with act.Fori(0, DOWN_GROUPS - 1) as q:
                        for s in range(SLOTS):
                            round_hi_down(l, h, q, s)
                    for s in range(FF_TILES % 4):
                        round_hi_down(l, h, DOWN_GROUPS - 1, s, 2 if s == FF_TILES % 4 - 1 else 1)

        @block.vector
        def _(dve):
            st = Steps(dve, dve_steps)
            v = nc.vector

            def split_lo(l, m, s, last=1):
                dve.wait_ge(hi_done, chunks(l, m, s))
                v.tensor_tensor(w_lo[:, s, :], raw[:, s, :], w_hi[:, s, :].bitcast(F32),
                                ALU.subtract).then_inc(lo_done, last)

            def split_x(l, stage, m):
                for r in range(4):
                    dve.wait_ge(xtmp_ready, stage * 4 + r + 1)
                    step(v.tensor_copy(xT[:, 4 * r:4 * r + 4, 0, :], xtmp[:]))
                    v.tensor_tensor(xT[:, 4 * r:4 * r + 4, 1, :], xtmp[:], xT[:, 4 * r:4 * r + 4, 0, :].bitcast(F32),
                                    ALU.subtract).then_inc(xT_ready, 1)
                    split_lo(l, m, r)

            def evac_in(l, tile, which):
                dve.wait_ge(corr_ready, l * TILES + tile + 1)
                v.tensor_tensor(hT[:, bass.ds(tile, 1), :].rearrange("p a b -> p (a b)"), ps[:, which, 0:T],
                                corr[:, which, :], ALU.add).then_inc(tile_evac, 1)

            def conv_tile(l, j, which):
                tile = IN_TILES + 2 * j + which
                f = j + FF_TILES * which
                dve.wait_ge(corr_ready, l * TILES + tile + 1)
                v.tensor_tensor(hbuf[:, which, 2:T + 2], ps[:, which, 0:T], corr[:, which, :],
                                ALU.add).then_inc(tile_evac, 1)
                dve.wait_ge(tile_evac, 2 + l * TILES + tile + 1)
                dve.wait_ge(conv_first, l * 2 * FF_TILES + 2 * j + which + 1)
                st.mark(v.scalar_tensor_tensor(cv[:, which, :], hbuf[:, which, 1:T + 1],
                                               vcol(l, V_CONVW + 2 * FF_TILES + f), cv[:, which, :],
                                               ALU.mult, ALU.add))
                st.wait()
                ins = v.scalar_tensor_tensor(cv[:, which, :], hbuf[:, which, 2:T + 2],
                                             vcol(l, V_CONVW + 4 * FF_TILES + f), cv[:, which, :],
                                             ALU.mult, ALU.add)
                if which:
                    ins.then_inc(conv_done, 1)
                else:
                    st.mark(ins)

            def gated(l, j):
                dve.wait_ge(sig_ready, l * FF_TILES + j + 1)
                st.mark(v.scalar_tensor_tensor(cv[:, 1, :], sig[:], 1.0, cv[:, 1, :], ALU.add, ALU.mult))
                st.wait()
                v.scalar_tensor_tensor(act_f[:], cv[:, 1, :], 0.5, cv[:, 0, :], ALU.mult,
                                       ALU.mult).then_inc(act_ready, 1)

            def gated_lo(l, j):
                dve.wait_ge(act_hi, l * FF_TILES + j + 1)
                ap = actT[:, bass.ds(j, 1), :, :].rearrange("p a h b -> p (a h) b")
                v.tensor_tensor(ap[:, 1, :], act_f[:], ap[:, 0, :].bitcast(F32), ALU.subtract).then_inc(act_lo, 1)

            def evac_half(l, h, half_no, m_last, stage, s_last):
                dve.wait_ge(chunk_used, SLOTS + m_last)
                dve.wait_ge(xres_ready, stage + 1)
                for t in range(NT):
                    for c in range(2):
                        y = xres[:, t, bass.ds(h * HALF + c * BANK, BANK)]
                        v.scalar_tensor_tensor(y, y, ALPHA, ps[:, 2 * t + c, :], ALU.mult,
                                               ALU.add).then_inc(acc_evac, 1)
                        dve.wait_ge(acc_evac, 4 + half_no * 4 + 2 * t + c + 1)
                        st.mark(v.bn_stats(stats[:, t, bass.ds(2 * h + c, 1), :].rearrange("p a b -> p (a b)"), y))

            def normalise(stage):
                st.wait()
                settle(dve)
                for t in range(NT):
                    v.bn_aggr(mv[:, t, :], stats[:, t, :, :].rearrange("p a b -> p (a b)")).then_inc(stats_ready, 1)
                dve.wait_ge(stats_ready, stage * 2 + 2)
                dve.wait_ge(rstd_ready, stage + 1)
                for t in range(NT):
                    v.tensor_scalar(xres[:, t, :], xres[:, t, :], mv[:, t, 0:1], rstd[:, 1, t:t + 1],
                                    ALU.subtract, ALU.mult).then_inc(z_ready, 1)

            def step(ins):
                st.mark(ins)
                st.wait()

            def exp_parts(x, n, r, acc, two_n):
                step(v.tensor_scalar(n, x, 1.0 / 0.6931471805599453, 12582912.0, ALU.mult, ALU.add))
                step(v.tensor_scalar(n, n, 12582912.0, None, ALU.subtract))
                step(v.scalar_tensor_tensor(r, n, -0.693359375, x, ALU.mult, ALU.add))
                step(v.scalar_tensor_tensor(r, n, 2.12194440e-4, r, ALU.mult, ALU.add))
                step(v.tensor_scalar(acc, r, 1.0 / 40320, None, ALU.mult))
                for c in (1 / 5040, 1 / 720, 1 / 120, 1 / 24, 1 / 6, 0.5, 1.0):
                    step(v.scalar_tensor_tensor(acc, acc, c, r, ALU.add, ALU.mult))
                step(v.tensor_scalar(n, n, 127.0, 0.0, ALU.add, ALU.max))
                step(v.tensor_scalar(two_n.bitcast(I32), n, 255.0, float(2 ** 23), ALU.min, ALU.mult))

            def state_parameters(l):
                lr = vec[:, bass.ds(l * NV + V_LR, 16)]
                li = vec[:, bass.ds(l * NV + V_LI, 16)]
                ldt = vec[:, bass.ds(l * NV + V_LDT, 16)]
                dt, mag, em1, zr, zi, th = (prm[:, i, :] for i in range(6))
                cs, sn, sh = (prm[:, i, :] for i in range(6, 9))
                n, r, acc, two_n, t1, t2 = (prm[:, i, :] for i in range(9, 15))
                step(v.tensor_scalar(t1, ldt, -150.0, 150.0, ALU.max, ALU.min))
                exp_parts(t1, n, r, acc, two_n)
                step(v.tensor_tensor(acc, acc, two_n, ALU.mult))
                step(v.tensor_tensor(dt, acc, two_n, ALU.add))
                step(v.tensor_tensor(th, li, dt, ALU.mult))
                step(v.tensor_scalar(n, th, 0.15915494309189535, 12582912.0, ALU.mult, ALU.add))
                step(v.tensor_scalar(n, n, 12582912.0, None, ALU.subtract))
                step(v.scalar_tensor_tensor(th, n, -6.28125, th, ALU.mult, ALU.add))
                step(v.scalar_tensor_tensor(th, n, -1.934051513671875e-3, th, ALU.mult, ALU.add))
                step(v.scalar_tensor_tensor(th, n, -1.2556659146019e-6, th, ALU.mult, ALU.add))
                step(v.tensor_scalar(sn, th, 3.1415925, -3.1415925, ALU.min, ALU.max))
                step(v.tensor_scalar(sh, sn, 0.5, None, ALU.mult))
                step(v.tensor_scalar(cs, sn, -1.0, None, ALU.mult))
                step(v.tensor_tensor(cs, cs, sn, ALU.max))
                ins = v.tensor_scalar(cs, cs, -1.0, 1.5707963267948966, ALU.mult, ALU.add)
                ins.then_inc(prm_dve, 1)
                step(v.tensor_tensor(t2, lr, dt, ALU.mult))
                step(v.tensor_scalar(t2, t2, -150.0, 150.0, ALU.max, ALU.min))
                exp_parts(t2, n, r, acc, two_n)
                step(v.tensor_tensor(acc, acc, two_n, ALU.mult))
                step(v.tensor_tensor(mag, acc, two_n, ALU.add))
                step(v.scalar_tensor_tensor(em1, two_n, -1.0, acc, ALU.add, ALU.add))
                dve.wait_ge(prm_act, l + 1)
                step(v.tensor_tensor(t1, sh, sh, ALU.mult))
                step(v.tensor_tensor(t2, em1, cs, ALU.mult))
                step(v.scalar_tensor_tensor(t1, t1, -2.0, t2, ALU.mult, ALU.add))
                step(v.tensor_tensor(t2, mag, sn, ALU.mult))
                step(v.tensor_tensor(n, lr, lr, ALU.mult))
                step(v.tensor_tensor(r, li, li, ALU.mult))
                step(v.tensor_tensor(n, n, r, ALU.add))
                step(v.reciprocal(n, n))
                step(v.tensor_tensor(zr, t1, lr, ALU.mult))
                step(v.tensor_tensor(r, t2, li, ALU.mult))
                step(v.tensor_tensor(zr, zr, r, ALU.add))
                step(v.tensor_tensor(zr, zr, n, ALU.mult))
                step(v.tensor_tensor(zi, t2, lr, ALU.mult))
                step(v.tensor_tensor(r, t1, li, ALU.mult))
                step(v.tensor_tensor(zi, zi, r, ALU.subtract))
                v.tensor_tensor(zi, zi, n, ALU.mult).then_inc(prm_ready, 1)
                dve.wait_ge(prm_ready, l + 1)

            def state_scan(l, c, slot):
                n = l * 4 + c
                co, si = phase[:, slot, 0], phase[:, slot, 1]
                p, q = ps[:, 2:4, :].rearrange("p a (j t) -> p (a j) t", j=2), \
                    ps[:, 4:6, :].rearrange("p a (j t) -> p (a j) t", j=2)
                dve.wait_ge(phase_ready, n + 1)
                dve.wait_ge(bu_ready, n + 1)
                v.tensor_tensor(vr[:], co, p, ALU.mult)
                v.tensor_tensor(vi[:], co, q, ALU.mult)
                v.tensor_tensor(s1[:], si, q, ALU.mult)
                v.tensor_tensor(s2[:], si, p, ALU.mult).then_inc(bu_used, 1)
                dve.wait_ge(bu_used, 1 + n + 1)
                v.tensor_tensor(vr[:], vr[:], s1[:], ALU.add)
                step(v.tensor_tensor(vi[:], vi[:], s2[:], ALU.subtract))
                for j in range(4):
                    for w in (vr, vi):
                        ins = v.tensor_tensor_scan(w[:, j, :], prm[:, 1, bass.ds(c * 4 + j, 1)].broadcast_to([P, T]),
                                                   w[:, j, :], 0.0, ALU.mult, ALU.add)
                step(ins)
                v.tensor_tensor(s1[:], co, vr[:], ALU.mult)
                step(v.tensor_tensor(s2[:], si, vr[:], ALU.mult))
                v.tensor_tensor(vr[:], si, vi[:], ALU.mult)
                v.tensor_tensor(vi[:], co, vi[:], ALU.mult).then_inc(phase_used, 1)
                dve.wait_ge(phase_used, 2 + n + 1)
                v.tensor_tensor(s1[:], s1[:], vr[:], ALU.subtract)
                v.tensor_tensor(s2[:], s2[:], vi[:], ALU.add).then_inc(s_ready, 1)
                dve.wait_ge(y_ready, n + 1)
                u = hT[:, bass.ds(SSM0 + c, 1), :].rearrange("p a b -> p (a b)")
                v.scalar_tensor_tensor(u, u, vcol(l, V_D + c), ps[:, 6, 0:T], ALU.mult, ALU.add).then_inc(y_used, 1)
                dve.wait_ge(y_used, 1 + n + 1)

            def pool_group(l, gi, w):
                u = hT[:, POOL0 + gi, :]
                step(v.tensor_copy(pool_pad[:, 0, PAD:], u))
                src, shift = 0, 1
                while shift < w:
                    step(v.tensor_tensor(pool_pad[:, 1 - src, PAD:], pool_pad[:, src, PAD:],
                                         pool_pad[:, src, PAD - shift:PAD + T - shift], ALU.add))
                    src, shift = 1 - src, 2 * shift
                if gi:
                    dve.wait_ge(pool_out, l * 4 + gi)
                sums = pool_pad[:, src, PAD:]
                step(v.tensor_tensor(pool_d[:, 0:w], sums[:, 0:w], const[:, C_RECIP:C_RECIP + w], ALU.mult))
                v.tensor_tensor(pool_d[:, 0:w], pool_d[:, 0:w], u[:, 0:w], ALU.subtract)
                v.scalar_tensor_tensor(pool_d[:, w:], sums[:, w:], 1.0 / w, u[:, w:], ALU.mult,
                                       ALU.subtract).then_inc(pool_in, 1)
                dve.wait_ge(pool_in, l * 4 + gi + 1)

            def rotate(x, swapped):
                cos = const[:, C_COS:C_COS + T].unsqueeze(1).broadcast_to([P, 2, T])
                sin = const[:, C_SIN:C_SIN + T].unsqueeze(1).broadcast_to([P, 2, T])
                v.tensor_tensor(rope[:], swapped, sin, ALU.mult)
                step(v.tensor_tensor(x, x, cos, ALU.mult))

            def attention_group(l, g):
                n = l * 4 + g
                swapped = ps[:, 7, :].rearrange("p (a b) -> p a b", a=2)
                dve.wait_ge(swap_ready, l * 5 + g + 2)
                rotate(hT[:, bass.ds(Q0 + 2 * g, 2), :], swapped)
                dve.wait_ge(attn_zero, l + 1)
                for half in range(2):
                    part = slice(64 * half, 64 * half + 64)
                    ins = v.tensor_tensor(qpad[part, half::2, :], hT[part, bass.ds(Q0 + 2 * g, 2), :], rope[part],
                                          ALU.add)
                ins.then_inc(q_ready, 1)
                dve.wait_ge(q_ready, n + 1)
                dve.wait_ge(score_ready, n + 1)
                causal = const[:, C_MASK + P:C_MASK + 2 * P].unsqueeze(1).broadcast_to([P, 4, P])
                window = const[:, C_MASK:C_MASK + 2 * P].unsqueeze(1).broadcast_to([P, 4, 2 * P])
                v.scalar_tensor_tensor(sc0[:], ps[:, 2, :].rearrange("p (h k) -> p h k", h=4), SCALE, causal,
                                       ALU.mult, ALU.add)
                step(v.scalar_tensor_tensor(sc1[:], ps[:, 3:5, :].rearrange("p a (h k) -> p (a h) k", h=2), SCALE,
                                            window, ALU.mult, ALU.add))
                v.tensor_reduce(sm[:, 0, 0:4], sc0[:], AX_X, ALU.max)
                step(v.tensor_reduce(sm[:, 1, 0:4], sc1[:], AX_X, ALU.max))
                sink = vec[:, bass.ds(l * NV + V_SINK + g * 4, 4)]
                v.tensor_tensor(sm[:, 0, 0:4], sm[:, 0, 0:4], sink, ALU.max)
                step(v.tensor_tensor(sm[:, 1, 0:4], sm[:, 1, 0:4], sink, ALU.max))
                v.tensor_scalar(sm[:, 2:4, 0:4], sm[:, 0:2, 0:4], -1.0, None, ALU.mult)
                v.tensor_tensor(sm[:, 6, 0:4], sink, sm[:, 0, 0:4], ALU.subtract)
                v.tensor_tensor(sm[:, 6, 4:8], sink, sm[:, 1, 0:4], ALU.subtract).then_inc(max_ready, 1)
                dve.wait_ge(max_ready, n + 1)
                dve.wait_ge(exp_ready, n + 1)
                v.tensor_tensor(sm[:, 7, 0:4], sm[:, 4, 0:4], sm[:, 6, 0:4], ALU.add)
                step(v.tensor_tensor(sm[:, 7, 4:8], sm[:, 5, 0:4], sm[:, 6, 4:8], ALU.add))
                step(v.reciprocal(sm[:, 7, :], sm[:, 7, :]))
                v.tensor_tensor(sc0[:], sc0[:], sm[:, 7, 0:4].unsqueeze(2).broadcast_to([P, 4, P]), ALU.mult)
                v.tensor_tensor(sc1[:], sc1[:], sm[:, 7, 4:8].unsqueeze(2).broadcast_to([P, 4, 2 * P]),
                                ALU.mult).then_inc(prob_ready, 1)
                dve.wait_ge(prob_ready, n + 1)
                dve.wait_ge(mix_hi, l * 12 + 8 + g + 1)
                for i in range(2):
                    dst = mixT[:, bass.ds(2 * g + i, 1), :, :].rearrange("p a h b -> p (a h) b")
                    v.tensor_tensor(dst[:, 1, :], ps[:, 2, i * T:(i + 1) * T], dst[:, 0, :].bitcast(F32),
                                    ALU.subtract).then_inc(mix_ready, 1)
                dve.wait_ge(mix_ready, l * 16 + 8 + g * 2 + 2)

            v.sem_inc(lo_done, SLOTS)
            v.sem_inc(tile_evac, 2)
            v.sem_inc(acc_evac, 4)
            v.sem_inc(bu_used, 1)
            v.sem_inc(y_used, 1)
            v.sem_inc(glu_sum, 1)
            v.sem_inc(phase_used, 2)
            v.sem_inc(xT_ready, 1)
            dve.wait_ge(x_loaded, 16)
            dve.wait_ge(vec_loaded, 16)
            dve.wait_ge(const_loaded, 16)
            v.sem_inc(z_ready, 2)
            with st.loop(DEPTH, DVE_LAYER) as l:
                split_x(l, l * 2, IN_M)
                evac_in(l, 0, 0)
                with st.loop(IN_TILES // 2 - 1, 0) as i:
                    split_lo(l, IN_M + 1 + i, 0)
                    split_lo(l, IN_M + 1 + i, 1)
                    evac_in(l, 2 * i + 1, 1)
                    split_lo(l, IN_M + 1 + i, 2)
                    split_lo(l, IN_M + 1 + i, 3)
                    evac_in(l, 2 * i + 2, 0)
                evac_in(l, IN_TILES - 1, 1)
                dve.wait_ge(tile_evac, 2 + l * TILES + IN_TILES)
                for s in range(SLOTS):
                    split_lo(l, GLU_M, s)
                state_parameters(l)
                settle(dve)
                with st.loop(2, 2 * 3) as cc:
                    for slot in range(2):
                        state_scan(l, cc * 2 + slot, slot)
                y = flat(hT[:, SSM0:SSM0 + 4, :])
                dve.wait_ge(gelu_act, 3 * l + 1)
                step(v.tensor_scalar(flat(s1[:]), flat(s1[:]), 0.044715, 1.0, ALU.mult, ALU.add))
                v.tensor_tensor(flat(s2[:]), flat(s1[:]), y, ALU.mult).then_inc(gelu_dve, 1)
                dve.wait_ge(gelu_act, 3 * l + 2)
                v.scalar_tensor_tensor(flat(vr[:]), flat(s2[:]), 1.0, y, ALU.add, ALU.mult).then_inc(gelu_dve, 1)
                dve.wait_ge(gelu_dve, 2 * l + 2)
                dve.wait_ge(gelu_act, 3 * l + 3)
                v.scalar_tensor_tensor(yT[:, :, 1, :], vr[:], 0.5, yT[:, :, 0, :].bitcast(F32), ALU.mult,
                                       ALU.subtract).then_inc(y_split, 1)
                for s in range(4):
                    dve.wait_ge(glu_corr, l * 4 + s + 1)
                    v.tensor_tensor(ab[:], ab[:], ps[:, 2:4, 0:T], ALU.add).then_inc(glu_sum, 1)
                    dve.wait_ge(glu_sig, l * 4 + s + 1)
                    step(v.tensor_scalar(ab[:, 1, :], ab[:, 1, :], 0.5, 0.5, ALU.mult, ALU.add))
                    v.tensor_tensor(ab[:, 0, :], ab[:, 0, :], ab[:, 1, :], ALU.mult).then_inc(glu_out, 1)
                    dve.wait_ge(mix_hi, l * 12 + s + 1)
                    v.tensor_tensor(mixT[:, 12 + s, 1, :], ab[:, 0, :], mixT[:, 12 + s, 0, :].bitcast(F32),
                                    ALU.subtract).then_inc(mix_ready, 1)
                dve.wait_ge(mix_ready, l * 16 + 4)
                step(v.memset(pool_pad[:, :, 0:PAD], 0.0))
                for gi, w in enumerate(POOL_WINDOWS):
                    pool_group(l, gi, w)
                    dve.wait_ge(mix_hi, l * 12 + 4 + gi + 1)
                    v.scalar_tensor_tensor(mixT[:, 8 + gi, 1, :], ps[:, 6, 0:T], vcol(l, V_PSC + gi),
                                           mixT[:, 8 + gi, 0, :].bitcast(F32), ALU.mult,
                                           ALU.subtract).then_inc(mix_ready, 1)
                dve.wait_ge(mix_ready, l * 16 + 8)

                dve.wait_ge(swap_ready, l * 5 + 1)
                keys = hT[:, K0:K0 + 2, :]
                rotate(keys, ps[:, 7, :].rearrange("p (a b) -> p a b", a=2))
                v.tensor_tensor(keys, keys, rope[:], ALU.add).then_inc(rope_ready, 1)
                dve.wait_ge(rope_ready, l + 1)
                settle(dve)
                with st.loop(4, 6) as g:
                    attention_group(l, g)

                for p_i, (m0, groups, last) in enumerate(((OUT_M, 4, 0), (DOWN_M, DOWN_GROUPS, FF_TILES % 4))):
                    if p_i:
                        step(v.memset(hbuf[:, :, 0:2], 0.0))
                        split_x(l, l * 2 + 1, UP_M)
                        conv_tile(l, 0, 0)
                        with st.loop(FF_TILES - 1, 4) as j:
                            split_lo(l, UP_M + 1 + j, 0)
                            split_lo(l, UP_M + 1 + j, 1)
                            conv_tile(l, j, 1)
                            split_lo(l, UP_M + 1 + j, 2)
                            gated(l, j)
                            split_lo(l, UP_M + 1 + j, 3)
                            gated_lo(l, j)
                            conv_tile(l, j + 1, 0)
                        conv_tile(l, FF_TILES - 1, 1)
                        gated(l, FF_TILES - 1)
                        gated_lo(l, FF_TILES - 1)
                    full = groups - (1 if last else 0)

                    def short_group(h):
                        for s in range(last):
                            split_lo(l, m0 + groups * h + groups - 1, s, 2 if s == last - 1 else 1)

                    with st.loop(full, 0) as q:
                        for s in range(SLOTS):
                            split_lo(l, m0 + q, s)
                    short_group(0)
                    for s in range(SLOTS):
                        split_lo(l, m0 + groups, s)
                    evac_half(l, 0, l * 4 + 2 * p_i, chunks(l, m0 + groups - 1, 3), l * 2 + p_i, last)
                    with st.loop(full - 1, 0) as q:
                        for s in range(SLOTS):
                            split_lo(l, m0 + groups + 1 + q, s)
                    short_group(1)
                    evac_half(l, 1, l * 4 + 2 * p_i + 1, chunks(l, m0 + 2 * groups - 1, 3), l * 2 + p_i, last)
                    normalise(l * 2 + p_i)

        @block.gpsimd
        def _(pool):
            st = Steps(pool, pool_steps)
            g_ = nc.gpsimd

            def step(ins):
                st.mark(ins)
                st.wait()

            def affine_rows(stage, done, parts):
                for c in range(D // GBC):
                    g_.dma_start(gb[:], a["gb"][bass.ds(stage, 1), :, c * GBC:(c + 1) * GBC]
                                 .rearrange("s g d -> (s g) d").partition_broadcast(P)).then_inc(gb_loaded, 16)
                    pool.wait_ge(gb_loaded, (stage * (D // GBC) + c + 1) * 16)
                    y = xres[:, :, c * GBC:(c + 1) * GBC]
                    step(g_.tensor_tensor(y, y, gb[:, 0:1, :].broadcast_to([P, NT, GBC]), ALU.mult))
                    step(g_.tensor_tensor(y, y, gb[:, 1:2, :].broadcast_to([P, NT, GBC]), ALU.add))
                    if (c + 1) % parts == 0:
                        pool.sem_inc(done, 1)

            def reciprocal_deviation(norm):
                pool.wait_ge(stats_ready, norm * 2 + 2)
                settle(pool)
                step(g_.tensor_scalar(rstd[:, 0, :], mv[:, :, 1], LN_EPS, None, ALU.add))
                g_.tensor_tensor(rstd[:, 1, :], rstd[:, 0, :], neg_half[:], ALU.pow).then_inc(rstd_ready, 1)
                pool.wait_ge(rstd_ready, norm + 1)

            def phase_table(c, n, slot):
                tab = phase[:, slot]
                pool.wait_ge(phase_used, n + 1)
                settle(pool)
                g_.memset(tab[:, 0, :, 0:1], 1.0)
                g_.memset(tab[:, 1, :, 0:1], 0.0)
                for i in range(2):
                    ins = g_.tensor_copy(tab[:, i, :, 1:2], prm[:, 6 + i, bass.ds(c * 4, 4)].unsqueeze(2))
                step(ins)
                m = 1
                while m < T - 1:
                    k = min(m, T - 1 - m)
                    co, si = tab[:, 0, :, 1:k + 1], tab[:, 1, :, 1:k + 1]
                    cm = tab[:, 0, :, m:m + 1].broadcast_to([P, 4, k])
                    sm_ = tab[:, 1, :, m:m + 1].broadcast_to([P, 4, k])
                    t0, t1 = ptmp[:, 0, :, 0:k], ptmp[:, 1, :, 0:k]
                    g_.tensor_tensor(t0, co, cm, ALU.mult)
                    step(g_.tensor_tensor(t1, si, sm_, ALU.mult))
                    step(g_.tensor_tensor(tab[:, 0, :, m + 1:m + k + 1], t0, t1, ALU.subtract))
                    g_.tensor_tensor(t0, co, sm_, ALU.mult)
                    step(g_.tensor_tensor(t1, si, cm, ALU.mult))
                    step(g_.tensor_tensor(tab[:, 1, :, m + 1:m + k + 1], t0, t1, ALU.add))
                    m *= 2
                pool.sem_inc(phase_ready, 1)

            def output_matrix(c, n):
                pool.wait_ge(c_loaded, (n + 1) * 16)
                pool.wait_ge(y_used, n + 1)
                settle(pool)
                zr = prm[:, 3, bass.ds(c * 4, 4)].unsqueeze(2).broadcast_to([P, 4, 32])
                zi = prm[:, 4, bass.ds(c * 4, 4)].unsqueeze(2).broadcast_to([P, 4, 32])
                cr, ci = (c_raw[:, i, :].rearrange("p (j h) -> p j h", j=4) for i in range(2))
                t0, t1 = (c_tmp[:, i, :].rearrange("p (j h) -> p j h", j=4) for i in range(2))
                dst = [c_pad[:, i, :].rearrange("p (j w) -> p j w", w=160)[:, :, 0:32] for i in range(2)]
                g_.tensor_tensor(t0, cr, zr, ALU.mult)
                step(g_.tensor_tensor(t1, ci, zi, ALU.mult))
                step(g_.tensor_tensor(dst[0], t0, t1, ALU.subtract))
                settle(pool)
                g_.tensor_tensor(t0, cr, zi, ALU.mult)
                step(g_.tensor_tensor(t1, ci, zr, ALU.mult))
                step(g_.tensor_tensor(t0, t0, t1, ALU.add))
                settle(pool)
                step(g_.tensor_scalar(dst[1], t0, -1.0, 0.0, ALU.mult, ALU.add))
                pool.sem_inc(cpad_ready, 1)

            step(g_.memset(neg_half[:], -0.5))
            with st.loop(DEPTH, POOL_LAYER) as l:
                pool.wait_ge(zT_ready, l * 8 + 4)
                affine_rows(l * 2, xres_ready, D // GBC)
                settle(pool)
                g_.memset(b_pad[:].rearrange("p a j m -> p (a j m)"), 0.0)
                step(g_.memset(flat(c_pad[:]), 0.0))
                pool.wait_ge(prm_ready, l + 1)
                settle(pool)
                with st.loop(2, POOL_STATES) as cc:
                    for slot in range(2):
                        c = cc * 2 + slot
                        n = l * 4 + c
                        pool.wait_ge(bu_used, n + 1)
                        for j in range(4):
                            g_.dma_start(b_pad[32 * j:32 * j + 32, :, j, :],
                                         a["ssm_b"][l, c, 32 * j:32 * j + 32]).then_inc(b_loaded, 16)
                        g_.dma_start(c_raw[:], a["ssm_c"][l, c]).then_inc(c_loaded, 16)
                        phase_table(c, n, slot)
                        output_matrix(c, n)
                g_.dma_start(pool_w[:], a["pool_w"][l].rearrange("g c d -> c g d")).then_inc(poolw_loaded, 16)
                pool.wait_ge(mix_ready, l * 16 + 8)
                settle(pool)
                step(g_.memset(flat(qpad[:]), 0.0))
                pool.sem_inc(attn_zero, 1)
                step(g_.memset(vpad[:].rearrange("p b h d -> p (b h d)"), 0.0))
                pool.wait_ge(vtok_ready, l + 1)
                settle(pool)
                with pool.Fori(0, 4) as g:
                    pool.wait_ge(mix_ready, l * 16 + 8 + 2 * g)
                    settle(pool)
                    for half in range(2):
                        ins = g_.tensor_copy(vpad[:, :, half, 64 * half:64 * half + 64], vtok[:, :, bass.ds(g * 64, 64)])
                    ins.then_inc(vpad_ready, 1)
                reciprocal_deviation(l * 2)
                pool.wait_ge(zT_ready, l * 8 + 8)
                affine_rows(l * 2 + 1, xres_ready, D // GBC)
                reciprocal_deviation(l * 2 + 1)
            pool.wait_ge(z_ready, 2 * (2 * DEPTH + 1))
            affine_rows(2 * DEPTH, out_ready, D // GBC // 4)


def kernel(**inputs):
    import numpy as np
    import concourse.bacc as bacc
    from concourse.bass_utils import run_bass_kernel_spmd

    def arr(name):
        return np.asarray(inputs[name])

    def tiles(w, n):
        return w.reshape(DEPTH, -1, P, n, P).transpose(0, 3, 2, 1, 4)

    def cols(v):
        v = v.reshape(*v.shape[:-1], -1, P)
        return np.moveaxis(v, -1, 0)

    f4 = np.float32
    order = [(t + 16) % IN_TILES for t in range(IN_TILES)]
    w_in = np.ascontiguousarray(tiles(arr("w_in"), IN_TILES)[:, order])
    w_up = tiles(arr("ffn_w_up"), 2 * FF_TILES).reshape(DEPTH, 2, FF_TILES, P, KT, P).transpose(0, 2, 1, 3, 4, 5)

    def chunked(w):
        w = w.reshape(DEPTH, -1, 2, P, 2, CHUNK).transpose(0, 1, 2, 4, 3, 5)
        return np.ascontiguousarray(w.reshape(DEPTH, -1, 4, P, CHUNK))

    glu_w = arr("ssm_glu_w").reshape(DEPTH, 4, P, 2, 4, P).transpose(0, 4, 2, 1, 3, 5)

    b_blk = np.zeros((DEPTH, 4, 4, 2, 16, 2, 2, 64), f4)
    c_blk = np.zeros((DEPTH, 4, 2, 64, 2, 4, 2, 16), f4)
    for part, (bn, cn) in enumerate((("ssm_b_re", "ssm_c_re"), ("ssm_b_im", "ssm_c_im"))):
        b = arr(bn).reshape(DEPTH, 4, 4, 2, 64, 16)
        c = arr(cn).reshape(DEPTH, 4, 4, 2, 16, 64)
        for g in range(2):
            b_blk[:, :, :, g, :, part, g, :] = b[:, :, :, g].transpose(0, 1, 2, 4, 3)
            c_blk[:, :, g, :, part, :, g, :] = c[:, :, :, g].transpose(0, 1, 4, 2, 3)

    gb = np.zeros((2 * DEPTH + 1, 2, D), f4)
    gb[0, 0] = 1
    for l in range(DEPTH):
        for i, n in enumerate(("ln1", "ln2")):
            gb[2 * l + 1 + i, 0], gb[2 * l + 1 + i, 1] = arr(n + "_g")[l], arr(n + "_b")[l]

    vec = np.zeros((P, DEPTH, NV), f4)
    for l in range(DEPTH):
        parts = [cols(arr("ffn_conv_w")[l]).reshape(P, -1), cols(arr("ffn_conv_b")[l]),
                 cols(gb[2 * l]).reshape(P, -1), cols(gb[2 * l + 1]).reshape(P, -1),
                 cols(arr("pool_scale")[l]), cols(arr("ssm_d")[l].reshape(-1)),
                 cols(arr("ssm_lam_re")[l].reshape(-1)), cols(arr("ssm_lam_im")[l].reshape(-1)),
                 cols(np.repeat(arr("ssm_log_dt")[l], 64)),
                 np.broadcast_to(arr("attn_sinks")[l], (P, 16))]
        vec[:, l] = np.concatenate(parts, axis=1)

    const = np.zeros((P, NC), f4)
    const[:, C_ID:C_ID + P] = np.eye(P)
    row = np.arange(P)
    const[row ^ 32, C_PERM + row] = 1
    inv = np.power(f4(10000.0), -np.arange(32, dtype=f4) / f4(32)).astype(f4)
    ang = (np.arange(T, dtype=f4)[None, :] * inv[row % 32][:, None]).astype(f4)
    const[:, C_COS:C_COS + T] = np.cos(ang)
    const[:, C_SIN:C_SIN + T] = np.sin(ang) * np.where(row % 64 < 32, -1, 1)[:, None]
    key = np.arange(P)
    const[:, C_MASK:C_MASK + P] = np.where(key[None, :] > row[:, None], 0, -1e30)
    const[:, C_MASK + P:C_MASK + 2 * P] = np.where(key[None, :] <= row[:, None], 0, -1e30)
    const[:, C_RECIP:C_RECIP + PAD] = 1.0 / np.arange(1, PAD + 1)

    arrays = {
        "x": arr("x")[0], "const": const, "vec": vec.reshape(P, -1), "gb": gb,
        "w_in": chunked(w_in), "w_up": chunked(w_up),
        "glu_w": np.ascontiguousarray(glu_w.reshape(DEPTH, 4, P, CHUNK)),
        "w_out": arr("w_out"), "w_down": arr("ffn_w_down"), "pool_w": arr("pool_w"),
        "ssm_b": b_blk.reshape(DEPTH, 4, P, 2, P), "ssm_c": c_blk.reshape(DEPTH, 4, P, 2, P),
    }
    nc = bacc.Bacc("TRN2", target_bir_lowering=False, num_devices=1)
    feeds, aps = {}, {}
    for name, v in arrays.items():
        v = np.ascontiguousarray(v)
        feeds["in_" + name] = v
        aps[name] = nc.dram_tensor("in_" + name, v.shape, F32, kind="ExternalInput").ap()
    aps["out"] = nc.dram_tensor("out", (T, D), F32, kind="ExternalOutput").ap()
    trunk(nc, aps)
    r = run_bass_kernel_spmd(nc, [feeds], core_ids=[0])
    return r.results[0]["out"].reshape(1, T, D)
```

```python
from contextlib import ExitStack, contextmanager

import concourse.bass as bass
from concourse import mybir

F32 = mybir.dt.float32
F32R = mybir.dt.float32r
I32 = mybir.dt.int32
ALU = mybir.AluOpType
ACT = mybir.ActivationFunctionType
AX_X = mybir.AxisListType.X

P = 128
D = 2048
T = 256
DEPTH = 2
D_FF = 5504
KT = D // P
NT = T // P
IN_TILES = 20
SSM0, Q0, K0, V0, POOL0 = 0, 4, 12, 14, 16
FF_TILES = D_FF // P
SLOTS = 4
CHUNK = 1024
HALF = D // 2
BANK = 512
GBC = 256
ALPHA = (2 * DEPTH) ** 0.25
LN_EPS = 1e-5
SCALE = 64 ** -0.5
POOL_WINDOWS = (2, 4, 8, 16)
PAD = max(POOL_WINDOWS)

IN_M = 0
GLU_M = IN_M + IN_TILES // 2
OUT_M = GLU_M + 1
UP_M = OUT_M + 2 * KT // 4
DOWN_M = UP_M + FF_TILES
DOWN_GROUPS = (FF_TILES + 3) // 4
LAYER_M = DOWN_M + 2 * DOWN_GROUPS
LAYER_CHUNKS = 4 * LAYER_M
SHORT = 2
TILES = IN_TILES + 2 * FF_TILES

V_CONVW = 0
V_CONVB = V_CONVW + 3 * 2 * FF_TILES
V_G0 = V_CONVB + 2 * FF_TILES
V_G1 = V_G0 + 2 * KT
V_PSC = V_G1 + 2 * KT
V_D = V_PSC + 4
V_LR = V_D + 4
V_LI = V_LR + 16
V_LDT = V_LI + 16
V_SINK = V_LDT + 16
NV = V_SINK + 16

C_ID, C_PERM, C_COS, C_SIN, C_MASK, C_RECIP = 0, 128, 256, 512, 768, 1024
C_HALF_PI = C_RECIP + PAD
NC = C_HALF_PI + 1

ROUND = 12582912.0

DVE_LAYER = 258
POOL_LAYER = 89
POOL_STATES = 13


class Steps:

    def __init__(self, eng, sem):
        self.eng, self.sem, self.base, self.n = eng, sem, 0, 0

    def mark(self, ins):
        ins.then_inc(self.sem, 1)
        self.n += 1

    def wait(self):
        self.eng.wait_ge(self.sem, self.base + self.n)

    @contextmanager
    def loop(self, n_iter, steps):
        base, n = self.base, self.n
        with self.eng.Fori(0, n_iter) as i:
            self.base = base + i * steps
            yield i
            if self.n - n != steps:
                raise ValueError(f"a loop body of {self.n - n} steps was declared with {steps}")
        self.base, self.n = base, n + n_iter * steps


def trunk(nc, a):
    ctx = ExitStack()
    with ctx:
        def sem(name):
            return ctx.enter_context(nc.semaphore(name))

        def sb(name, shape, dt=F32, stack=ctx):
            return stack.enter_context(nc.sbuf_tensor(name, shape, dt))

        raw = sb("w_raw", [P, SLOTS, CHUNK])
        w_hi = sb("w_hi", [P, SLOTS, CHUNK], F32R)
        w_lo = sb("w_lo", [P, SLOTS, CHUNK], F32R)
        xT = sb("xT", [P, KT, 2, T], F32R)
        xres = sb("xres", [P, NT, D])
        gb = sb("gb", [P, 2, GBC])
        xtmp = sb("xtmp", [P, 4, T])
        vec = sb("vec", [P, DEPTH * NV])
        const = sb("const", [P, NC])
        stats = sb("stats", [P, NT, 4, 6])
        mv = sb("mv", [P, NT, 2])
        rstd = sb("rstd", [P, 2, NT])
        neg_half = sb("neg_half", [P, NT])
        state = sb("state", [P, 5, DEPTH, 16])
        corr = sb("corr", [P, 2, T])

        mixers = ExitStack()
        with mixers:
            hT = sb("hT", [P, IN_TILES, T], F32, mixers)
            ssm = ExitStack()
            with ssm:
                s1 = sb("s1", [P, 4, T], F32, ssm)
                s2 = sb("s2", [P, 4, T], F32, ssm)
                vr = sb("vr", [P, 4, T], F32, ssm)
                vi = sb("vi", [P, 4, T], F32, ssm)
                m1 = sb("m1", [P, 4, T], F32, ssm)
                m2 = sb("m2", [P, 4, T], F32, ssm)
                prm = sb("prm", [P, 12, DEPTH, 16], F32, ssm)
                b_pad = sb("b_pad", [P, 2, 4, P], F32, ssm)
                c_raw = sb("c_raw", [P, 2, P], F32, ssm)
                c_pad = sb("c_pad", [P, 2, 640], F32, ssm)
                c_tmp = sb("c_tmp", [P, 2, P], F32, ssm)
                ptmp = sb("ptmp", [P, 4, T], F32, ssm)
                tokens = sb("tokens", [P, 1, T], F32, ssm)
                phase = sb("phase", [P, 2, 16, T], F32, ssm)
            mixT = sb("mixT", [P, KT, 2, T], F32R, mixers)
            glu = ExitStack()
            with glu:
                yT = sb("yT", [P, 4, 2, T], F32R, glu)
                pool_pad = sb("pool_pad", [P, 2, PAD + T], F32, glu)
                pool_d = sb("pool_d", [P, T], F32, glu)
                pool_w = sb("pool_w", [P, 4, P], F32, glu)
                ab = sb("ab", [P, 2, T], F32, glu)
            attn = ExitStack()
            with attn:
                qpad = sb("qpad", [P, 4, T], F32, attn)
                kdup = sb("kdup", [P, 4, T], F32, attn)
                vtok = sb("vtok", [P, NT, 4 * 64], F32, attn)
                vpad = sb("vpad", [P, NT, 2, P], F32, attn)
                rope = sb("rope", [P, 2, T], F32, attn)
                sc0 = sb("sc0", [P, 4, P], F32, attn)
                sc1 = sb("sc1", [P, 4, 2 * P], F32, attn)
                pT = sb("pT", [P, 12, P], F32, attn)
                sm = sb("sm", [P, 8, 8], F32, attn)
        mlp = ExitStack()
        with mlp:
            actT = sb("actT", [P, FF_TILES, 2, T], F32R, mlp)
            hbuf = sb("hbuf", [P, 2, T + 2], F32, mlp)
            cv = sb("cv", [P, 2, T], F32, mlp)
            sig = sb("sig", [P, T], F32, mlp)
            act_f = sb("act_f", [P, T], F32, mlp)

        ps = ctx.enter_context(nc.psum_tensor("ps", [P, 8, BANK], F32))

        x_loaded, const_loaded, vec_loaded = sem("x_loaded"), sem("const_loaded"), sem("vec_loaded")
        raw_loaded = [sem(f"raw_loaded{s}") for s in range(SLOTS)]
        hi_done, lo_done, chunk_used = sem("hi_done"), sem("lo_done"), sem("chunk_used")
        corr_ready, tile_evac = sem("corr_ready"), sem("tile_evac")
        z_ready, zT_ready, xtmp_ready, xT_ready = (sem("z_ready"), sem("zT_ready"), sem("xtmp_ready"),
                                                  sem("xT_ready"))
        gb_loaded, xres_ready = sem("gb_loaded"), sem("xres_ready")
        acc_evac, stats_ready, rstd_ready = sem("acc_evac"), sem("stats_ready"), sem("rstd_ready")
        prm_dve, prm_act, prm_ready = sem("prm_dve"), sem("prm_act"), sem("prm_ready")
        b_loaded, c_loaded = sem("b_loaded"), sem("c_loaded")
        turns_ready, phase_ready, cpad_ready = sem("turns_ready"), sem("phase_ready"), sem("cpad_ready")
        tokens_loaded, abs_ready = sem("tokens_loaded"), sem("abs_ready")
        bu_ready, bu_used, s_ready = sem("bu_ready"), sem("bu_used"), sem("s_ready")
        y_ready, y_used = sem("y_ready"), sem("y_used")
        gelu_dve, gelu_act, y_split = sem("gelu_dve"), sem("gelu_act"), sem("y_split")
        glu_corr, glu_sum, glu_sig, glu_out = sem("glu_corr"), sem("glu_sum"), sem("glu_sig"), sem("glu_out")
        mix_hi, mix_ready = sem("mix_hi"), sem("mix_ready")
        poolw_loaded, pool_in, pool_out = sem("poolw_loaded"), sem("pool_in"), sem("pool_out")
        swap_ready, rope_ready, kdup_ready = sem("swap_ready"), sem("rope_ready"), sem("kdup_ready")
        vT_ready, vtok_ready, vpad_ready = sem("vT_ready"), sem("vtok_ready"), sem("vpad_ready")
        q_ready = sem("q_ready")
        score_ready, max_ready, exp_ready, prob_ready = (sem("score_ready"), sem("max_ready"), sem("exp_ready"),
                                                         sem("prob_ready"))
        pT_ready, pT_copied, o_ready, attn_zero = sem("pT_ready"), sem("pT_copied"), sem("o_ready"), sem("attn_zero")
        conv_first, conv_done, sig_ready = sem("conv_first"), sem("conv_done"), sem("sig_ready")
        act_ready, act_hi, act_lo = sem("act_ready"), sem("act_hi"), sem("act_lo")
        dve_steps, pool_steps = sem("dve_steps"), sem("pool_steps")
        apart = sem("apart")
        out_ready, out_written = sem("out_ready"), sem("out_written")

        def settle(eng):
            eng.sem_inc(apart, 1)

        def chunks(l, m, s):
            return l * LAYER_CHUNKS + m * 4 + s + 1

        def vcol(l, col):
            return vec[:, bass.ds(l * NV + col, 1)]

        def flat(ap):
            return ap.rearrange("p a b -> p (a b)")

        block = ctx.enter_context(nc.Block())

        @block.sync
        def _(sp):
            sp.dma_start(xres[:], a["x"].rearrange("(t p) d -> p t d", p=P)).then_inc(x_loaded, 16)
            sp.dma_start(const[:], a["const"]).then_inc(const_loaded, 16)
            sp.dma_start(vec[:], a["vec"]).then_inc(vec_loaded, 16)

            def load(l, m, s, src):
                sp.wait_ge(lo_done, chunks(l, m, s))
                settle(sp)
                sp.dma_start(raw[:, s, :], src).then_inc(raw_loaded[s], 16)

            with sp.Fori(0, DEPTH) as l:
                with sp.Fori(0, IN_TILES // 2) as i:
                    for s in range(SLOTS):
                        load(l, IN_M + i, s, a["w_in"][l, i, s])
                for s in range(SLOTS):
                    load(l, GLU_M, s, a["glu_w"][l, s])
                with sp.Fori(0, 2) as h:
                    for k in range(KT):
                        e = (k + KT // 2) % KT
                        load(l, OUT_M + 4 * h + k // 4, k % 4,
                             a["w_out"][l, e * P:(e + 1) * P, bass.ds(h * HALF, HALF)])
                with sp.Fori(0, FF_TILES) as j:
                    for s in range(SLOTS):
                        load(l, UP_M + j, s, a["w_up"][l, j, s])
                with sp.Fori(0, 2) as h:
                    for k in range(FF_TILES):
                        load(l, DOWN_M + DOWN_GROUPS * h + k // 4, k % 4,
                             a["w_down"][l, k * P:(k + 1) * P, bass.ds(h * HALF, HALF)])
            for c in range(4):
                sp.wait_ge(out_ready, c + 1)
                sp.dma_start(a["out"].rearrange("(t p) d -> p t d", p=P)[:, :, c * BANK:(c + 1) * BANK],
                             xres[:, :, c * BANK:(c + 1) * BANK]).then_inc(out_written, 16)
            sp.wait_ge(out_written, 64)

        @block.tensor
        def _(pe):
            ident = const[:, C_ID:C_ID + P]
            perm = const[:, C_PERM:C_PERM + P]

            def parts_ready(l, m, s):
                pe.wait_ge(lo_done, SLOTS + chunks(l, m, s))

            def transpose_z(stage):
                for r in range(4):
                    if r >= 2:
                        pe.wait_ge(xtmp_ready, stage * 4 + r - 1)
                    for t in range(NT):
                        pe.wait_ge(z_ready, stage * 2 + t + 1)
                        for d in range(4):
                            mm = nc.tensor.transpose(
                                ps[:, 4 + 2 * (r % 2) + d // 2, bass.ds((d % 2) * T + t * P, P)],
                                xres[:, t, (4 * r + d) * P:(4 * r + d + 1) * P], ident)
                    mm.then_inc(zT_ready, 1)

            def project_tile(l, m, which, tile, stage):
                pe.wait_ge(tile_evac, l * TILES + tile + 1)
                for c in range(2):
                    s = 2 * which + c
                    parts_ready(l, m, s)
                    for k in range(8):
                        kk = 8 * c + k
                        if kk % 4 == 0:
                            pe.wait_ge(xT_ready, 1 + stage * 4 + kk // 4 + 1)
                        nc.tensor.matmul(ps[:, which, :], w_hi[:, s, k * P:(k + 1) * P], flat(xT[:, kk]),
                                         start=(kk == 0), stop=False)
                        mm = nc.tensor.matmul(ps[:, which, 0:T], w_lo[:, s, k * P:(k + 1) * P], xT[:, kk, 0, :],
                                              start=False, stop=(kk == KT - 1))
                    mm.then_inc(chunk_used, 1)

            def project_tokens(l, m0, act, n_k, half_no, before_k):
                for k in range(n_k):
                    before_k(k)
                    m, s = m0 + k // 4, k % 4
                    parts_ready(l, m, s)
                    for t in range(NT):
                        hi = act(k)[:, 0, t * P:(t + 1) * P]
                        lo = act(k)[:, 1, t * P:(t + 1) * P]
                        for c in range(2):
                            if k == 0:
                                pe.wait_ge(acc_evac, half_no * 4 + 2 * t + c + 1)
                            cols = slice(c * BANK, (c + 1) * BANK)
                            acc = ps[:, 2 * t + c, :]
                            nc.tensor.matmul(acc, hi, w_hi[:, s, cols], start=(k == 0), stop=False)
                            nc.tensor.matmul(acc, hi, w_lo[:, s, cols], start=False, stop=False)
                            mm = nc.tensor.matmul(acc, lo, w_hi[:, s, cols], start=False, stop=(k == n_k - 1))
                    mm.then_inc(chunk_used, 2 if k == n_k - 1 and n_k % 4 else 1)

            def input_of_states(l, c):
                pe.wait_ge(b_loaded, (l * 4 + c + 1) * 64)
                pe.wait_ge(bu_used, l * 4 + c + 1)
                for ri in range(2):
                    for j in range(4):
                        mm = nc.tensor.matmul(ps[:, 2 + 2 * ri + j // 2, bass.ds((j % 2) * T, T)], b_pad[:, ri, j, :],
                                              hT[:, bass.ds(SSM0 + c, 1), :].rearrange("p a b -> p (a b)"),
                                              start=True, stop=True)
                mm.then_inc(bu_ready, 1)

            def output_of_states(l, c):
                pe.wait_ge(s_ready, l * 4 + c + 1)
                pe.wait_ge(cpad_ready, l * 4 + c + 1)
                for j in range(4):
                    for ri, src in enumerate((s1, s2)):
                        mm = nc.tensor.matmul(flat(ps[:, 6:8, :])[:, bass.ds(c * T, T)], c_pad[:, ri, j * P:(j + 1) * P], src[:, j, :],
                                              start=(j == 0 and ri == 0), stop=(j == 3 and ri == 1))
                mm.then_inc(y_ready, 1)

            def attention_group(l, g):
                n = l * 4 + g
                nc.tensor.matmul(ps[:, 7, :], perm,
                                 hT[:, bass.ds(Q0 + 2 * g, 2), :].rearrange("p a b -> p (a b)"),
                                 start=True, stop=True).then_inc(swap_ready, 1)
                pe.wait_ge(q_ready, n + 1)
                for h in range(4):
                    nc.tensor.matmul(ps[:, 2, h * P:(h + 1) * P], qpad[:, h, 0:P],
                                     kdup[:, bass.ds(g, 1), 0:P].rearrange("p a b -> p (a b)"),
                                     start=True, stop=True)
                for h in range(4):
                    mm = nc.tensor.matmul(ps[:, 3 + h // 2, bass.ds((h % 2) * T, T)], qpad[:, h, P:T],
                                          kdup[:, bass.ds(g, 1), :].rearrange("p a b -> p (a b)"),
                                          start=True, stop=True)
                mm.then_inc(score_ready, 1)
                pe.wait_ge(prob_ready, n + 1)
                for h in range(4):
                    for b, src in enumerate((sc0[:, h, :], sc1[:, h, 0:P], sc1[:, h, P:2 * P])):
                        i = 3 * h + b
                        mm = nc.tensor.transpose(ps[:, 5 + i // 4, bass.ds((i % 4) * P, P)], src, ident)
                mm.then_inc(pT_ready, 1)
                pe.wait_ge(pT_copied, n + 1)
                pe.wait_ge(vpad_ready, n + 1)
                for hp in range(2):
                    for q in range(2):
                        out = ps[:, 2, bass.ds(hp * T + q * P, P)]
                        pairs = [(vpad[:, 0, par, :], pT[:, 3 * (2 * hp + par) + q, :]) for par in range(2)]
                        if q:
                            pairs += [(vpad[:, 1, par, :], pT[:, 3 * (2 * hp + par) + 2, :]) for par in range(2)]
                        for i, (v, p) in enumerate(pairs):
                            mm = nc.tensor.matmul(out, v, p, start=(i == 0), stop=(i == len(pairs) - 1))
                mm.then_inc(o_ready, 1)

            nc.tensor.sem_inc(chunk_used, SLOTS)
            pe.wait_ge(const_loaded, 16)
            with pe.Fori(0, DEPTH) as l:
                transpose_z(l * 2)

                def project_pair(i):
                    for which in range(2):
                        project_tile(l, IN_M + i, which, i * 2 + which, l * 2)

                project_pair(0)
                pe.wait_ge(tile_evac, l * TILES + 2 + 1)
                input_of_states(l, 0)
                project_pair(1)
                with pe.Fori(0, 3) as c:
                    project_pair(2 * c + 2)
                    input_of_states(l, c + 1)
                    project_pair(2 * c + 3)
                    output_of_states(l, c)
                project_pair(8)
                project_pair(9)
                output_of_states(l, 3)

                pe.wait_ge(y_split, l + 1)
                for s in range(4):
                    parts_ready(l, GLU_M, s)
                    pe.wait_ge(glu_sum, l * 4 + s + 1)
                    for k in range(4):
                        for ab_i in range(2):
                            wcol = slice((2 * k + ab_i) * P, (2 * k + ab_i + 1) * P)
                            nc.tensor.matmul(ps[:, 2 + ab_i, :], w_hi[:, s, wcol], flat(yT[:, k]),
                                             start=(k == 0), stop=False)
                            mm = nc.tensor.matmul(ps[:, 2 + ab_i, 0:T], w_lo[:, s, wcol], yT[:, k, 0, :],
                                                  start=False, stop=(k == 3))
                    mm.then_inc(chunk_used, 1)

                pe.wait_ge(poolw_loaded, (l + 1) * 16)
                for gi in range(4):
                    pe.wait_ge(pool_in, l * 4 + gi + 1)
                    nc.tensor.matmul(ps[:, 6, 0:T], pool_w[:, gi, :], pool_d[:], start=True,
                                     stop=True).then_inc(pool_out, 1)

                nc.tensor.matmul(ps[:, 7, :], perm, flat(hT[:, K0:K0 + 2, :]), start=True,
                                 stop=True).then_inc(swap_ready, 1)
                for b in range(NT):
                    for i in range(2):
                        mm = nc.tensor.transpose(ps[:, 5, bass.ds(b * T + i * P, P)], hT[:, V0 + i, b * P:(b + 1) * P],
                                                 ident)
                mm.then_inc(vT_ready, 1)
                pe.wait_ge(kdup_ready, l + 1)
                settle(pe)
                with pe.Fori(0, 4) as g:
                    attention_group(l, g)

                with pe.Fori(0, 2) as h:
                    project_tokens(l, OUT_M + 4 * h, lambda k: mixT[:, (k + KT // 2) % KT], KT, l * 4 + h,
                                   lambda k: pe.wait_ge(mix_ready, l * 16 + k + 1))
                transpose_z(l * 2 + 1)
                with pe.Fori(0, FF_TILES) as j:
                    for which in range(2):
                        project_tile(l, UP_M + j, which, IN_TILES + j * 2 + which, l * 2 + 1)
                with pe.Fori(0, 2) as h:
                    project_tokens(l, DOWN_M + DOWN_GROUPS * h, lambda k: actT[:, k], FF_TILES, l * 4 + 2 + h,
                                   lambda k: pe.wait_ge(act_lo, l * FF_TILES + k + 1))

        @block.scalar
        def _(act):
            def round_hi(l, m, s):
                act.wait_ge(raw_loaded[s], loads(l, m, s))
                act.wait_ge(chunk_used, chunks(l, m, s))
                nc.scalar.activation(w_hi[:, s, :], raw[:, s, :], ACT.Copy).then_inc(hi_done, 1)

            def loads(l, m, s):
                return (l * (LAYER_M - (SHORT if s == 3 else 0)) + m + 1) * 16

            def round_hi_down(l, h, q, s, count=1):
                act.wait_ge(raw_loaded[s], loads(l, DOWN_M + (DOWN_GROUPS - (1 if s == 3 else 0)) * h + q, s))
                act.wait_ge(chunk_used, chunks(l, DOWN_M + DOWN_GROUPS * h + q, s))
                nc.scalar.activation(w_hi[:, s, :], raw[:, s, :], ACT.Copy).then_inc(hi_done, count)

            def correction(l, tile, which, m, s):
                act.wait_ge(chunk_used, SLOTS + chunks(l, m, s))
                act.wait_ge(tile_evac, l * TILES + tile + 1)
                nc.scalar.activation(corr[:, which, :], ps[:, which, T:2 * T], ACT.Copy).then_inc(corr_ready, 1)

            def affine(l, stage, col, m):
                for r in range(4):
                    act.wait_ge(zT_ready, stage * 4 + r + 1)
                    act.wait_ge(xT_ready, stage * 4 + r + 1)
                    for d in range(4):
                        ins = nc.scalar.activation(
                            xtmp[:, d, :], ps[:, 4 + 2 * (r % 2) + d // 2, bass.ds((d % 2) * T, T)],
                            ACT.Identity, scale=vcol(l, col + 4 * r + d), bias=vcol(l, col + KT + 4 * r + d))
                    ins.then_inc(xtmp_ready, 1)
                    round_hi(l, m, r)

            def conv_first_tap(l, j, which, tile):
                f = j + FF_TILES * which
                act.wait_ge(tile_evac, 2 + l * TILES + tile + 1)
                nc.scalar.activation(cv[:, which, :], hbuf[:, which, 0:T], ACT.Identity,
                                     scale=vcol(l, V_CONVW + f), bias=vcol(l, V_CONVB + f)).then_inc(conv_first, 1)

            def gate_part(l, j, with_chunks, m):
                tile = IN_TILES + 2 * j + 1
                correction(l, tile, 1, UP_M + j, 3)
                conv_first_tap(l, j, 1, tile)
                if with_chunks:
                    round_hi(l, m, 2)
                act.wait_ge(conv_done, l * FF_TILES + j + 1)
                nc.scalar.activation(sig[:], cv[:, 1, :], ACT.Tanh, scale=0.5).then_inc(sig_ready, 1)
                if with_chunks:
                    round_hi(l, m, 3)
                act.wait_ge(act_ready, l * FF_TILES + j + 1)
                nc.scalar.activation(actT[:, bass.ds(j, 1), 0, :].rearrange("p a b -> p (a b)"), act_f[:],
                                     ACT.Copy).then_inc(act_hi, 1)

            def value_part(l, j):
                tile = IN_TILES + 2 * j
                correction(l, tile, 0, UP_M + j, 1)
                conv_first_tap(l, j, 0, tile)

            def phase_table(l, c):
                n = l * 4 + c
                act.wait_ge(turns_ready, n + 1)
                settle(act)
                y, co = phase[:, 1, bass.ds(c * 4, 4), :], phase[:, 0, bass.ds(c * 4, 4), :]
                nc.scalar.activation(co, y, ACT.Abs).then_inc(abs_ready, 1)
                act.wait_ge(abs_ready, n + 1)
                settle(act)
                nc.scalar.activation(y, y, ACT.Sin, scale=6.283185)
                nc.scalar.activation(co, co, ACT.Sin, scale=-6.283185,
                                     bias=const[:, C_HALF_PI:C_HALF_PI + 1]).then_inc(phase_ready, 1)

            act.wait_ge(vec_loaded, 16)
            act.wait_ge(const_loaded, 16)
            act.wait_ge(prm_dve, 1)
            nc.scalar.activation(prm[:, 4:7], prm[:, 4:7], ACT.Sin).then_inc(prm_act, 1)
            with act.Fori(0, DEPTH) as l:
                affine(l, l * 2, V_G0, IN_M)
                correction(l, 0, 0, IN_M, 1)

                def pair_part(i):
                    round_hi(l, IN_M + 1 + i, 0)
                    round_hi(l, IN_M + 1 + i, 1)
                    correction(l, 2 * i + 1, 1, IN_M + i, 3)
                    round_hi(l, IN_M + 1 + i, 2)
                    round_hi(l, IN_M + 1 + i, 3)
                    correction(l, 2 * i + 2, 0, IN_M + 1 + i, 1)

                pair_part(0)
                phase_table(l, 0)
                with act.Fori(0, 3) as c:
                    pair_part(2 * c + 1)
                    pair_part(2 * c + 2)
                    phase_table(l, c + 1)
                pair_part(7)
                pair_part(8)
                correction(l, IN_TILES - 1, 1, IN_M + IN_TILES // 2 - 1, 3)
                for s in range(SLOTS):
                    round_hi(l, GLU_M, s)

                act.wait_ge(y_used, l + 1)
                nc.scalar.activation(flat(s1[:]), flat(hT[:, SSM0:SSM0 + 4, :]), ACT.Square).then_inc(gelu_act, 1)
                act.wait_ge(gelu_dve, 2 * l + 1)
                nc.scalar.activation(flat(s2[:]), flat(s2[:]), ACT.Tanh,
                                     scale=0.7978845608028654).then_inc(gelu_act, 1)
                act.wait_ge(gelu_dve, 2 * l + 2)
                nc.scalar.activation(yT[:, :, 0, :], vr[:], ACT.Copy, scale=0.5).then_inc(gelu_act, 1)
                for s in range(4):
                    act.wait_ge(chunk_used, SLOTS + chunks(l, GLU_M, s))
                    if s:
                        act.wait_ge(mix_ready, l * 16 + s)
                    nc.scalar.activation(ab[:], ps[:, 2:4, T:2 * T], ACT.Copy).then_inc(glu_corr, 1)
                    act.wait_ge(glu_sum, 1 + l * 4 + s + 1)
                    nc.scalar.activation(ab[:, 1, :], ab[:, 1, :], ACT.Tanh, scale=0.5).then_inc(glu_sig, 1)
                    act.wait_ge(glu_out, l * 4 + s + 1)
                    nc.scalar.activation(mixT[:, 12 + s, 0, :], ab[:, 0, :], ACT.Copy).then_inc(mix_hi, 1)
                for gi in range(4):
                    act.wait_ge(pool_out, l * 4 + gi + 1)
                    nc.scalar.activation(mixT[:, 8 + gi, 0, :], ps[:, 6, 0:T], ACT.Copy,
                                         scale=vcol(l, V_PSC + gi)).then_inc(mix_hi, 1)
                act.wait_ge(vT_ready, l + 1)
                nc.scalar.activation(flat(vtok[:]), ps[:, 5, :], ACT.Copy).then_inc(vtok_ready, 1)
                act.wait_ge(rope_ready, l + 1)
                for kv in range(2):
                    for half in range(2):
                        ins = nc.scalar.activation(kdup[64 * half:64 * half + 64, kv::2, :],
                                                   hT[64 * kv:64 * kv + 64, K0:K0 + 2, :], ACT.Copy)
                ins.then_inc(kdup_ready, 1)
                with act.Fori(0, 4) as g:
                    n = l * 4 + g
                    act.wait_ge(max_ready, n + 1)
                    for b, scores in enumerate((sc0, sc1)):
                        for h in range(4):
                            nc.scalar.activation(scores[:, h, :], scores[:, h, :], ACT.Exp,
                                                 bias=sm[:, 2 + b, h:h + 1], accum_out=sm[:, 4 + b, h:h + 1])
                    nc.scalar.activation(sm[:, 6, :], sm[:, 6, :], ACT.Exp).then_inc(exp_ready, 1)
                    act.wait_ge(pT_ready, n + 1)
                    nc.scalar.activation(flat(pT[:]), ps[:, 5:8, :].rearrange("p a b -> p (a b)"),
                                         ACT.Copy).then_inc(pT_copied, 1)
                    act.wait_ge(o_ready, n + 1)
                    nc.scalar.activation(mixT[:, bass.ds(2 * g, 2), 0, :],
                                         ps[:, 2, :].rearrange("p (a b) -> p a b", a=2), ACT.Copy).then_inc(mix_hi, 1)

                with act.Fori(0, 8) as q:
                    for s in range(SLOTS):
                        round_hi(l, OUT_M + q, s)
                affine(l, l * 2 + 1, V_G1, UP_M)
                value_part(l, 0)
                with act.Fori(0, FF_TILES - 1) as j:
                    round_hi(l, UP_M + 1 + j, 0)
                    round_hi(l, UP_M + 1 + j, 1)
                    gate_part(l, j, True, UP_M + 1 + j)
                    value_part(l, j + 1)
                gate_part(l, FF_TILES - 1, False, 0)
                with act.Fori(0, 2) as h:
                    with act.Fori(0, DOWN_GROUPS - 1) as q:
                        for s in range(SLOTS):
                            round_hi_down(l, h, q, s)
                    for s in range(FF_TILES % 4):
                        round_hi_down(l, h, DOWN_GROUPS - 1, s, 2 if s == FF_TILES % 4 - 1 else 1)

        @block.vector
        def _(dve):
            st = Steps(dve, dve_steps)
            v = nc.vector

            def split_lo(l, m, s, last=1):
                dve.wait_ge(hi_done, chunks(l, m, s))
                v.tensor_tensor(w_lo[:, s, :], raw[:, s, :], w_hi[:, s, :].bitcast(F32),
                                ALU.subtract).then_inc(lo_done, last)

            def split_x(l, stage, m):
                for r in range(4):
                    dve.wait_ge(xtmp_ready, stage * 4 + r + 1)
                    step(v.tensor_copy(xT[:, 4 * r:4 * r + 4, 0, :], xtmp[:]))
                    v.tensor_tensor(xT[:, 4 * r:4 * r + 4, 1, :], xtmp[:], xT[:, 4 * r:4 * r + 4, 0, :].bitcast(F32),
                                    ALU.subtract).then_inc(xT_ready, 1)
                    split_lo(l, m, r)

            def evac_in(l, tile, which):
                dve.wait_ge(corr_ready, l * TILES + tile + 1)
                v.tensor_tensor(hT[:, bass.ds(tile, 1), :].rearrange("p a b -> p (a b)"), ps[:, which, 0:T],
                                corr[:, which, :], ALU.add).then_inc(tile_evac, 1)

            def conv_tile(l, j, which):
                tile = IN_TILES + 2 * j + which
                f = j + FF_TILES * which
                dve.wait_ge(corr_ready, l * TILES + tile + 1)
                v.tensor_tensor(hbuf[:, which, 2:T + 2], ps[:, which, 0:T], corr[:, which, :],
                                ALU.add).then_inc(tile_evac, 1)
                dve.wait_ge(tile_evac, 2 + l * TILES + tile + 1)
                dve.wait_ge(conv_first, l * 2 * FF_TILES + 2 * j + which + 1)
                st.mark(v.scalar_tensor_tensor(cv[:, which, :], hbuf[:, which, 1:T + 1],
                                               vcol(l, V_CONVW + 2 * FF_TILES + f), cv[:, which, :],
                                               ALU.mult, ALU.add))
                st.wait()
                ins = v.scalar_tensor_tensor(cv[:, which, :], hbuf[:, which, 2:T + 2],
                                             vcol(l, V_CONVW + 4 * FF_TILES + f), cv[:, which, :],
                                             ALU.mult, ALU.add)
                if which:
                    ins.then_inc(conv_done, 1)
                else:
                    st.mark(ins)

            def gated(l, j):
                dve.wait_ge(sig_ready, l * FF_TILES + j + 1)
                st.mark(v.scalar_tensor_tensor(cv[:, 1, :], sig[:], 1.0, cv[:, 1, :], ALU.add, ALU.mult))
                st.wait()
                v.scalar_tensor_tensor(act_f[:], cv[:, 1, :], 0.5, cv[:, 0, :], ALU.mult,
                                       ALU.mult).then_inc(act_ready, 1)

            def gated_lo(l, j):
                dve.wait_ge(act_hi, l * FF_TILES + j + 1)
                ap = actT[:, bass.ds(j, 1), :, :].rearrange("p a h b -> p (a h) b")
                v.tensor_tensor(ap[:, 1, :], act_f[:], ap[:, 0, :].bitcast(F32), ALU.subtract).then_inc(act_lo, 1)

            def evac_half(l, h, half_no, m_last, stage, s_last):
                dve.wait_ge(chunk_used, SLOTS + m_last)
                dve.wait_ge(xres_ready, stage + 1)
                for t in range(NT):
                    for c in range(2):
                        y = xres[:, t, bass.ds(h * HALF + c * BANK, BANK)]
                        v.scalar_tensor_tensor(y, y, ALPHA, ps[:, 2 * t + c, :], ALU.mult,
                                               ALU.add).then_inc(acc_evac, 1)
                        dve.wait_ge(acc_evac, 4 + half_no * 4 + 2 * t + c + 1)
                        st.mark(v.bn_stats(stats[:, t, bass.ds(2 * h + c, 1), :].rearrange("p a b -> p (a b)"), y))

            def normalise(stage):
                st.wait()
                settle(dve)
                for t in range(NT):
                    v.bn_aggr(mv[:, t, :], stats[:, t, :, :].rearrange("p a b -> p (a b)")).then_inc(stats_ready, 1)
                dve.wait_ge(stats_ready, stage * 2 + 2)
                dve.wait_ge(rstd_ready, stage + 1)
                for t in range(NT):
                    v.tensor_scalar(xres[:, t, :], xres[:, t, :], mv[:, t, 0:1], rstd[:, 1, t:t + 1],
                                    ALU.subtract, ALU.mult).then_inc(z_ready, 1)

            def step(ins):
                st.mark(ins)
                st.wait()

            def exp_parts(x, n, r, acc, two_n):
                step(v.tensor_scalar(n, x, 1.0 / 0.6931471805599453, 12582912.0, ALU.mult, ALU.add))
                step(v.tensor_scalar(n, n, 12582912.0, None, ALU.subtract))
                step(v.scalar_tensor_tensor(r, n, -0.693359375, x, ALU.mult, ALU.add))
                step(v.scalar_tensor_tensor(r, n, 2.12194440e-4, r, ALU.mult, ALU.add))
                step(v.tensor_scalar(acc, r, 1.0 / 40320, None, ALU.mult))
                for c in (1 / 5040, 1 / 720, 1 / 120, 1 / 24, 1 / 6, 0.5, 1.0):
                    step(v.scalar_tensor_tensor(acc, acc, c, r, ALU.add, ALU.mult))
                step(v.tensor_scalar(n, n, 127.0, 0.0, ALU.add, ALU.max))
                step(v.tensor_scalar(two_n.bitcast(I32), n, 255.0, float(2 ** 23), ALU.min, ALU.mult))

            def state_parameters():
                by_layer = vec[:].rearrange("p (l n) -> p l n", l=DEPTH)
                lr = by_layer[:, :, V_LR:V_LR + 16]
                li = by_layer[:, :, V_LI:V_LI + 16]
                ldt = by_layer[:, :, V_LDT:V_LDT + 16]
                mag, zr, zi, f_hi, f_lo = (state[:, i] for i in range(5))
                dt, em1, th, f = (prm[:, i] for i in range(4))
                cs, sn, sh = (prm[:, i] for i in range(4, 7))
                n, r, acc, two_n, t1 = (prm[:, i] for i in range(7, 12))
                t2 = f
                step(v.tensor_scalar(t1, ldt, -150.0, 150.0, ALU.max, ALU.min))
                exp_parts(t1, n, r, acc, two_n)
                step(v.tensor_tensor(acc, acc, two_n, ALU.mult))
                step(v.tensor_tensor(dt, acc, two_n, ALU.add))
                step(v.tensor_tensor(th, li, dt, ALU.mult))
                step(v.tensor_scalar(n, th, 0.15915494309189535, ROUND, ALU.mult, ALU.add))
                step(v.tensor_scalar(n, n, ROUND, None, ALU.subtract))
                step(v.scalar_tensor_tensor(th, n, -6.28125, th, ALU.mult, ALU.add))
                step(v.scalar_tensor_tensor(th, n, -1.934051513671875e-3, th, ALU.mult, ALU.add))
                step(v.scalar_tensor_tensor(th, n, -1.2556659146019e-6, th, ALU.mult, ALU.add))
                step(v.tensor_scalar(sn, th, 3.1415925, -3.1415925, ALU.min, ALU.max))
                step(v.tensor_scalar(sh, sn, 0.5, None, ALU.mult))
                step(v.tensor_scalar(cs, sn, -1.0, None, ALU.mult))
                step(v.tensor_tensor(cs, cs, sn, ALU.max))
                v.tensor_scalar(cs, cs, -1.0, 1.5707963267948966, ALU.mult, ALU.add).then_inc(prm_dve, 1)
                step(v.tensor_scalar(f, th, 0.15915494309189535, None, ALU.mult))
                step(v.tensor_scalar(f_hi, f, 192.0, None, ALU.add))
                step(v.tensor_scalar(f_hi, f_hi, 192.0, None, ALU.subtract))
                step(v.tensor_tensor(f_lo, f, f_hi, ALU.subtract))
                v.sem_inc(prm_ready, 1)
                step(v.tensor_tensor(t2, lr, dt, ALU.mult))
                step(v.tensor_scalar(t2, t2, -150.0, 150.0, ALU.max, ALU.min))
                exp_parts(t2, n, r, acc, two_n)
                step(v.tensor_tensor(acc, acc, two_n, ALU.mult))
                step(v.tensor_tensor(mag, acc, two_n, ALU.add))
                step(v.scalar_tensor_tensor(em1, two_n, -1.0, acc, ALU.add, ALU.add))
                dve.wait_ge(prm_act, 1)
                step(v.tensor_tensor(t1, sh, sh, ALU.mult))
                step(v.tensor_tensor(t2, em1, cs, ALU.mult))
                step(v.scalar_tensor_tensor(t1, t1, -2.0, t2, ALU.mult, ALU.add))
                step(v.tensor_tensor(t2, mag, sn, ALU.mult))
                step(v.tensor_tensor(n, lr, lr, ALU.mult))
                step(v.tensor_tensor(r, li, li, ALU.mult))
                step(v.tensor_tensor(n, n, r, ALU.add))
                step(v.reciprocal(n, n))
                step(v.tensor_tensor(zr, t1, lr, ALU.mult))
                step(v.tensor_tensor(r, t2, li, ALU.mult))
                step(v.tensor_tensor(zr, zr, r, ALU.add))
                step(v.tensor_tensor(zr, zr, n, ALU.mult))
                step(v.tensor_tensor(zi, t2, lr, ALU.mult))
                step(v.tensor_tensor(r, t1, li, ALU.mult))
                step(v.tensor_tensor(zi, zi, r, ALU.subtract))
                v.tensor_tensor(zi, zi, n, ALU.mult).then_inc(prm_ready, 1)

            def states_and_pairs(l, c):
                n = l * 4 + c
                m = IN_M + 2 * c + 2
                co, si = phase[:, 0, bass.ds(c * 4, 4), :], phase[:, 1, bass.ds(c * 4, 4), :]
                p, q = ps[:, 2:4, :].rearrange("p a (j t) -> p (a j) t", j=2), \
                    ps[:, 4:6, :].rearrange("p a (j t) -> p (a j) t", j=2)
                split_lo(l, m, 0)
                split_lo(l, m, 1)
                dve.wait_ge(phase_ready, n + 1)
                dve.wait_ge(bu_ready, n + 1)
                v.tensor_tensor(vr[:], co, p, ALU.mult)
                v.tensor_tensor(m1[:], si, q, ALU.mult)
                evac_in(l, 4 * c + 3, 1)
                split_lo(l, m, 2)
                v.tensor_tensor(vi[:], co, q, ALU.mult)
                v.tensor_tensor(m2[:], si, p, ALU.mult).then_inc(bu_used, 1)
                split_lo(l, m, 3)
                dve.wait_ge(bu_used, 1 + n + 1)
                v.tensor_tensor(vr[:], vr[:], m1[:], ALU.add)
                st.mark(v.tensor_tensor(vi[:], vi[:], m2[:], ALU.subtract))
                evac_in(l, 4 * c + 4, 0)
                split_lo(l, m + 1, 0)
                st.wait()
                settle(dve)
                for j in range(4):
                    for w in (vr, vi):
                        ins = v.tensor_tensor_scan(w[:, j, :],
                                                   flat(state[:, 0])[:, bass.ds(n * 4 + j, 1)].broadcast_to([P, T]),
                                                   w[:, j, :], 0.0, ALU.mult, ALU.add)
                st.mark(ins)
                split_lo(l, m + 1, 1)
                evac_in(l, 4 * c + 5, 1)
                split_lo(l, m + 1, 2)
                st.wait()
                dve.wait_ge(y_ready, n + 1)
                v.tensor_tensor(s1[:], co, vr[:], ALU.mult)
                v.tensor_tensor(m1[:], si, vi[:], ALU.mult)
                v.tensor_tensor(s2[:], si, vr[:], ALU.mult)
                st.mark(v.tensor_tensor(m2[:], co, vi[:], ALU.mult))
                split_lo(l, m + 1, 3)
                st.wait()
                v.tensor_tensor(s1[:], s1[:], m1[:], ALU.subtract)
                v.tensor_tensor(s2[:], s2[:], m2[:], ALU.add).then_inc(s_ready, 1)
                evac_in(l, 4 * c + 6, 0)
                dve.wait_ge(s_ready, n + 1)
                settle(dve)

            def pool_group(l, gi, w):
                u = hT[:, POOL0 + gi, :]
                step(v.tensor_copy(pool_pad[:, 0, PAD:], u))
                src, shift = 0, 1
                while shift < w:
                    step(v.tensor_tensor(pool_pad[:, 1 - src, PAD:], pool_pad[:, src, PAD:],
                                         pool_pad[:, src, PAD - shift:PAD + T - shift], ALU.add))
                    src, shift = 1 - src, 2 * shift
                if gi:
                    dve.wait_ge(pool_out, l * 4 + gi)
                sums = pool_pad[:, src, PAD:]
                step(v.tensor_tensor(pool_d[:, 0:w], sums[:, 0:w], const[:, C_RECIP:C_RECIP + w], ALU.mult))
                v.tensor_tensor(pool_d[:, 0:w], pool_d[:, 0:w], u[:, 0:w], ALU.subtract)
                v.scalar_tensor_tensor(pool_d[:, w:], sums[:, w:], 1.0 / w, u[:, w:], ALU.mult,
                                       ALU.subtract).then_inc(pool_in, 1)
                dve.wait_ge(pool_in, l * 4 + gi + 1)

            def rotate(x, swapped):
                cos = const[:, C_COS:C_COS + T].unsqueeze(1).broadcast_to([P, 2, T])
                sin = const[:, C_SIN:C_SIN + T].unsqueeze(1).broadcast_to([P, 2, T])
                v.tensor_tensor(rope[:], swapped, sin, ALU.mult)
                step(v.tensor_tensor(x, x, cos, ALU.mult))

            def attention_group(l, g):
                n = l * 4 + g
                swapped = ps[:, 7, :].rearrange("p (a b) -> p a b", a=2)
                dve.wait_ge(swap_ready, l * 5 + g + 2)
                rotate(hT[:, bass.ds(Q0 + 2 * g, 2), :], swapped)
                dve.wait_ge(attn_zero, l + 1)
                for half in range(2):
                    part = slice(64 * half, 64 * half + 64)
                    ins = v.tensor_tensor(qpad[part, half::2, :], hT[part, bass.ds(Q0 + 2 * g, 2), :], rope[part],
                                          ALU.add)
                ins.then_inc(q_ready, 1)
                dve.wait_ge(q_ready, n + 1)
                dve.wait_ge(score_ready, n + 1)
                causal = const[:, C_MASK + P:C_MASK + 2 * P].unsqueeze(1).broadcast_to([P, 4, P])
                window = const[:, C_MASK:C_MASK + 2 * P].unsqueeze(1).broadcast_to([P, 4, 2 * P])
                v.scalar_tensor_tensor(sc0[:], ps[:, 2, :].rearrange("p (h k) -> p h k", h=4), SCALE, causal,
                                       ALU.mult, ALU.add)
                step(v.scalar_tensor_tensor(sc1[:], ps[:, 3:5, :].rearrange("p a (h k) -> p (a h) k", h=2), SCALE,
                                            window, ALU.mult, ALU.add))
                v.tensor_reduce(sm[:, 0, 0:4], sc0[:], AX_X, ALU.max)
                step(v.tensor_reduce(sm[:, 1, 0:4], sc1[:], AX_X, ALU.max))
                sink = vec[:, bass.ds(l * NV + V_SINK + g * 4, 4)]
                v.tensor_tensor(sm[:, 0, 0:4], sm[:, 0, 0:4], sink, ALU.max)
                step(v.tensor_tensor(sm[:, 1, 0:4], sm[:, 1, 0:4], sink, ALU.max))
                v.tensor_scalar(sm[:, 2:4, 0:4], sm[:, 0:2, 0:4], -1.0, None, ALU.mult)
                v.tensor_tensor(sm[:, 6, 0:4], sink, sm[:, 0, 0:4], ALU.subtract)
                v.tensor_tensor(sm[:, 6, 4:8], sink, sm[:, 1, 0:4], ALU.subtract).then_inc(max_ready, 1)
                dve.wait_ge(max_ready, n + 1)
                dve.wait_ge(exp_ready, n + 1)
                v.tensor_tensor(sm[:, 7, 0:4], sm[:, 4, 0:4], sm[:, 6, 0:4], ALU.add)
                step(v.tensor_tensor(sm[:, 7, 4:8], sm[:, 5, 0:4], sm[:, 6, 4:8], ALU.add))
                step(v.reciprocal(sm[:, 7, :], sm[:, 7, :]))
                v.tensor_tensor(sc0[:], sc0[:], sm[:, 7, 0:4].unsqueeze(2).broadcast_to([P, 4, P]), ALU.mult)
                v.tensor_tensor(sc1[:], sc1[:], sm[:, 7, 4:8].unsqueeze(2).broadcast_to([P, 4, 2 * P]),
                                ALU.mult).then_inc(prob_ready, 1)
                dve.wait_ge(prob_ready, n + 1)
                dve.wait_ge(mix_hi, l * 12 + 8 + g + 1)
                for i in range(2):
                    dst = mixT[:, bass.ds(2 * g + i, 1), :, :].rearrange("p a h b -> p (a h) b")
                    v.tensor_tensor(dst[:, 1, :], ps[:, 2, i * T:(i + 1) * T], dst[:, 0, :].bitcast(F32),
                                    ALU.subtract).then_inc(mix_ready, 1)
                dve.wait_ge(mix_ready, l * 16 + 8 + g * 2 + 2)

            v.sem_inc(lo_done, SLOTS)
            v.sem_inc(tile_evac, 2)
            v.sem_inc(acc_evac, 4)
            v.sem_inc(bu_used, 1)
            v.sem_inc(y_ready, 1)
            v.sem_inc(glu_sum, 1)
            v.sem_inc(xT_ready, 1)
            dve.wait_ge(x_loaded, 16)
            v.sem_inc(z_ready, 2)
            dve.wait_ge(vec_loaded, 16)
            dve.wait_ge(const_loaded, 16)
            state_parameters()
            dve.wait_ge(prm_ready, 2)
            settle(dve)
            with st.loop(DEPTH, DVE_LAYER) as l:
                split_x(l, l * 2, IN_M)
                evac_in(l, 0, 0)
                split_lo(l, IN_M + 1, 0)
                split_lo(l, IN_M + 1, 1)
                evac_in(l, 1, 1)
                split_lo(l, IN_M + 1, 2)
                split_lo(l, IN_M + 1, 3)
                evac_in(l, 2, 0)
                with st.loop(4, 3) as c:
                    states_and_pairs(l, c)
                evac_in(l, IN_TILES - 1, 1)
                dve.wait_ge(tile_evac, 2 + l * TILES + IN_TILES)
                for s in range(SLOTS):
                    split_lo(l, GLU_M, s)
                dve.wait_ge(y_ready, 1 + l * 4 + 4)
                for c in range(4):
                    u = hT[:, SSM0 + c, :]
                    ins = v.scalar_tensor_tensor(u, u, vcol(l, V_D + c), ps[:, 6 + c // 2, bass.ds((c % 2) * T, T)],
                                                 ALU.mult, ALU.add)
                ins.then_inc(y_used, 1)
                dve.wait_ge(y_used, l + 1)
                y = flat(hT[:, SSM0:SSM0 + 4, :])
                dve.wait_ge(gelu_act, 3 * l + 1)
                step(v.tensor_scalar(flat(s1[:]), flat(s1[:]), 0.044715, 1.0, ALU.mult, ALU.add))
                v.tensor_tensor(flat(s2[:]), flat(s1[:]), y, ALU.mult).then_inc(gelu_dve, 1)
                dve.wait_ge(gelu_act, 3 * l + 2)
                v.scalar_tensor_tensor(flat(vr[:]), flat(s2[:]), 1.0, y, ALU.add, ALU.mult).then_inc(gelu_dve, 1)
                dve.wait_ge(gelu_dve, 2 * l + 2)
                dve.wait_ge(gelu_act, 3 * l + 3)
                v.scalar_tensor_tensor(yT[:, :, 1, :], vr[:], 0.5, yT[:, :, 0, :].bitcast(F32), ALU.mult,
                                       ALU.subtract).then_inc(y_split, 1)
                for s in range(4):
                    dve.wait_ge(glu_corr, l * 4 + s + 1)
                    v.tensor_tensor(ab[:], ab[:], ps[:, 2:4, 0:T], ALU.add).then_inc(glu_sum, 1)
                    dve.wait_ge(glu_sig, l * 4 + s + 1)
                    step(v.tensor_scalar(ab[:, 1, :], ab[:, 1, :], 0.5, 0.5, ALU.mult, ALU.add))
                    v.tensor_tensor(ab[:, 0, :], ab[:, 0, :], ab[:, 1, :], ALU.mult).then_inc(glu_out, 1)
                    dve.wait_ge(mix_hi, l * 12 + s + 1)
                    v.tensor_tensor(mixT[:, 12 + s, 1, :], ab[:, 0, :], mixT[:, 12 + s, 0, :].bitcast(F32),
                                    ALU.subtract).then_inc(mix_ready, 1)
                dve.wait_ge(mix_ready, l * 16 + 4)
                step(v.memset(pool_pad[:, :, 0:PAD], 0.0))
                for gi, w in enumerate(POOL_WINDOWS):
                    pool_group(l, gi, w)
                    dve.wait_ge(mix_hi, l * 12 + 4 + gi + 1)
                    v.scalar_tensor_tensor(mixT[:, 8 + gi, 1, :], ps[:, 6, 0:T], vcol(l, V_PSC + gi),
                                           mixT[:, 8 + gi, 0, :].bitcast(F32), ALU.mult,
                                           ALU.subtract).then_inc(mix_ready, 1)
                dve.wait_ge(mix_ready, l * 16 + 8)

                dve.wait_ge(swap_ready, l * 5 + 1)
                keys = hT[:, K0:K0 + 2, :]
                rotate(keys, ps[:, 7, :].rearrange("p (a b) -> p a b", a=2))
                v.tensor_tensor(keys, keys, rope[:], ALU.add).then_inc(rope_ready, 1)
                dve.wait_ge(rope_ready, l + 1)
                settle(dve)
                with st.loop(4, 6) as g:
                    attention_group(l, g)

                for p_i, (m0, groups, last) in enumerate(((OUT_M, 4, 0), (DOWN_M, DOWN_GROUPS, FF_TILES % 4))):
                    if p_i:
                        step(v.memset(hbuf[:, :, 0:2], 0.0))
                        split_x(l, l * 2 + 1, UP_M)
                        conv_tile(l, 0, 0)
                        with st.loop(FF_TILES - 1, 4) as j:
                            split_lo(l, UP_M + 1 + j, 0)
                            split_lo(l, UP_M + 1 + j, 1)
                            conv_tile(l, j, 1)
                            split_lo(l, UP_M + 1 + j, 2)
                            gated(l, j)
                            split_lo(l, UP_M + 1 + j, 3)
                            gated_lo(l, j)
                            conv_tile(l, j + 1, 0)
                        conv_tile(l, FF_TILES - 1, 1)
                        gated(l, FF_TILES - 1)
                        gated_lo(l, FF_TILES - 1)
                    full = groups - (1 if last else 0)

                    def short_group(h):
                        for s in range(last):
                            split_lo(l, m0 + groups * h + groups - 1, s, 2 if s == last - 1 else 1)

                    with st.loop(full, 0) as q:
                        for s in range(SLOTS):
                            split_lo(l, m0 + q, s)
                    short_group(0)
                    for s in range(SLOTS):
                        split_lo(l, m0 + groups, s)
                    evac_half(l, 0, l * 4 + 2 * p_i, chunks(l, m0 + groups - 1, 3), l * 2 + p_i, last)
                    with st.loop(full - 1, 0) as q:
                        for s in range(SLOTS):
                            split_lo(l, m0 + groups + 1 + q, s)
                    short_group(1)
                    evac_half(l, 1, l * 4 + 2 * p_i + 1, chunks(l, m0 + 2 * groups - 1, 3), l * 2 + p_i, last)
                    normalise(l * 2 + p_i)

        @block.gpsimd
        def _(pool):
            st = Steps(pool, pool_steps)
            g_ = nc.gpsimd

            def step(ins):
                st.mark(ins)
                st.wait()

            def affine_rows(stage, done, parts):
                for c in range(D // GBC):
                    g_.dma_start(gb[:], a["gb"][bass.ds(stage, 1), :, c * GBC:(c + 1) * GBC]
                                 .rearrange("s g d -> (s g) d").partition_broadcast(P)).then_inc(gb_loaded, 16)
                    pool.wait_ge(gb_loaded, (stage * (D // GBC) + c + 1) * 16)
                    y = xres[:, :, c * GBC:(c + 1) * GBC]
                    step(g_.tensor_tensor(y, y, gb[:, 0:1, :].broadcast_to([P, NT, GBC]), ALU.mult))
                    step(g_.tensor_tensor(y, y, gb[:, 1:2, :].broadcast_to([P, NT, GBC]), ALU.add))
                    if (c + 1) % parts == 0:
                        pool.sem_inc(done, 1)

            def reciprocal_deviation(norm):
                pool.wait_ge(stats_ready, norm * 2 + 2)
                settle(pool)
                step(g_.tensor_scalar(rstd[:, 0, :], mv[:, :, 1], LN_EPS, None, ALU.add))
                g_.tensor_tensor(rstd[:, 1, :], rstd[:, 0, :], neg_half[:], ALU.pow).then_inc(rstd_ready, 1)
                pool.wait_ge(rstd_ready, norm + 1)

            def turns_table(l, c):
                hi, lo = phase[:, 0, bass.ds(c * 4, 4), :], phase[:, 1, bass.ds(c * 4, 4), :]
                f_hi, f_lo = (flat(state[:, i])[:, bass.ds(l * 16 + c * 4, 4)].unsqueeze(2).broadcast_to([P, 4, T])
                              for i in (3, 4))
                t = tokens[:].broadcast_to([P, 4, T])
                g_.tensor_tensor(hi, f_hi, t, ALU.mult)
                step(g_.tensor_tensor(lo, f_lo, t, ALU.mult))
                settle(pool)
                step(g_.tensor_tensor(ptmp[:], hi, lo, ALU.add))
                settle(pool)
                step(g_.tensor_scalar(ptmp[:], ptmp[:], ROUND, None, ALU.add))
                settle(pool)
                step(g_.tensor_scalar(ptmp[:], ptmp[:], ROUND, None, ALU.subtract))
                settle(pool)
                step(g_.tensor_tensor(hi, hi, ptmp[:], ALU.subtract))
                settle(pool)
                step(g_.tensor_tensor(ptmp[:], lo, hi, ALU.add))
                settle(pool)
                step(g_.tensor_scalar(ptmp[:], ptmp[:], 0.5, -0.5, ALU.min, ALU.max))
                settle(pool)
                step(g_.tensor_copy(lo, ptmp[:]))
                pool.sem_inc(turns_ready, 1)

            def output_matrix(c, n):
                pool.wait_ge(c_loaded, (n + 1) * 16)
                pool.wait_ge(y_ready, n + 1)
                settle(pool)
                zr, zi = (flat(state[:, i])[:, bass.ds(n * 4, 4)].unsqueeze(2).broadcast_to([P, 4, 32])
                          for i in (1, 2))
                cr, ci = (c_raw[:, i, :].rearrange("p (j h) -> p j h", j=4) for i in range(2))
                t0, t1 = (c_tmp[:, i, :].rearrange("p (j h) -> p j h", j=4) for i in range(2))
                dst = [c_pad[:, i, :].rearrange("p (j w) -> p j w", w=160)[:, :, 0:32] for i in range(2)]
                g_.tensor_tensor(t0, cr, zr, ALU.mult)
                step(g_.tensor_tensor(t1, ci, zi, ALU.mult))
                step(g_.tensor_tensor(dst[0], t0, t1, ALU.subtract))
                settle(pool)
                g_.tensor_tensor(t0, cr, zi, ALU.mult)
                step(g_.tensor_tensor(t1, ci, zr, ALU.mult))
                step(g_.tensor_tensor(t0, t0, t1, ALU.add))
                settle(pool)
                step(g_.tensor_scalar(dst[1], t0, -1.0, 0.0, ALU.mult, ALU.add))
                pool.sem_inc(cpad_ready, 1)

            step(g_.memset(neg_half[:], -0.5))
            with st.loop(DEPTH, POOL_LAYER) as l:
                pool.wait_ge(zT_ready, l * 8 + 1)
                settle(pool)
                g_.dma_start(tokens[:].rearrange("p a t -> p (a t)"),
                             a["tokens"].partition_broadcast(P)).then_inc(tokens_loaded, 16)
                g_.memset(b_pad[:].rearrange("p a j m -> p (a j m)"), 0.0)
                step(g_.memset(flat(c_pad[:]), 0.0))
                settle(pool)

                def load_matrices(c):
                    pool.wait_ge(bu_used, l * 4 + c + 1)
                    settle(pool)
                    for j in range(4):
                        g_.dma_start(b_pad[32 * j:32 * j + 32, :, j, :],
                                     a["ssm_b"][l, c, 32 * j:32 * j + 32]).then_inc(b_loaded, 16)
                    g_.dma_start(c_raw[:], a["ssm_c"][l, c]).then_inc(c_loaded, 16)

                load_matrices(0)
                pool.wait_ge(tokens_loaded, (l + 1) * 16)
                pool.wait_ge(prm_ready, 1)
                settle(pool)
                turns_table(l, 0)
                turns_table(l, 1)
                pool.wait_ge(prm_ready, 2)
                with st.loop(2, POOL_STATES) as c:
                    output_matrix(c, l * 4 + c)
                    load_matrices(c + 1)
                    turns_table(l, c + 2)
                output_matrix(2, l * 4 + 2)
                load_matrices(3)
                output_matrix(3, l * 4 + 3)
                pool.wait_ge(zT_ready, l * 8 + 4)
                affine_rows(l * 2, xres_ready, D // GBC)
                settle(pool)
                g_.dma_start(pool_w[:], a["pool_w"][l].rearrange("g c d -> c g d")).then_inc(poolw_loaded, 16)
                pool.wait_ge(mix_ready, l * 16 + 8)
                settle(pool)
                step(g_.memset(flat(qpad[:]), 0.0))
                pool.sem_inc(attn_zero, 1)
                step(g_.memset(vpad[:].rearrange("p b h d -> p (b h d)"), 0.0))
                pool.wait_ge(vtok_ready, l + 1)
                settle(pool)
                with pool.Fori(0, 4) as g:
                    pool.wait_ge(mix_ready, l * 16 + 8 + 2 * g)
                    settle(pool)
                    for half in range(2):
                        ins = g_.tensor_copy(vpad[:, :, half, 64 * half:64 * half + 64], vtok[:, :, bass.ds(g * 64, 64)])
                    ins.then_inc(vpad_ready, 1)
                reciprocal_deviation(l * 2)
                pool.wait_ge(zT_ready, l * 8 + 8)
                affine_rows(l * 2 + 1, xres_ready, D // GBC)
                reciprocal_deviation(l * 2 + 1)
            pool.wait_ge(z_ready, 2 * (2 * DEPTH + 1))
            affine_rows(2 * DEPTH, out_ready, D // GBC // 4)


def kernel(**inputs):
    import numpy as np
    import concourse.bacc as bacc
    from concourse.bass_utils import run_bass_kernel_spmd

    def arr(name):
        return np.asarray(inputs[name])

    def tiles(w, n):
        return w.reshape(DEPTH, -1, P, n, P).transpose(0, 3, 2, 1, 4)

    def cols(v):
        v = v.reshape(*v.shape[:-1], -1, P)
        return np.moveaxis(v, -1, 0)

    f4 = np.float32
    order = [(t + 16) % IN_TILES for t in range(IN_TILES)]
    w_in = np.ascontiguousarray(tiles(arr("w_in"), IN_TILES)[:, order])
    w_up = tiles(arr("ffn_w_up"), 2 * FF_TILES).reshape(DEPTH, 2, FF_TILES, P, KT, P).transpose(0, 2, 1, 3, 4, 5)

    def chunked(w):
        w = w.reshape(DEPTH, -1, 2, P, 2, CHUNK).transpose(0, 1, 2, 4, 3, 5)
        return np.ascontiguousarray(w.reshape(DEPTH, -1, 4, P, CHUNK))

    glu_w = arr("ssm_glu_w").reshape(DEPTH, 4, P, 2, 4, P).transpose(0, 4, 2, 1, 3, 5)

    b_blk = np.zeros((DEPTH, 4, 4, 2, 16, 2, 2, 64), f4)
    c_blk = np.zeros((DEPTH, 4, 2, 64, 2, 4, 2, 16), f4)
    for part, (bn, cn) in enumerate((("ssm_b_re", "ssm_c_re"), ("ssm_b_im", "ssm_c_im"))):
        b = arr(bn).reshape(DEPTH, 4, 4, 2, 64, 16)
        c = arr(cn).reshape(DEPTH, 4, 4, 2, 16, 64)
        for g in range(2):
            b_blk[:, :, :, g, :, part, g, :] = b[:, :, :, g].transpose(0, 1, 2, 4, 3)
            c_blk[:, :, g, :, part, :, g, :] = c[:, :, :, g].transpose(0, 1, 4, 2, 3)

    gb = np.zeros((2 * DEPTH + 1, 2, D), f4)
    gb[0, 0] = 1
    for l in range(DEPTH):
        for i, n in enumerate(("ln1", "ln2")):
            gb[2 * l + 1 + i, 0], gb[2 * l + 1 + i, 1] = arr(n + "_g")[l], arr(n + "_b")[l]

    vec = np.zeros((P, DEPTH, NV), f4)
    for l in range(DEPTH):
        parts = [cols(arr("ffn_conv_w")[l]).reshape(P, -1), cols(arr("ffn_conv_b")[l]),
                 cols(gb[2 * l]).reshape(P, -1), cols(gb[2 * l + 1]).reshape(P, -1),
                 cols(arr("pool_scale")[l]), cols(arr("ssm_d")[l].reshape(-1)),
                 cols(arr("ssm_lam_re")[l].reshape(-1)), cols(arr("ssm_lam_im")[l].reshape(-1)),
                 cols(np.repeat(arr("ssm_log_dt")[l], 64)),
                 np.broadcast_to(arr("attn_sinks")[l], (P, 16))]
        vec[:, l] = np.concatenate(parts, axis=1)

    const = np.zeros((P, NC), f4)
    const[:, C_ID:C_ID + P] = np.eye(P)
    row = np.arange(P)
    const[row ^ 32, C_PERM + row] = 1
    inv = np.power(f4(10000.0), -np.arange(32, dtype=f4) / f4(32)).astype(f4)
    ang = (np.arange(T, dtype=f4)[None, :] * inv[row % 32][:, None]).astype(f4)
    const[:, C_COS:C_COS + T] = np.cos(ang)
    const[:, C_SIN:C_SIN + T] = np.sin(ang) * np.where(row % 64 < 32, -1, 1)[:, None]
    key = np.arange(P)
    const[:, C_MASK:C_MASK + P] = np.where(key[None, :] > row[:, None], 0, -1e30)
    const[:, C_MASK + P:C_MASK + 2 * P] = np.where(key[None, :] <= row[:, None], 0, -1e30)
    const[:, C_RECIP:C_RECIP + PAD] = 1.0 / np.arange(1, PAD + 1)
    const[:, C_HALF_PI] = np.pi / 2

    arrays = {
        "x": arr("x")[0], "const": const, "vec": vec.reshape(P, -1), "gb": gb, "tokens": np.arange(T, dtype=f4),
        "w_in": chunked(w_in), "w_up": chunked(w_up),
        "glu_w": np.ascontiguousarray(glu_w.reshape(DEPTH, 4, P, CHUNK)),
        "w_out": arr("w_out"), "w_down": arr("ffn_w_down"), "pool_w": arr("pool_w"),
        "ssm_b": b_blk.reshape(DEPTH, 4, P, 2, P), "ssm_c": c_blk.reshape(DEPTH, 4, P, 2, P),
    }
    nc = bacc.Bacc("TRN2", target_bir_lowering=False, num_devices=1)
    feeds, aps = {}, {}
    for name, v in arrays.items():
        v = np.ascontiguousarray(v)
        feeds["in_" + name] = v
        aps[name] = nc.dram_tensor("in_" + name, v.shape, F32, kind="ExternalInput").ap()
    aps["out"] = nc.dram_tensor("out", (T, D), F32, kind="ExternalOutput").ap()
    trunk(nc, aps)
    r = run_bass_kernel_spmd(nc, [feeds], core_ids=[0])
    return r.results[0]["out"].reshape(1, T, D)
```

```python
from contextlib import ExitStack, contextmanager

import concourse.bass as bass
from concourse import mybir

F32 = mybir.dt.float32
F32R = mybir.dt.float32r
I32 = mybir.dt.int32
ALU = mybir.AluOpType
ACT = mybir.ActivationFunctionType
AX_X = mybir.AxisListType.X

P = 128
D = 2048
T = 256
DEPTH = 2
D_FF = 5504
KT = D // P
NT = T // P
IN_TILES = 20
SSM0, Q0, K0, V0, POOL0 = 0, 4, 12, 14, 16
FF_TILES = D_FF // P
SLOTS = 4
CHUNK = 1024
HALF = D // 2
BANK = 512
GBC = 256
ALPHA = (2 * DEPTH) ** 0.25
LN_EPS = 1e-5
SCALE = 64 ** -0.5
POOL_WINDOWS = (2, 4, 8, 16)
PAD = max(POOL_WINDOWS)

IN_M = 0
GLU_M = IN_M + IN_TILES // 2
OUT_M = GLU_M + 1
UP_M = OUT_M + 2 * KT // 4
DOWN_M = UP_M + FF_TILES
DOWN_GROUPS = (FF_TILES + 3) // 4
LAYER_M = DOWN_M + 2 * DOWN_GROUPS
LAYER_CHUNKS = 4 * LAYER_M
SHORT = 2
TILES = IN_TILES + 2 * FF_TILES

V_CONVW = 0
V_CONVB = V_CONVW + 3 * 2 * FF_TILES
V_G0 = V_CONVB + 2 * FF_TILES
V_G1 = V_G0 + 2 * KT
V_PSC = V_G1 + 2 * KT
V_D = V_PSC + 4
V_LR = V_D + 4
V_LI = V_LR + 16
V_LDT = V_LI + 16
V_SINK = V_LDT + 16
NV = V_SINK + 16

C_ID, C_PERM, C_COS, C_SIN, C_MASK, C_RECIP = 0, 128, 256, 512, 768, 1024
C_HALF_PI = C_RECIP + PAD
C_ROUND = C_HALF_PI + 1
C_ZERO = C_ROUND + 1
NC = C_ZERO + 1

ROUND = 12582912.0

DVE_LAYER = 266
POOL_LAYER = 89
POOL_STATES = 13


class Steps:

    def __init__(self, eng, sem):
        self.eng, self.sem, self.base, self.n = eng, sem, 0, 0

    def mark(self, ins):
        ins.then_inc(self.sem, 1)
        self.n += 1

    def wait(self):
        self.eng.wait_ge(self.sem, self.base + self.n)

    @contextmanager
    def loop(self, n_iter, steps):
        base, n = self.base, self.n
        with self.eng.Fori(0, n_iter) as i:
            self.base = base + i * steps
            yield i
            if self.n - n != steps:
                raise ValueError(f"a loop body of {self.n - n} steps was declared with {steps}")
        self.base, self.n = base, n + n_iter * steps


def trunk(nc, a):
    ctx = ExitStack()
    with ctx:
        def sem(name):
            return ctx.enter_context(nc.semaphore(name))

        def sb(name, shape, dt=F32, stack=ctx):
            return stack.enter_context(nc.sbuf_tensor(name, shape, dt))

        raw = sb("w_raw", [P, SLOTS, CHUNK])
        w_hi = sb("w_hi", [P, SLOTS, CHUNK], F32R)
        w_lo = sb("w_lo", [P, SLOTS, CHUNK], F32R)
        last = ExitStack()
        with last:
            gb_last = sb("gb_last", [P, 2, D], F32, last)
        xT = sb("xT", [P, KT, 2, T], F32R)
        xres = sb("xres", [P, NT, D])
        gb = sb("gb", [P, 2, GBC])
        xtmp = sb("xtmp", [P, 2, 2, T])
        vec = sb("vec", [P, DEPTH * NV])
        const = sb("const", [P, NC])
        stats = sb("stats", [P, NT, 4, 6])
        mv = sb("mv", [P, NT, 2])
        rstd = sb("rstd", [P, 2, NT])
        neg_half = sb("neg_half", [P, NT])
        state = sb("state", [P, 5, DEPTH, 16])
        corr = sb("corr", [P, 2, T])

        mixers = ExitStack()
        with mixers:
            hT = sb("hT", [P, IN_TILES, T], F32, mixers)
            ssm = ExitStack()
            with ssm:
                s1 = sb("s1", [P, 4, T], F32, ssm)
                s2 = sb("s2", [P, 4, T], F32, ssm)
                vr = sb("vr", [P, 4, T], F32, ssm)
                vi = sb("vi", [P, 4, T], F32, ssm)
                m1 = sb("m1", [P, 4, T], F32, ssm)
                m2 = sb("m2", [P, 4, T], F32, ssm)
                prm = sb("prm", [P, 12, DEPTH, 16], F32, ssm)
                b_pad = sb("b_pad", [P, 2, 4, P], F32, ssm)
                c_raw = sb("c_raw", [P, 2, P], F32, ssm)
                c_pad = sb("c_pad", [P, 2, 640], F32, ssm)
                c_tmp = sb("c_tmp", [P, 2, P], F32, ssm)
                ptmp = sb("ptmp", [P, 4, T], F32, ssm)
                tokens = sb("tokens", [P, 1, T], F32, ssm)
                phase = sb("phase", [P, 2, 16, T], F32, ssm)
            mixT = sb("mixT", [P, KT, 2, T], F32R, mixers)
            odd = ExitStack()
            with odd:
                sc0_odd = sb("sc0_odd", [P, 4, P], F32, odd)
                sc1_odd = sb("sc1_odd", [P, 4, 2 * P], F32, odd)
            yT = sb("yT", [P, 4, 2, T], F32R, mixers)
            pool_pad = sb("pool_pad", [P, 2, PAD + T], F32, mixers)
            pool_d = sb("pool_d", [P, T], F32, mixers)
            pool_w = sb("pool_w", [P, 4, P], F32, mixers)
            ab = sb("ab", [P, 2, T], F32, mixers)
            qpad = sb("qpad", [P, 4, T], F32, mixers)
            kdup = sb("kdup", [P, 4, T], F32, mixers)
            vtok = sb("vtok", [P, NT, 4 * 64], F32, mixers)
            vpad = sb("vpad", [P, NT, 2, P], F32, mixers)
            rope = sb("rope", [P, 2, T], F32, mixers)
            sc0 = sb("sc0", [P, 4, P], F32, mixers)
            sc1 = sb("sc1", [P, 4, 2 * P], F32, mixers)
            pT = sb("pT", [P, 12, P], F32, mixers)
            sm = sb("sm", [P, 8, 8], F32, mixers)
            score_buf = ((sc0, sc1), (sc0_odd, sc1_odd))
        mlp = ExitStack()
        with mlp:
            actT = sb("actT", [P, FF_TILES, 2, T], F32R, mlp)
            hbuf = sb("hbuf", [P, 2, T + 2], F32, mlp)
            cv = sb("cv", [P, 2, T], F32, mlp)
            sig = sb("sig", [P, T], F32, mlp)
            act_f = sb("act_f", [P, T], F32, mlp)

        ps = ctx.enter_context(nc.psum_tensor("ps", [P, 8, BANK], F32))

        x_loaded, const_loaded, vec_loaded = sem("x_loaded"), sem("const_loaded"), sem("vec_loaded")
        raw_loaded = [sem(f"raw_loaded{s}") for s in range(SLOTS)]
        hi_done, lo_done, chunk_used = sem("hi_done"), sem("lo_done"), sem("chunk_used")
        corr_ready, tile_evac = sem("corr_ready"), sem("tile_evac")
        z_ready, zT_ready, xtmp_ready, xT_ready = (sem("z_ready"), sem("zT_ready"), sem("xtmp_ready"),
                                                  sem("xT_ready"))
        gb_loaded, xres_ready = sem("gb_loaded"), sem("xres_ready")
        acc_done, acc_evac, stats_ready, rstd_ready = sem("acc_done"), sem("acc_evac"), sem("stats_ready"), sem("rstd_ready")
        prm_dve, prm_act, prm_ready = sem("prm_dve"), sem("prm_act"), sem("prm_ready")
        b_loaded, c_loaded = sem("b_loaded"), sem("c_loaded")
        turns_ready, phase_ready, cpad_ready = sem("turns_ready"), sem("phase_ready"), sem("cpad_ready")
        pads_zero = sem("pads_zero")
        tokens_loaded, abs_ready = sem("tokens_loaded"), sem("abs_ready")
        bu_ready, bu_used, s_ready = sem("bu_ready"), sem("bu_used"), sem("s_ready")
        y_ready, y_used = sem("y_ready"), sem("y_used")
        gelu_dve, gelu_act, y_split = sem("gelu_dve"), sem("gelu_act"), sem("y_split")
        glu_corr, glu_sum, glu_sig, glu_out = sem("glu_corr"), sem("glu_sum"), sem("glu_sig"), sem("glu_out")
        mix_hi, mix_ready = sem("mix_hi"), sem("mix_ready")
        poolw_loaded, pool_in, pool_out = sem("poolw_loaded"), sem("pool_in"), sem("pool_out")
        swap_ready, rope_ready, kdup_ready = sem("swap_ready"), sem("rope_ready"), sem("kdup_ready")
        vT_ready, vtok_ready, vpad_ready = sem("vT_ready"), sem("vtok_ready"), sem("vpad_ready")
        q_ready = sem("q_ready")
        score_ready, max_ready, exp_ready, prob_ready = (sem("score_ready"), sem("max_ready"), sem("exp_ready"),
                                                         sem("prob_ready"))
        pT_ready, pT_copied, o_ready, attn_zero = sem("pT_ready"), sem("pT_copied"), sem("o_ready"), sem("attn_zero")
        conv_first, conv_done, sig_ready = sem("conv_first"), sem("conv_done"), sem("sig_ready")
        act_ready, act_hi, act_lo = sem("act_ready"), sem("act_hi"), sem("act_lo")
        dve_steps, pool_steps = sem("dve_steps"), sem("pool_steps")
        apart = sem("apart")
        out_scaled, out_ready, out_written = sem("out_scaled"), sem("out_ready"), sem("out_written")
        gb_last_loaded = sem("gb_last_loaded")

        def settle(eng):
            eng.sem_inc(apart, 1)

        def chunks(l, m, s):
            return l * LAYER_CHUNKS + m * 4 + s + 1

        def vcol(l, col):
            return vec[:, bass.ds(l * NV + col, 1)]

        def flat(ap):
            return ap.rearrange("p a b -> p (a b)")

        block = ctx.enter_context(nc.Block())

        @block.sync
        def _(sp):
            sp.dma_start(vec[:], a["vec"]).then_inc(vec_loaded, 16)
            sp.dma_start(const[:], a["const"]).then_inc(const_loaded, 16)
            sp.dma_start(xres[:], a["x"].rearrange("(t p) d -> p t d", p=P)).then_inc(x_loaded, 16)

            def load(l, m, s, src):
                sp.wait_ge(lo_done, chunks(l, m, s))
                settle(sp)
                sp.dma_start(raw[:, s, :], src).then_inc(raw_loaded[s], 16)

            with sp.Fori(0, DEPTH) as l:
                def load_pair(i):
                    for s in range(SLOTS):
                        load(l, IN_M + i, s, a["w_in"][l, i, s])

                def load_b(c):
                    sp.wait_ge(bu_used, l * 4 + c + 1)
                    settle(sp)
                    for j in range(4):
                        sp.dma_start(b_pad[32 * j:32 * j + 32, :, j, :],
                                     a["ssm_b"][l, c, 32 * j:32 * j + 32]).then_inc(b_loaded, 16)

                def load_c(c):
                    sp.dma_start(c_raw[:], a["ssm_c"][l, c]).then_inc(c_loaded, 16)

                load_pair(0)
                sp.wait_ge(pads_zero, l + 1)
                load_b(0)
                load_c(0)
                load_pair(1)
                with sp.Fori(0, 3) as c:
                    load_pair(2 * c + 2)
                    load_b(c + 1)
                    load_pair(2 * c + 3)
                    sp.wait_ge(cpad_ready, l * 4 + c + 1)
                    settle(sp)
                    load_c(c + 1)
                load_pair(8)
                load_pair(9)
                for s in range(SLOTS):
                    load(l, GLU_M, s, a["glu_w"][l, s])
                sp.wait_ge(s_ready, (l + 1) * 4)
                settle(sp)
                sp.dma_start(pool_w[:], a["pool_w"][l].rearrange("g c d -> c g d")).then_inc(poolw_loaded, 16)
                with sp.Fori(0, 2) as h:
                    for k in range(KT):
                        e = (k + KT // 2) % KT
                        load(l, OUT_M + 4 * h + k // 4, k % 4,
                             a["w_out"][l, e * P:(e + 1) * P, bass.ds(h * HALF, HALF)])
                with sp.Fori(0, FF_TILES) as j:
                    for s in range(SLOTS):
                        load(l, UP_M + j, s, a["w_up"][l, j, s])
                with sp.Fori(0, 2) as h:
                    for k in range(FF_TILES):
                        load(l, DOWN_M + DOWN_GROUPS * h + k // 4, k % 4,
                             a["w_down"][l, k * P:(k + 1) * P, bass.ds(h * HALF, HALF)])
            for c in range(4):
                sp.wait_ge(out_ready, c + 1)
                sp.dma_start(a["out"].rearrange("(t p) d -> p t d", p=P)[:, :, c * BANK:(c + 1) * BANK],
                             xres[:, :, c * BANK:(c + 1) * BANK]).then_inc(out_written, 16)
            sp.wait_ge(out_written, 64)

        @block.tensor
        def _(pe):
            ident = const[:, C_ID:C_ID + P]
            perm = const[:, C_PERM:C_PERM + P]

            def parts_ready(l, m, s):
                pe.wait_ge(lo_done, SLOTS + chunks(l, m, s))

            def transpose_z(stage):
                for r in range(4):
                    if r >= 2:
                        pe.wait_ge(xtmp_ready, stage * 8 + 2 * r - 2)
                    for t in range(NT):
                        pe.wait_ge(z_ready, stage * 4 + 2 * (r // 2) + t + 1)
                        for d in range(4):
                            mm = nc.tensor.transpose(
                                ps[:, 4 + 2 * (r % 2) + d // 2, bass.ds((d % 2) * T + t * P, P)],
                                xres[:, t, (4 * r + d) * P:(4 * r + d + 1) * P], ident)
                    mm.then_inc(zT_ready, 1)

            def project_tile(l, m, which, tile, stage):
                pe.wait_ge(tile_evac, l * TILES + tile + 1)
                for c in range(2):
                    s = 2 * which + c
                    parts_ready(l, m, s)
                    for k in range(8):
                        kk = 8 * c + k
                        if kk % 4 == 0:
                            pe.wait_ge(xT_ready, 2 + stage * 8 + 2 * (kk // 4) + 2)
                        nc.tensor.matmul(ps[:, which, :], w_hi[:, s, k * P:(k + 1) * P], flat(xT[:, kk]),
                                         start=(kk == 0), stop=False)
                        mm = nc.tensor.matmul(ps[:, which, 0:T], w_lo[:, s, k * P:(k + 1) * P], xT[:, kk, 0, :],
                                              start=False, stop=(kk == KT - 1))
                    mm.then_inc(chunk_used, 1)

            def project_tokens(l, m0, act, n_k, half_no, before_k):
                for k in range(n_k):
                    before_k(k)
                    m, s = m0 + k // 4, k % 4
                    parts_ready(l, m, s)
                    for t in range(NT):
                        hi = act(k)[:, 0, t * P:(t + 1) * P]
                        lo = act(k)[:, 1, t * P:(t + 1) * P]
                        for c in range(2):
                            if k == 0:
                                pe.wait_ge(acc_evac, half_no * 4 + 2 * t + c + 1)
                            cols = slice(c * BANK, (c + 1) * BANK)
                            acc = ps[:, 2 * t + c, :]
                            nc.tensor.matmul(acc, hi, w_hi[:, s, cols], start=(k == 0), stop=False)
                            nc.tensor.matmul(acc, hi, w_lo[:, s, cols], start=False, stop=False)
                            mm = nc.tensor.matmul(acc, lo, w_hi[:, s, cols], start=False, stop=(k == n_k - 1))
                            if k == n_k - 1 and 2 * t + c < 3:
                                mm.then_inc(acc_done, 1)
                    mm.then_inc(chunk_used, 2 if k == n_k - 1 and n_k % 4 else 1)

            def input_of_states(l, c):
                pe.wait_ge(b_loaded, (l * 4 + c + 1) * 64)
                pe.wait_ge(bu_used, l * 4 + c + 1)
                for ri in range(2):
                    for j in range(4):
                        mm = nc.tensor.matmul(ps[:, 2 + 2 * ri + j // 2, bass.ds((j % 2) * T, T)], b_pad[:, ri, j, :],
                                              hT[:, bass.ds(SSM0 + c, 1), :].rearrange("p a b -> p (a b)"),
                                              start=True, stop=True)
                mm.then_inc(bu_ready, 1)

            def output_of_states(l, c):
                pe.wait_ge(s_ready, l * 4 + c + 1)
                pe.wait_ge(cpad_ready, l * 4 + c + 1)
                for j in range(4):
                    for ri, src in enumerate((s1, s2)):
                        mm = nc.tensor.matmul(flat(ps[:, 6:8, :])[:, bass.ds(c * T, T)], c_pad[:, ri, j * P:(j + 1) * P], src[:, j, :],
                                              start=(j == 0 and ri == 0), stop=(j == 3 and ri == 1))
                mm.then_inc(y_ready, 1)

            def swap_halves(tile):
                nc.tensor.matmul(ps[:, 1, :], perm, hT[:, bass.ds(tile, 2), :].rearrange("p a b -> p (a b)"),
                                 start=True, stop=True).then_inc(swap_ready, 1)

            def scores(l, g):
                pe.wait_ge(q_ready, l * 4 + g + 1)
                keys = kdup[:, bass.ds(g, 1), :].rearrange("p a b -> p (a b)")
                for h in range(4):
                    nc.tensor.matmul(ps[:, 2, h * P:(h + 1) * P], qpad[:, h, 0:P], keys[:, 0:P],
                                     start=True, stop=True)
                for h in range(4):
                    mm = nc.tensor.matmul(ps[:, 3 + h // 2, bass.ds((h % 2) * T, T)], qpad[:, h, P:T], keys,
                                          start=True, stop=True)
                mm.then_inc(score_ready, 1)

            def transpose_probs(l, g):
                pe.wait_ge(prob_ready, l * 4 + g + 1)
                sc0, sc1 = score_buf[g % 2]
                for h in range(4):
                    for b, src in enumerate((sc0[:, h, :], sc1[:, h, 0:P], sc1[:, h, P:2 * P])):
                        i = 3 * h + b
                        mm = nc.tensor.transpose(ps[:, 5 + i // 4, bass.ds((i % 4) * P, P)], src, ident)
                mm.then_inc(pT_ready, 1)

            def attention_output(l, g, bank):
                pe.wait_ge(pT_copied, l * 4 + g + 1)
                pe.wait_ge(vpad_ready, l * 4 + g + 1)
                pe.wait_ge(mix_ready, l * 16 + 8 + 2 * g)
                settle(pe)
                for hp in range(2):
                    for q in range(2):
                        out = ps[:, bank, bass.ds(hp * T + q * P, P)]
                        pairs = [(vpad[:, 0, par, :], pT[:, 3 * (2 * hp + par) + q, :]) for par in range(2)]
                        if q:
                            pairs += [(vpad[:, 1, par, :], pT[:, 3 * (2 * hp + par) + 2, :]) for par in range(2)]
                        for i, (v, p) in enumerate(pairs):
                            mm = nc.tensor.matmul(out, v, p, start=(i == 0), stop=(i == len(pairs) - 1))
                mm.then_inc(o_ready, 1)

            nc.tensor.sem_inc(chunk_used, SLOTS)
            pe.wait_ge(const_loaded, 16)
            pe.wait_ge(x_loaded, 16)
            settle(pe)
            with pe.Fori(0, DEPTH) as l:
                transpose_z(l * 2)

                def project_pair(i):
                    for which in range(2):
                        project_tile(l, IN_M + i, which, i * 2 + which, l * 2)

                project_pair(0)
                pe.wait_ge(tile_evac, l * TILES + 2 + 1)
                input_of_states(l, 0)
                project_pair(1)
                with pe.Fori(0, 3) as c:
                    project_pair(2 * c + 2)
                    input_of_states(l, c + 1)
                    project_pair(2 * c + 3)
                    output_of_states(l, c)
                project_pair(8)
                project_pair(9)
                output_of_states(l, 3)

                pe.wait_ge(tile_evac, l * TILES + IN_TILES + 2)
                swap_halves(K0)
                for b in range(NT):
                    for i in range(2):
                        mm = nc.tensor.transpose(ps[:, 0, bass.ds(b * T + i * P, P)], hT[:, V0 + i, b * P:(b + 1) * P],
                                                 ident)
                mm.then_inc(vT_ready, 1)

                def glu_pair(s):
                    parts_ready(l, GLU_M, s)
                    pe.wait_ge(glu_sum, l * 4 + s + 1)
                    for k in range(4):
                        for ab_i in range(2):
                            wcol = slice((2 * k + ab_i) * P, (2 * k + ab_i + 1) * P)
                            nc.tensor.matmul(ps[:, 2 + ab_i, :], w_hi[:, s, wcol], flat(yT[:, k]),
                                             start=(k == 0), stop=False)
                            mm = nc.tensor.matmul(ps[:, 2 + ab_i, 0:T], w_lo[:, s, wcol], yT[:, k, 0, :],
                                                  start=False, stop=(k == 3))
                    mm.then_inc(chunk_used, 1)

                def pool_product(gi):
                    pe.wait_ge(pool_in, l * 4 + gi + 1)
                    nc.tensor.matmul(ps[:, 6 + gi % 2, 0:T], pool_w[:, gi, :], pool_d[:], start=True,
                                     stop=True).then_inc(pool_out, 1)

                pe.wait_ge(y_split, l + 1)
                glu_pair(0)
                pe.wait_ge(rope_ready, l + 1)
                swap_halves(Q0)
                pe.wait_ge(poolw_loaded, (l + 1) * 16)
                pool_product(0)
                for s in range(1, 4):
                    glu_pair(s)
                    pool_product(s)

                pe.wait_ge(kdup_ready, l + 1)
                pe.wait_ge(glu_sum, l * 4 + 5)
                scores(l, 0)
                swap_halves(Q0 + 2)
                for g in range(3):
                    scores(l, g + 1)
                    if g < 2:
                        swap_halves(Q0 + 4 + 2 * g)
                    transpose_probs(l, g)
                    attention_output(l, g, 0)
                pe.wait_ge(max_ready, l * 4 + 4)

                def out_step(h, k):
                    if h == 0 and k == 2:
                        transpose_probs(l, 3)
                    if h == 0 and k == 3:
                        attention_output(l, 3, 4)
                    pe.wait_ge(mix_ready, l * 16 + max(k + 1, KT - 2))

                for h in range(2):
                    project_tokens(l, OUT_M + 4 * h, lambda k: mixT[:, (k + KT // 2) % KT], KT, l * 4 + h,
                                   lambda k: out_step(h, k))
                transpose_z(l * 2 + 1)
                with pe.Fori(0, FF_TILES) as j:
                    for which in range(2):
                        project_tile(l, UP_M + j, which, IN_TILES + j * 2 + which, l * 2 + 1)
                with pe.Fori(0, 2) as h:
                    project_tokens(l, DOWN_M + DOWN_GROUPS * h, lambda k: actT[:, k], FF_TILES, l * 4 + 2 + h,
                                   lambda k: pe.wait_ge(act_lo, l * FF_TILES + k + 1))

        @block.scalar
        def _(act):
            def round_hi(l, m, s):
                act.wait_ge(raw_loaded[s], loads(l, m, s))
                act.wait_ge(chunk_used, chunks(l, m, s))
                nc.scalar.activation(w_hi[:, s, :], raw[:, s, :], ACT.Copy).then_inc(hi_done, 1)

            def loads(l, m, s):
                return (l * (LAYER_M - (SHORT if s == 3 else 0)) + m + 1) * 16

            def round_hi_down(l, h, q, s, count=1):
                act.wait_ge(raw_loaded[s], loads(l, DOWN_M + (DOWN_GROUPS - (1 if s == 3 else 0)) * h + q, s))
                act.wait_ge(chunk_used, chunks(l, DOWN_M + DOWN_GROUPS * h + q, s))
                nc.scalar.activation(w_hi[:, s, :], raw[:, s, :], ACT.Copy).then_inc(hi_done, count)

            def correction(l, tile, which, m, s):
                act.wait_ge(chunk_used, SLOTS + chunks(l, m, s))
                act.wait_ge(tile_evac, l * TILES + tile + 1)
                nc.scalar.activation(corr[:, which, :], ps[:, which, T:2 * T], ACT.Copy).then_inc(corr_ready, 1)

            def affine(l, stage, col, m):
                for r in range(4):
                    act.wait_ge(zT_ready, stage * 4 + r + 1)
                    for u in range(2):
                        act.wait_ge(xT_ready, stage * 8 + 2 * r + u + 1)
                        for i in range(2):
                            d = 2 * u + i
                            ins = nc.scalar.activation(
                                xtmp[:, u, i, :], ps[:, 4 + 2 * (r % 2) + u, bass.ds(i * T, T)],
                                ACT.Identity, scale=vcol(l, col + 4 * r + d), bias=vcol(l, col + KT + 4 * r + d))
                        ins.then_inc(xtmp_ready, 1)
                    round_hi(l, m, r)

            def conv_first_tap(l, j, which, tile):
                f = j + FF_TILES * which
                act.wait_ge(tile_evac, 2 + l * TILES + tile + 1)
                nc.scalar.activation(cv[:, which, :], hbuf[:, which, 0:T], ACT.Identity,
                                     scale=vcol(l, V_CONVW + f), bias=vcol(l, V_CONVB + f)).then_inc(conv_first, 1)

            def gate_part(l, j, with_chunks, m, ahead=False):
                tile = IN_TILES + 2 * j + 1
                correction(l, tile, 1, UP_M + j, 3)
                conv_first_tap(l, j, 1, tile)
                if with_chunks:
                    round_hi(l, m, 2)
                act.wait_ge(conv_done, l * FF_TILES + j + 1)
                nc.scalar.activation(sig[:], cv[:, 1, :], ACT.Tanh, scale=0.5).then_inc(sig_ready, 1)
                if with_chunks:
                    round_hi(l, m, 3)
                act.wait_ge(act_ready, l * FF_TILES + j + 1)
                nc.scalar.activation(actT[:, bass.ds(j, 1), 0, :].rearrange("p a b -> p (a b)"), act_f[:],
                                     ACT.Copy).then_inc(act_hi, 1)
                if ahead:
                    round_hi(l, m + 1, 0)

            def value_part(l, j):
                tile = IN_TILES + 2 * j
                correction(l, tile, 0, UP_M + j, 1)
                conv_first_tap(l, j, 0, tile)

            def phase_table(l, c):
                n = l * 4 + c
                act.wait_ge(turns_ready, n + 1)
                settle(act)
                y, co = phase[:, 1, bass.ds(c * 4, 4), :], phase[:, 0, bass.ds(c * 4, 4), :]
                nc.scalar.activation(co, y, ACT.Abs).then_inc(abs_ready, 1)
                act.wait_ge(abs_ready, n + 1)
                settle(act)
                nc.scalar.activation(y, y, ACT.Sin, scale=6.283185)
                nc.scalar.activation(co, co, ACT.Sin, scale=-6.283185,
                                     bias=const[:, C_HALF_PI:C_HALF_PI + 1]).then_inc(phase_ready, 1)

            act.wait_ge(vec_loaded, 16)
            act.wait_ge(const_loaded, 16)
            act.wait_ge(prm_dve, 1)
            nc.scalar.activation(prm[:, 4:7], prm[:, 4:7], ACT.Sin).then_inc(prm_act, 1)
            with act.Fori(0, DEPTH) as l:
                affine(l, l * 2, V_G0, IN_M)
                correction(l, 0, 0, IN_M, 1)

                def pair_part(i):
                    round_hi(l, IN_M + 1 + i, 0)
                    round_hi(l, IN_M + 1 + i, 1)
                    correction(l, 2 * i + 1, 1, IN_M + i, 3)
                    round_hi(l, IN_M + 1 + i, 2)
                    round_hi(l, IN_M + 1 + i, 3)
                    correction(l, 2 * i + 2, 0, IN_M + 1 + i, 1)

                pair_part(0)
                phase_table(l, 0)
                with act.Fori(0, 3) as c:
                    pair_part(2 * c + 1)
                    pair_part(2 * c + 2)
                    phase_table(l, c + 1)
                pair_part(7)
                pair_part(8)
                correction(l, IN_TILES - 1, 1, IN_M + IN_TILES // 2 - 1, 3)
                for s in range(SLOTS):
                    round_hi(l, GLU_M, s)

                act.wait_ge(y_used, l + 1)
                nc.scalar.activation(flat(s1[:]), flat(hT[:, SSM0:SSM0 + 4, :]), ACT.Square).then_inc(gelu_act, 1)
                act.wait_ge(gelu_dve, 2 * l + 1)
                nc.scalar.activation(flat(s2[:]), flat(s2[:]), ACT.Tanh,
                                     scale=0.7978845608028654).then_inc(gelu_act, 1)
                act.wait_ge(gelu_dve, 2 * l + 2)
                nc.scalar.activation(yT[:, :, 0, :], vr[:], ACT.Copy, scale=0.5).then_inc(gelu_act, 1)
                act.wait_ge(vT_ready, l + 1)
                nc.scalar.activation(flat(vtok[:]), ps[:, 0, :], ACT.Copy).then_inc(vtok_ready, 1)
                act.wait_ge(rope_ready, l + 1)
                for kv in range(2):
                    for half in range(2):
                        ins = nc.scalar.activation(kdup[64 * half:64 * half + 64, kv::2, :],
                                                   hT[64 * kv:64 * kv + 64, K0:K0 + 2, :], ACT.Copy)
                ins.then_inc(kdup_ready, 1)
                for s in range(4):
                    act.wait_ge(chunk_used, SLOTS + chunks(l, GLU_M, s))
                    nc.scalar.activation(ab[:], ps[:, 2:4, T:2 * T], ACT.Copy).then_inc(glu_corr, 1)
                    act.wait_ge(glu_sum, 1 + l * 4 + s + 1)
                    nc.scalar.activation(ab[:, 1, :], ab[:, 1, :], ACT.Tanh, scale=0.5).then_inc(glu_sig, 1)
                    act.wait_ge(glu_out, l * 4 + s + 1)
                    nc.scalar.activation(mixT[:, 12 + s, 0, :], ab[:, 0, :], ACT.Copy).then_inc(mix_hi, 1)
                    act.wait_ge(pool_out, l * 4 + s + 1)
                    nc.scalar.activation(mixT[:, 8 + s, 0, :], ps[:, 6 + s % 2, 0:T], ACT.Copy,
                                         scale=vcol(l, V_PSC + s)).then_inc(mix_hi, 1)
                    act.wait_ge(mix_ready, l * 16 + 2 * s + 1)

                def exponentials(g):
                    act.wait_ge(max_ready, l * 4 + g + 1)
                    for b, scores in enumerate(score_buf[g % 2]):
                        for h in range(4):
                            nc.scalar.activation(scores[:, h, :], scores[:, h, :], ACT.Exp,
                                                 bias=sm[:, 2 + b, h:h + 1], accum_out=sm[:, 4 + b, h:h + 1])
                    nc.scalar.activation(sm[:, 6, :], sm[:, 6, :], ACT.Exp).then_inc(exp_ready, 1)

                def copy_probs(g):
                    act.wait_ge(pT_ready, l * 4 + g + 1)
                    nc.scalar.activation(flat(pT[:]), ps[:, 5:8, :].rearrange("p a b -> p (a b)"),
                                         ACT.Copy).then_inc(pT_copied, 1)

                def output_hi(g, bank):
                    act.wait_ge(o_ready, l * 4 + g + 1)
                    nc.scalar.activation(mixT[:, bass.ds(2 * g, 2), 0, :],
                                         ps[:, bank, :].rearrange("p (a b) -> p a b", a=2),
                                         ACT.Copy).then_inc(mix_hi, 1)

                exponentials(0)
                for s in range(SLOTS):
                    round_hi(l, OUT_M, s)
                for g in range(3):
                    copy_probs(g)
                    exponentials(g + 1)
                    output_hi(g, 0)
                copy_probs(3)
                output_hi(3, 4)

                with act.Fori(0, 7) as q:
                    for s in range(SLOTS):
                        round_hi(l, OUT_M + 1 + q, s)
                affine(l, l * 2 + 1, V_G1, UP_M)
                round_hi(l, UP_M + 1, 0)
                value_part(l, 0)

                def up_pair(j, ahead):
                    round_hi(l, UP_M + 1 + j, 1)
                    gate_part(l, j, True, UP_M + 1 + j, ahead)
                    value_part(l, j + 1)

                with act.Fori(0, FF_TILES - 2) as j:
                    up_pair(j, True)
                up_pair(FF_TILES - 2, False)
                gate_part(l, FF_TILES - 1, False, 0)
                with act.Fori(0, 2) as h:
                    with act.Fori(0, DOWN_GROUPS - 1) as q:
                        for s in range(SLOTS):
                            round_hi_down(l, h, q, s)
                    for s in range(FF_TILES % 4):
                        round_hi_down(l, h, DOWN_GROUPS - 1, s, 2 if s == FF_TILES % 4 - 1 else 1)

        @block.vector
        def _(dve):
            st = Steps(dve, dve_steps)
            v = nc.vector

            def split_lo(l, m, s, last=1):
                dve.wait_ge(hi_done, chunks(l, m, s))
                v.tensor_tensor(w_lo[:, s, :], raw[:, s, :], w_hi[:, s, :].bitcast(F32),
                                ALU.subtract).then_inc(lo_done, last)

            def split_x(l, stage, m):
                for r in range(4):
                    for u in range(2):
                        k = 4 * r + 2 * u
                        dve.wait_ge(xtmp_ready, stage * 8 + 2 * r + u + 1)
                        step(v.tensor_copy(xT[:, k:k + 2, 0, :], xtmp[:, u]))
                        v.tensor_tensor(xT[:, k:k + 2, 1, :], xtmp[:, u], xT[:, k:k + 2, 0, :].bitcast(F32),
                                        ALU.subtract).then_inc(xT_ready, 1)
                    split_lo(l, m, r)

            def evac_in(l, tile, which):
                dve.wait_ge(corr_ready, l * TILES + tile + 1)
                v.tensor_tensor(hT[:, bass.ds(tile, 1), :].rearrange("p a b -> p (a b)"), ps[:, which, 0:T],
                                corr[:, which, :], ALU.add).then_inc(tile_evac, 1)

            def conv_tile(l, j, which):
                tile = IN_TILES + 2 * j + which
                f = j + FF_TILES * which
                dve.wait_ge(corr_ready, l * TILES + tile + 1)
                v.tensor_tensor(hbuf[:, which, 2:T + 2], ps[:, which, 0:T], corr[:, which, :],
                                ALU.add).then_inc(tile_evac, 1)
                dve.wait_ge(tile_evac, 2 + l * TILES + tile + 1)
                dve.wait_ge(conv_first, l * 2 * FF_TILES + 2 * j + which + 1)
                st.mark(v.scalar_tensor_tensor(cv[:, which, :], hbuf[:, which, 1:T + 1],
                                               vcol(l, V_CONVW + 2 * FF_TILES + f), cv[:, which, :],
                                               ALU.mult, ALU.add))
                st.wait()
                ins = v.scalar_tensor_tensor(cv[:, which, :], hbuf[:, which, 2:T + 2],
                                             vcol(l, V_CONVW + 4 * FF_TILES + f), cv[:, which, :],
                                             ALU.mult, ALU.add)
                if which:
                    ins.then_inc(conv_done, 1)
                else:
                    st.mark(ins)

            def gated(l, j):
                dve.wait_ge(sig_ready, l * FF_TILES + j + 1)
                st.mark(v.scalar_tensor_tensor(cv[:, 1, :], sig[:], 1.0, cv[:, 1, :], ALU.add, ALU.mult))
                st.wait()
                v.scalar_tensor_tensor(act_f[:], cv[:, 1, :], 0.5, cv[:, 0, :], ALU.mult,
                                       ALU.mult).then_inc(act_ready, 1)

            def gated_lo(l, j):
                dve.wait_ge(act_hi, l * FF_TILES + j + 1)
                ap = actT[:, bass.ds(j, 1), :, :].rearrange("p a h b -> p (a h) b")
                v.tensor_tensor(ap[:, 1, :], act_f[:], ap[:, 0, :].bitcast(F32), ALU.subtract).then_inc(act_lo, 1)

            def evac_half(l, h, half_no, m_last, stage, between):
                dve.wait_ge(xres_ready, stage + 1)
                settle(dve)
                banks = [(t, c, xres[:, t, bass.ds(h * HALF + c * BANK, BANK)]) for t in range(NT) for c in range(2)]
                for i, (t, c, y) in enumerate(banks):
                    if i < 3:
                        dve.wait_ge(acc_done, half_no * 3 + i + 1)
                    else:
                        dve.wait_ge(chunk_used, SLOTS + m_last)
                    v.scalar_tensor_tensor(y, y, ALPHA, ps[:, i, :], ALU.mult, ALU.add).then_inc(acc_evac, 1)
                between()
                for i, (t, c, y) in enumerate(banks):
                    dve.wait_ge(acc_evac, 4 + half_no * 4 + i + 1)
                    st.mark(v.bn_stats(stats[:, t, bass.ds(2 * h + c, 1), :].rearrange("p a b -> p (a b)"), y))

            def normalise(stage):
                st.wait()
                settle(dve)
                for t in range(NT):
                    v.bn_aggr(mv[:, t, :], stats[:, t, :, :].rearrange("p a b -> p (a b)")).then_inc(stats_ready, 1)
                dve.wait_ge(stats_ready, stage * 2 + 2)
                dve.wait_ge(rstd_ready, stage + 1)
                for h in range(2):
                    for t in range(NT):
                        y = xres[:, t, h * HALF:(h + 1) * HALF]
                        v.tensor_scalar(y, y, mv[:, t, 0:1], rstd[:, 1, t:t + 1],
                                        ALU.subtract, ALU.mult).then_inc(z_ready, 1)

            def step(ins):
                st.mark(ins)
                st.wait()

            def exp_parts(x, n, r, acc, two_n):
                step(v.tensor_scalar(n, x, 1.0 / 0.6931471805599453, ROUND, ALU.mult, ALU.add))
                step(v.tensor_scalar(n, n, ROUND, None, ALU.subtract))
                step(v.scalar_tensor_tensor(r, n, -0.693359375, x, ALU.mult, ALU.add))
                step(v.scalar_tensor_tensor(r, n, 2.12194440e-4, r, ALU.mult, ALU.add))
                step(v.tensor_scalar(acc, r, 1.0 / 40320, None, ALU.mult))
                for c in (1 / 5040, 1 / 720, 1 / 120, 1 / 24, 1 / 6, 0.5, 1.0):
                    step(v.scalar_tensor_tensor(acc, acc, c, r, ALU.add, ALU.mult))
                step(v.tensor_scalar(n, n, 127.0, 0.0, ALU.add, ALU.max))
                step(v.tensor_scalar(two_n.bitcast(I32), n, 255.0, float(2 ** 23), ALU.min, ALU.mult))

            def state_parameters():
                by_layer = vec[:].rearrange("p (l n) -> p l n", l=DEPTH)
                lr = by_layer[:, :, V_LR:V_LR + 16]
                li = by_layer[:, :, V_LI:V_LI + 16]
                ldt = by_layer[:, :, V_LDT:V_LDT + 16]
                mag, zr, zi, f_hi, f_lo = (state[:, i] for i in range(5))
                dt, em1, th, f = (prm[:, i] for i in range(4))
                cs, sn, sh = (prm[:, i] for i in range(4, 7))
                n, r, acc, two_n, t1 = (prm[:, i] for i in range(7, 12))
                t2 = f
                step(v.tensor_scalar(t1, ldt, -150.0, 150.0, ALU.max, ALU.min))
                exp_parts(t1, n, r, acc, two_n)
                step(v.tensor_tensor(acc, acc, two_n, ALU.mult))
                step(v.tensor_tensor(dt, acc, two_n, ALU.add))
                step(v.tensor_tensor(th, li, dt, ALU.mult))
                step(v.tensor_scalar(n, th, 0.15915494309189535, ROUND, ALU.mult, ALU.add))
                step(v.tensor_scalar(n, n, ROUND, None, ALU.subtract))
                step(v.scalar_tensor_tensor(th, n, -6.28125, th, ALU.mult, ALU.add))
                step(v.scalar_tensor_tensor(th, n, -1.934051513671875e-3, th, ALU.mult, ALU.add))
                step(v.scalar_tensor_tensor(th, n, -1.2556659146019e-6, th, ALU.mult, ALU.add))
                step(v.tensor_scalar(sn, th, 3.1415925, -3.1415925, ALU.min, ALU.max))
                step(v.tensor_scalar(sh, sn, 0.5, None, ALU.mult))
                step(v.tensor_scalar(cs, sn, -1.0, None, ALU.mult))
                step(v.tensor_tensor(cs, cs, sn, ALU.max))
                v.tensor_scalar(cs, cs, -1.0, 1.5707963267948966, ALU.mult, ALU.add).then_inc(prm_dve, 1)
                step(v.tensor_scalar(f, th, 0.15915494309189535, None, ALU.mult))
                step(v.tensor_scalar(f_hi, f, 192.0, None, ALU.add))
                step(v.tensor_scalar(f_hi, f_hi, 192.0, None, ALU.subtract))
                step(v.tensor_tensor(f_lo, f, f_hi, ALU.subtract))
                v.sem_inc(prm_ready, 1)
                step(v.tensor_tensor(t2, lr, dt, ALU.mult))
                step(v.tensor_scalar(t2, t2, -150.0, 150.0, ALU.max, ALU.min))
                exp_parts(t2, n, r, acc, two_n)
                step(v.tensor_tensor(acc, acc, two_n, ALU.mult))
                step(v.tensor_tensor(mag, acc, two_n, ALU.add))
                step(v.scalar_tensor_tensor(em1, two_n, -1.0, acc, ALU.add, ALU.add))
                dve.wait_ge(prm_act, 1)
                step(v.tensor_tensor(t1, sh, sh, ALU.mult))
                step(v.tensor_tensor(t2, em1, cs, ALU.mult))
                step(v.scalar_tensor_tensor(t1, t1, -2.0, t2, ALU.mult, ALU.add))
                step(v.tensor_tensor(t2, mag, sn, ALU.mult))
                step(v.tensor_tensor(n, lr, lr, ALU.mult))
                step(v.tensor_tensor(r, li, li, ALU.mult))
                step(v.tensor_tensor(n, n, r, ALU.add))
                step(v.reciprocal(n, n))
                step(v.tensor_tensor(zr, t1, lr, ALU.mult))
                step(v.tensor_tensor(r, t2, li, ALU.mult))
                step(v.tensor_tensor(zr, zr, r, ALU.add))
                step(v.tensor_tensor(zr, zr, n, ALU.mult))
                step(v.tensor_tensor(zi, t2, lr, ALU.mult))
                step(v.tensor_tensor(r, t1, li, ALU.mult))
                step(v.tensor_tensor(zi, zi, r, ALU.subtract))
                v.tensor_tensor(zi, zi, n, ALU.mult).then_inc(prm_ready, 1)

            def states_and_pairs(l, c):
                n = l * 4 + c
                m = IN_M + 2 * c + 2
                co, si = phase[:, 0, bass.ds(c * 4, 4), :], phase[:, 1, bass.ds(c * 4, 4), :]
                p, q = ps[:, 2:4, :].rearrange("p a (j t) -> p (a j) t", j=2), \
                    ps[:, 4:6, :].rearrange("p a (j t) -> p (a j) t", j=2)
                split_lo(l, m, 0)
                split_lo(l, m, 1)
                dve.wait_ge(phase_ready, n + 1)
                dve.wait_ge(bu_ready, n + 1)
                v.tensor_tensor(vr[:], co, p, ALU.mult)
                v.tensor_tensor(m1[:], si, q, ALU.mult)
                evac_in(l, 4 * c + 3, 1)
                split_lo(l, m, 2)
                v.tensor_tensor(vi[:], co, q, ALU.mult)
                v.tensor_tensor(m2[:], si, p, ALU.mult).then_inc(bu_used, 1)
                split_lo(l, m, 3)
                dve.wait_ge(bu_used, 1 + n + 1)
                v.tensor_tensor(vr[:], vr[:], m1[:], ALU.add)
                st.mark(v.tensor_tensor(vi[:], vi[:], m2[:], ALU.subtract))
                st.wait()
                settle(dve)
                for j in range(4):
                    for w in (vr, vi):
                        ins = v.tensor_tensor_scan(w[:, j, :],
                                                   flat(state[:, 0])[:, bass.ds(n * 4 + j, 1)].broadcast_to([P, T]),
                                                   w[:, j, :], 0.0, ALU.mult, ALU.add)
                st.mark(ins)
                evac_in(l, 4 * c + 4, 0)
                split_lo(l, m + 1, 0)
                split_lo(l, m + 1, 1)
                st.wait()
                dve.wait_ge(y_ready, n + 1)
                v.tensor_tensor(s1[:], co, vr[:], ALU.mult)
                v.tensor_tensor(m1[:], si, vi[:], ALU.mult)
                evac_in(l, 4 * c + 5, 1)
                split_lo(l, m + 1, 2)
                v.tensor_tensor(s2[:], si, vr[:], ALU.mult)
                st.mark(v.tensor_tensor(m2[:], co, vi[:], ALU.mult))
                split_lo(l, m + 1, 3)
                st.wait()
                v.tensor_tensor(s1[:], s1[:], m1[:], ALU.subtract)
                v.tensor_tensor(s2[:], s2[:], m2[:], ALU.add).then_inc(s_ready, 1)
                evac_in(l, 4 * c + 6, 0)
                dve.wait_ge(s_ready, n + 1)
                settle(dve)

            def pool_group(l, gi, w):
                u = hT[:, POOL0 + gi, :]
                step(v.tensor_copy(pool_pad[:, 0, PAD:], u))
                src, shift = 0, 1
                while shift < w:
                    step(v.tensor_tensor(pool_pad[:, 1 - src, PAD:], pool_pad[:, src, PAD:],
                                         pool_pad[:, src, PAD - shift:PAD + T - shift], ALU.add))
                    src, shift = 1 - src, 2 * shift
                if gi:
                    dve.wait_ge(pool_out, l * 4 + gi)
                sums = pool_pad[:, src, PAD:]
                step(v.tensor_tensor(pool_d[:, 0:w], sums[:, 0:w], const[:, C_RECIP:C_RECIP + w], ALU.mult))
                v.tensor_tensor(pool_d[:, 0:w], pool_d[:, 0:w], u[:, 0:w], ALU.subtract)
                v.scalar_tensor_tensor(pool_d[:, w:], sums[:, w:], 1.0 / w, u[:, w:], ALU.mult,
                                       ALU.subtract).then_inc(pool_in, 1)
                dve.wait_ge(pool_in, l * 4 + gi + 1)

            def rotate(x, swapped):
                cos = const[:, C_COS:C_COS + T].unsqueeze(1).broadcast_to([P, 2, T])
                sin = const[:, C_SIN:C_SIN + T].unsqueeze(1).broadcast_to([P, 2, T])
                v.tensor_tensor(rope[:], swapped, sin, ALU.mult)
                step(v.tensor_tensor(x, x, cos, ALU.mult))

            def rotate_queries(l, g):
                dve.wait_ge(swap_ready, l * 5 + g + 2)
                rotate(hT[:, bass.ds(Q0 + 2 * g, 2), :], ps[:, 1, :].rearrange("p (a b) -> p a b", a=2))
                dve.wait_ge(attn_zero, l + 1)
                for half in range(2):
                    part = slice(64 * half, 64 * half + 64)
                    ins = v.tensor_tensor(qpad[part, half::2, :], hT[part, bass.ds(Q0 + 2 * g, 2), :], rope[part],
                                          ALU.add)
                ins.then_inc(q_ready, 1)
                dve.wait_ge(q_ready, l * 4 + g + 1)

            def softmax(l, g, before_sums):
                n = l * 4 + g
                sc0, sc1 = score_buf[g % 2]
                if g >= 2:
                    dve.wait_ge(pT_ready, n - 1)
                dve.wait_ge(score_ready, n + 1)
                causal = const[:, C_MASK + P:C_MASK + 2 * P].unsqueeze(1).broadcast_to([P, 4, P])
                window = const[:, C_MASK:C_MASK + 2 * P].unsqueeze(1).broadcast_to([P, 4, 2 * P])
                v.scalar_tensor_tensor(sc0[:], ps[:, 2, :].rearrange("p (h k) -> p h k", h=4), SCALE, causal,
                                       ALU.mult, ALU.add)
                step(v.scalar_tensor_tensor(sc1[:], ps[:, 3:5, :].rearrange("p a (h k) -> p (a h) k", h=2), SCALE,
                                            window, ALU.mult, ALU.add))
                v.tensor_reduce(sm[:, 0, 0:4], sc0[:], AX_X, ALU.max)
                step(v.tensor_reduce(sm[:, 1, 0:4], sc1[:], AX_X, ALU.max))
                sink = vec[:, bass.ds(l * NV + V_SINK + g * 4, 4)]
                v.tensor_tensor(sm[:, 0, 0:4], sm[:, 0, 0:4], sink, ALU.max)
                step(v.tensor_tensor(sm[:, 1, 0:4], sm[:, 1, 0:4], sink, ALU.max))
                v.tensor_scalar(sm[:, 2:4, 0:4], sm[:, 0:2, 0:4], -1.0, None, ALU.mult)
                v.tensor_tensor(sm[:, 6, 0:4], sink, sm[:, 0, 0:4], ALU.subtract)
                v.tensor_tensor(sm[:, 6, 4:8], sink, sm[:, 1, 0:4], ALU.subtract).then_inc(max_ready, 1)
                before_sums()
                dve.wait_ge(max_ready, n + 1)
                dve.wait_ge(exp_ready, n + 1)
                settle(dve)
                v.tensor_tensor(sm[:, 7, 0:4], sm[:, 4, 0:4], sm[:, 6, 0:4], ALU.add)
                step(v.tensor_tensor(sm[:, 7, 4:8], sm[:, 5, 0:4], sm[:, 6, 4:8], ALU.add))
                step(v.reciprocal(sm[:, 7, :], sm[:, 7, :]))
                v.tensor_tensor(sc0[:], sc0[:], sm[:, 7, 0:4].unsqueeze(2).broadcast_to([P, 4, P]), ALU.mult)
                v.tensor_tensor(sc1[:], sc1[:], sm[:, 7, 4:8].unsqueeze(2).broadcast_to([P, 4, 2 * P]),
                                ALU.mult).then_inc(prob_ready, 1)
                dve.wait_ge(prob_ready, n + 1)

            def output_lo(l, g, bank):
                dve.wait_ge(mix_hi, l * 12 + 8 + g + 1)
                for i in range(2):
                    dst = mixT[:, bass.ds(2 * g + i, 1), :, :].rearrange("p a h b -> p (a h) b")
                    v.tensor_tensor(dst[:, 1, :], ps[:, bank, i * T:(i + 1) * T], dst[:, 0, :].bitcast(F32),
                                    ALU.subtract).then_inc(mix_ready, 1)

            v.sem_inc(lo_done, SLOTS)
            v.sem_inc(tile_evac, 2)
            v.sem_inc(acc_evac, 4)
            v.sem_inc(bu_used, 1)
            v.sem_inc(y_ready, 1)
            v.sem_inc(glu_sum, 1)
            v.sem_inc(xT_ready, 2)
            v.sem_inc(z_ready, 4)
            dve.wait_ge(vec_loaded, 16)
            dve.wait_ge(const_loaded, 16)
            state_parameters()
            dve.wait_ge(prm_ready, 2)
            settle(dve)
            with st.loop(DEPTH, DVE_LAYER) as l:
                split_x(l, l * 2, IN_M)
                evac_in(l, 0, 0)
                split_lo(l, IN_M + 1, 0)
                split_lo(l, IN_M + 1, 1)
                evac_in(l, 1, 1)
                split_lo(l, IN_M + 1, 2)
                split_lo(l, IN_M + 1, 3)
                evac_in(l, 2, 0)
                with st.loop(4, 3) as c:
                    states_and_pairs(l, c)
                evac_in(l, IN_TILES - 1, 1)
                dve.wait_ge(tile_evac, 2 + l * TILES + IN_TILES)
                for s in range(3):
                    split_lo(l, GLU_M, s)
                dve.wait_ge(y_ready, 1 + l * 4 + 4)
                for c in range(4):
                    u = hT[:, SSM0 + c, :]
                    ins = v.scalar_tensor_tensor(u, u, vcol(l, V_D + c), ps[:, 6 + c // 2, bass.ds((c % 2) * T, T)],
                                                 ALU.mult, ALU.add)
                ins.then_inc(y_used, 1)
                split_lo(l, GLU_M, 3)
                dve.wait_ge(y_used, l + 1)
                y = flat(hT[:, SSM0:SSM0 + 4, :])
                dve.wait_ge(gelu_act, 3 * l + 1)
                step(v.tensor_scalar(flat(s1[:]), flat(s1[:]), 0.044715, 1.0, ALU.mult, ALU.add))
                v.tensor_tensor(flat(s2[:]), flat(s1[:]), y, ALU.mult).then_inc(gelu_dve, 1)
                dve.wait_ge(swap_ready, l * 5 + 1)
                keys = hT[:, K0:K0 + 2, :]
                rotate(keys, ps[:, 1, :].rearrange("p (a b) -> p a b", a=2))
                v.tensor_tensor(keys, keys, rope[:], ALU.add).then_inc(rope_ready, 1)
                dve.wait_ge(gelu_act, 3 * l + 2)
                v.scalar_tensor_tensor(flat(vr[:]), flat(s2[:]), 1.0, y, ALU.add, ALU.mult).then_inc(gelu_dve, 1)
                step(v.memset(pool_pad[:, :, 0:PAD], 0.0))
                pool_group(l, 0, POOL_WINDOWS[0])
                dve.wait_ge(gelu_dve, 2 * l + 2)
                dve.wait_ge(gelu_act, 3 * l + 3)
                v.scalar_tensor_tensor(yT[:, :, 1, :], vr[:], 0.5, yT[:, :, 0, :].bitcast(F32), ALU.mult,
                                       ALU.subtract).then_inc(y_split, 1)
                for s in range(4):
                    dve.wait_ge(glu_corr, l * 4 + s + 1)
                    v.tensor_tensor(ab[:], ab[:], ps[:, 2:4, 0:T], ALU.add).then_inc(glu_sum, 1)
                    if s < 3:
                        pool_group(l, s + 1, POOL_WINDOWS[s + 1])
                    else:
                        dve.wait_ge(rope_ready, l + 1)
                        rotate_queries(l, 0)
                    dve.wait_ge(glu_sig, l * 4 + s + 1)
                    step(v.tensor_scalar(ab[:, 1, :], ab[:, 1, :], 0.5, 0.5, ALU.mult, ALU.add))
                    v.tensor_tensor(ab[:, 0, :], ab[:, 0, :], ab[:, 1, :], ALU.mult).then_inc(glu_out, 1)
                    dve.wait_ge(mix_hi, l * 12 + 2 * s + 1)
                    v.tensor_tensor(mixT[:, 12 + s, 1, :], ab[:, 0, :], mixT[:, 12 + s, 0, :].bitcast(F32),
                                    ALU.subtract).then_inc(mix_ready, 1)
                    dve.wait_ge(mix_hi, l * 12 + 2 * s + 2)
                    v.scalar_tensor_tensor(mixT[:, 8 + s, 1, :], ps[:, 6 + s % 2, 0:T], vcol(l, V_PSC + s),
                                           mixT[:, 8 + s, 0, :].bitcast(F32), ALU.mult,
                                           ALU.subtract).then_inc(mix_ready, 1)

                softmax(l, 0, lambda: rotate_queries(l, 1))
                for g in range(2):
                    softmax(l, g + 1, lambda: rotate_queries(l, g + 2))
                    split_lo(l, OUT_M, g)
                    output_lo(l, g, 0)
                softmax(l, 3, lambda: (output_lo(l, 2, 0), split_lo(l, OUT_M, 2), split_lo(l, OUT_M, 3)))
                output_lo(l, 3, 4)

                for p_i, (m0, groups, last) in enumerate(((OUT_M, 4, 0), (DOWN_M, DOWN_GROUPS, FF_TILES % 4))):
                    if p_i:
                        step(v.memset(hbuf[:, :, 0:2], 0.0))
                        split_x(l, l * 2 + 1, UP_M)
                        split_lo(l, UP_M + 1, 0)
                        conv_tile(l, 0, 0)

                        def up_pair(j, ahead):
                            split_lo(l, UP_M + 1 + j, 1)
                            conv_tile(l, j, 1)
                            split_lo(l, UP_M + 1 + j, 2)
                            gated(l, j)
                            split_lo(l, UP_M + 1 + j, 3)
                            gated_lo(l, j)
                            if ahead:
                                split_lo(l, UP_M + 2 + j, 0)
                            conv_tile(l, j + 1, 0)

                        with st.loop(FF_TILES - 2, 4) as j:
                            up_pair(j, True)
                        up_pair(FF_TILES - 2, False)
                        conv_tile(l, FF_TILES - 1, 1)
                        gated(l, FF_TILES - 1)
                        gated_lo(l, FF_TILES - 1)
                    full = groups - (1 if last else 0)

                    def short_group(h):
                        for s in range(last):
                            split_lo(l, m0 + groups * h + groups - 1, s, 2 if s == last - 1 else 1)

                    ahead = 0 if p_i else 1
                    with st.loop(full - ahead, 0) as q:
                        for s in range(SLOTS):
                            split_lo(l, m0 + ahead + q, s)
                    short_group(0)
                    split_lo(l, m0 + groups, 0)
                    split_lo(l, m0 + groups, 1)
                    evac_half(l, 0, l * 4 + 2 * p_i, chunks(l, m0 + groups - 1, 3), l * 2 + p_i,
                              lambda: (split_lo(l, m0 + groups, 2), split_lo(l, m0 + groups, 3)))
                    with st.loop(full - 1, 0) as q:
                        for s in range(SLOTS):
                            split_lo(l, m0 + groups + 1 + q, s)
                    short_group(1)
                    evac_half(l, 1, l * 4 + 2 * p_i + 1, chunks(l, m0 + 2 * groups - 1, 3), l * 2 + p_i,
                              lambda: None)
                    normalise(l * 2 + p_i)
                dve.wait_ge(gb_last_loaded, (l + 1) * 16)
            dve.wait_ge(z_ready, 4 * (2 * DEPTH + 1))
            settle(dve)
            for c in range(4):
                cols = slice(c * BANK, (c + 1) * BANK)
                y = xres[:, :, cols]
                v.tensor_tensor(y, y, gb_last[:, 0:1, cols].broadcast_to([P, NT, BANK]),
                                ALU.mult).then_inc(out_scaled, 1)
                dve.wait_ge(out_scaled, c + 1)
                v.tensor_tensor(y, y, gb_last[:, 1:2, cols].broadcast_to([P, NT, BANK]),
                                ALU.add).then_inc(out_ready, 1)

        @block.gpsimd
        def _(pool):
            st = Steps(pool, pool_steps)
            g_ = nc.gpsimd

            def step(ins):
                st.mark(ins)
                st.wait()

            def affine_rows(stage, part=None):
                n = D // GBC
                for c in {None: range(n), 0: range(n // 2), 1: range(n // 2, n)}[part]:
                    g_.dma_start(gb[:], a["gb"][bass.ds(stage, 1), :, c * GBC:(c + 1) * GBC]
                                 .rearrange("s g d -> (s g) d").partition_broadcast(P)).then_inc(gb_loaded, 16)
                    pool.wait_ge(gb_loaded, (stage * (D // GBC) + c + 1) * 16)
                    y = xres[:, :, c * GBC:(c + 1) * GBC]
                    step(g_.tensor_tensor(y, y, gb[:, 0:1, :].broadcast_to([P, NT, GBC]), ALU.mult))
                    step(g_.tensor_tensor(y, y, gb[:, 1:2, :].broadcast_to([P, NT, GBC]), ALU.add))
                if part != 0:
                    pool.sem_inc(xres_ready, 1)

            def reciprocal_deviation(norm):
                pool.wait_ge(stats_ready, norm * 2 + 2)
                settle(pool)
                step(g_.tensor_scalar(rstd[:, 0, :], mv[:, :, 1], LN_EPS, None, ALU.add))
                g_.tensor_tensor(rstd[:, 1, :], rstd[:, 0, :], neg_half[:], ALU.pow).then_inc(rstd_ready, 1)
                pool.wait_ge(rstd_ready, norm + 1)

            def turns_table(l, c):
                hi, lo = phase[:, 0, bass.ds(c * 4, 4), :], phase[:, 1, bass.ds(c * 4, 4), :]
                f_hi, f_lo = (flat(state[:, i])[:, bass.ds(l * 16 + c * 4, 4)].unsqueeze(2).broadcast_to([P, 4, T])
                              for i in (3, 4))
                t = tokens[:].broadcast_to([P, 4, T])

                def same(column):
                    return const[:, column:column + 1].unsqueeze(2).broadcast_to([P, 4, T])

                g_.tensor_tensor(hi, f_hi, t, ALU.mult)
                step(g_.tensor_tensor(lo, f_lo, t, ALU.mult))
                settle(pool)
                step(g_.tensor_tensor(ptmp[:], hi, lo, ALU.add))
                settle(pool)
                step(g_.tensor_tensor(ptmp[:], ptmp[:], same(C_ROUND), ALU.add))
                settle(pool)
                step(g_.tensor_tensor(ptmp[:], ptmp[:], same(C_ROUND), ALU.subtract))
                settle(pool)
                step(g_.tensor_tensor(hi, hi, ptmp[:], ALU.subtract))
                settle(pool)
                step(g_.tensor_tensor(ptmp[:], lo, hi, ALU.add))
                settle(pool)
                step(g_.tensor_scalar(ptmp[:], ptmp[:], 0.5, -0.5, ALU.min, ALU.max))
                settle(pool)
                step(g_.tensor_tensor(lo, ptmp[:], same(C_ZERO), ALU.add))
                pool.sem_inc(turns_ready, 1)

            def output_matrix(c, n):
                pool.wait_ge(c_loaded, (n + 1) * 16)
                pool.wait_ge(y_ready, n + 1)
                settle(pool)
                zr, zi = (flat(state[:, i])[:, bass.ds(n * 4, 4)].unsqueeze(2).broadcast_to([P, 4, 32])
                          for i in (1, 2))
                cr, ci = (c_raw[:, i, :].rearrange("p (j h) -> p j h", j=4) for i in range(2))
                t0, t1 = (c_tmp[:, i, :].rearrange("p (j h) -> p j h", j=4) for i in range(2))
                dst = [c_pad[:, i, :].rearrange("p (j w) -> p j w", w=160)[:, :, 0:32] for i in range(2)]
                g_.tensor_tensor(t0, cr, zr, ALU.mult)
                step(g_.tensor_tensor(t1, ci, zi, ALU.mult))
                step(g_.tensor_tensor(dst[0], t0, t1, ALU.subtract))
                settle(pool)
                g_.tensor_tensor(t0, cr, zi, ALU.mult)
                step(g_.tensor_tensor(t1, ci, zr, ALU.mult))
                step(g_.tensor_tensor(t0, t0, t1, ALU.add))
                settle(pool)
                step(g_.tensor_scalar(dst[1], t0, -1.0, 0.0, ALU.mult, ALU.add))
                pool.sem_inc(cpad_ready, 1)

            step(g_.memset(neg_half[:], -0.5))
            with st.loop(DEPTH, POOL_LAYER) as l:
                pool.wait_ge(zT_ready, l * 8 + 1)
                settle(pool)
                g_.dma_start(tokens[:].rearrange("p a t -> p (a t)"),
                             a["tokens"].partition_broadcast(P)).then_inc(tokens_loaded, 16)
                g_.memset(b_pad[:].rearrange("p a j m -> p (a j m)"), 0.0)
                step(g_.memset(flat(c_pad[:]), 0.0))
                settle(pool)

                pool.sem_inc(pads_zero, 1)
                pool.wait_ge(tokens_loaded, (l + 1) * 16)
                pool.wait_ge(prm_ready, 1)
                settle(pool)
                turns_table(l, 0)
                turns_table(l, 1)
                pool.wait_ge(prm_ready, 2)
                with st.loop(2, POOL_STATES) as c:
                    output_matrix(c, l * 4 + c)
                    turns_table(l, c + 2)
                output_matrix(2, l * 4 + 2)
                output_matrix(3, l * 4 + 3)
                pool.wait_ge(zT_ready, l * 8 + 4)
                affine_rows(l * 2, 0)
                settle(pool)
                pool.wait_ge(y_used, l + 1)
                settle(pool)
                step(g_.memset(flat(qpad[:]), 0.0))
                pool.sem_inc(attn_zero, 1)
                step(g_.memset(vpad[:].rearrange("p b h d -> p (b h d)"), 0.0))
                pool.wait_ge(vtok_ready, l + 1)
                settle(pool)
                with pool.Fori(0, 4) as g:
                    pool.wait_ge(mix_ready, l * 16 + 8 + 2 * g)
                    settle(pool)
                    for half in range(2):
                        ins = g_.tensor_copy(vpad[:, :, half, 64 * half:64 * half + 64], vtok[:, :, bass.ds(g * 64, 64)])
                    ins.then_inc(vpad_ready, 1)
                affine_rows(l * 2, 1)
                reciprocal_deviation(l * 2)
                pool.wait_ge(zT_ready, l * 8 + 8)
                affine_rows(l * 2 + 1)
                pool.wait_ge(act_lo, (l + 1) * FF_TILES)
                settle(pool)
                g_.dma_start(flat(gb_last[:]), a["gb"][2 * DEPTH].rearrange("g d -> (g d)")
                             .partition_broadcast(P)).then_inc(gb_last_loaded, 16)
                reciprocal_deviation(l * 2 + 1)


def kernel(**inputs):
    import numpy as np
    import concourse.bacc as bacc
    from concourse.bass_utils import run_bass_kernel_spmd

    def arr(name):
        return np.asarray(inputs[name])

    def tiles(w, n):
        return w.reshape(DEPTH, -1, P, n, P).transpose(0, 3, 2, 1, 4)

    def cols(v):
        v = v.reshape(*v.shape[:-1], -1, P)
        return np.moveaxis(v, -1, 0)

    f4 = np.float32
    order = [(t + 16) % IN_TILES for t in range(IN_TILES)]
    w_in = np.ascontiguousarray(tiles(arr("w_in"), IN_TILES)[:, order])
    w_up = tiles(arr("ffn_w_up"), 2 * FF_TILES).reshape(DEPTH, 2, FF_TILES, P, KT, P).transpose(0, 2, 1, 3, 4, 5)

    def chunked(w):
        w = w.reshape(DEPTH, -1, 2, P, 2, CHUNK).transpose(0, 1, 2, 4, 3, 5)
        return np.ascontiguousarray(w.reshape(DEPTH, -1, 4, P, CHUNK))

    glu_w = arr("ssm_glu_w").reshape(DEPTH, 4, P, 2, 4, P).transpose(0, 4, 2, 1, 3, 5)

    b_blk = np.zeros((DEPTH, 4, 4, 2, 16, 2, 2, 64), f4)
    c_blk = np.zeros((DEPTH, 4, 2, 64, 2, 4, 2, 16), f4)
    for part, (bn, cn) in enumerate((("ssm_b_re", "ssm_c_re"), ("ssm_b_im", "ssm_c_im"))):
        b = arr(bn).reshape(DEPTH, 4, 4, 2, 64, 16)
        c = arr(cn).reshape(DEPTH, 4, 4, 2, 16, 64)
        for g in range(2):
            b_blk[:, :, :, g, :, part, g, :] = b[:, :, :, g].transpose(0, 1, 2, 4, 3)
            c_blk[:, :, g, :, part, :, g, :] = c[:, :, :, g].transpose(0, 1, 4, 2, 3)

    gb = np.zeros((2 * DEPTH + 1, 2, D), f4)
    gb[0, 0] = 1
    for l in range(DEPTH):
        for i, n in enumerate(("ln1", "ln2")):
            gb[2 * l + 1 + i, 0], gb[2 * l + 1 + i, 1] = arr(n + "_g")[l], arr(n + "_b")[l]

    vec = np.zeros((P, DEPTH, NV), f4)
    for l in range(DEPTH):
        parts = [cols(arr("ffn_conv_w")[l]).reshape(P, -1), cols(arr("ffn_conv_b")[l]),
                 cols(gb[2 * l]).reshape(P, -1), cols(gb[2 * l + 1]).reshape(P, -1),
                 cols(arr("pool_scale")[l]), cols(arr("ssm_d")[l].reshape(-1)),
                 cols(arr("ssm_lam_re")[l].reshape(-1)), cols(arr("ssm_lam_im")[l].reshape(-1)),
                 cols(np.repeat(arr("ssm_log_dt")[l], 64)),
                 np.broadcast_to(arr("attn_sinks")[l], (P, 16))]
        vec[:, l] = np.concatenate(parts, axis=1)

    const = np.zeros((P, NC), f4)
    const[:, C_ID:C_ID + P] = np.eye(P)
    row = np.arange(P)
    const[row ^ 32, C_PERM + row] = 1
    inv = np.power(f4(10000.0), -np.arange(32, dtype=f4) / f4(32)).astype(f4)
    ang = (np.arange(T, dtype=f4)[None, :] * inv[row % 32][:, None]).astype(f4)
    const[:, C_COS:C_COS + T] = np.cos(ang)
    const[:, C_SIN:C_SIN + T] = np.sin(ang) * np.where(row % 64 < 32, -1, 1)[:, None]
    key = np.arange(P)
    const[:, C_MASK:C_MASK + P] = np.where(key[None, :] > row[:, None], 0, -1e30)
    const[:, C_MASK + P:C_MASK + 2 * P] = np.where(key[None, :] <= row[:, None], 0, -1e30)
    const[:, C_RECIP:C_RECIP + PAD] = 1.0 / np.arange(1, PAD + 1)
    const[:, C_HALF_PI] = np.pi / 2
    const[:, C_ROUND] = ROUND

    arrays = {
        "x": arr("x")[0], "const": const, "vec": vec.reshape(P, -1), "gb": gb, "tokens": np.arange(T, dtype=f4),
        "w_in": chunked(w_in), "w_up": chunked(w_up),
        "glu_w": np.ascontiguousarray(glu_w.reshape(DEPTH, 4, P, CHUNK)),
        "w_out": arr("w_out"), "w_down": arr("ffn_w_down"), "pool_w": arr("pool_w"),
        "ssm_b": b_blk.reshape(DEPTH, 4, P, 2, P), "ssm_c": c_blk.reshape(DEPTH, 4, P, 2, P),
    }
    nc = bacc.Bacc("TRN2", target_bir_lowering=False, num_devices=1)
    feeds, aps = {}, {}
    for name, v in arrays.items():
        v = np.ascontiguousarray(v)
        feeds["in_" + name] = v
        aps[name] = nc.dram_tensor("in_" + name, v.shape, F32, kind="ExternalInput").ap()
    aps["out"] = nc.dram_tensor("out", (T, D), F32, kind="ExternalOutput").ap()
    trunk(nc, aps)
    r = run_bass_kernel_spmd(nc, [feeds], core_ids=[0])
    return r.results[0]["out"].reshape(1, T, D)
```
